# Optimizing a Trainium2 kernel written in Bass

```python
import math
import jax, jax.numpy as jnp
from jax import lax
import numpy as np

D_MODEL = 1024
BATCH = 1
SEQ = 512
DEPTH = 1

A_HEADS = 8
A_HEAD_DIM = 64
A_PATTERNS = ((128, 1), (512, 4), (2048, 16))
B_HEADS = 8
B_HEAD_DIM = 128
CONV_K = 5
CHUNK = 64
N_EXPERTS = 32
TOP_K = 4
D_FF = D_MODEL
SWIGLU_LIMIT = 7.0
SWIGLU_ALPHA = 1.702
MOE_BLOCK = 128
EPS = 1e-6
NEG_INF = -1e30

A_WIDTH = A_HEADS * A_HEAD_DIM
B_WIDTH = B_HEADS * B_HEAD_DIM
IN_SPLITS = (A_WIDTH, A_WIDTH, A_WIDTH, 3 * B_WIDTH, B_WIDTH,
             B_HEADS, B_HEADS, B_HEADS, B_HEADS, D_MODEL, D_MODEL)
IN_COLS = sum(IN_SPLITS)

kernel_name = 'hybrid_dilated_attn_gdn_moe_encoder'

def rms_norm(x, w):
    xf = x.astype(jnp.float32)
    y = xf * lax.rsqrt(jnp.mean(xf * xf, axis=-1, keepdims=True) + EPS)
    return (y * w.astype(jnp.float32)).astype(x.dtype)

def l2_normalize(x):
    xf = x.astype(jnp.float32)
    return xf * lax.rsqrt(jnp.sum(xf * xf, axis=-1, keepdims=True) + EPS)

def alibi_slopes(n_heads):
    return jnp.asarray(2.0 ** (-8.0 * np.arange(1, n_heads + 1) / n_heads), dtype=jnp.float32)

def dilated_window_attention(q, k, v, window, dilation, slopes):
    Bsz, S, H, dh = q.shape
    blk = window // (2 * dilation)
    L = S // dilation
    nb = -(-L // blk)
    Lp = nb * blk

    def by_residue(t):
        t = t.astype(jnp.float32).reshape(Bsz, L, dilation, H, dh).transpose(0, 3, 2, 1, 4)
        return jnp.pad(t, ((0, 0), (0, 0), (0, 0), (0, Lp - L), (0, 0)))

    def key_blocks(t):
        t = jnp.pad(by_residue(t), ((0, 0), (0, 0), (0, 0), (blk, blk), (0, 0)))
        t = t.reshape(Bsz, H, dilation, nb + 2, blk, dh)
        return (t[:, :, :, :-2], t[:, :, :, 1:-1], t[:, :, :, 2:])

    qr = by_residue(q).reshape(Bsz, H, dilation, nb, blk, dh)
    kbs = key_blocks(k)
    vbs = key_blocks(v)
    scores = jnp.concatenate(
        [jnp.einsum('bhrnqd,bhrnkd->bhrnqk', qr, kk) for kk in kbs], axis=-1) * (dh ** -0.5)
    q_idx = jnp.arange(nb)[:, None] * blk + jnp.arange(blk)[None, :]
    k_idx = (jnp.arange(nb)[:, None] - 1) * blk + jnp.arange(3 * blk)[None, :]
    diff = k_idx[:, None, :] - q_idx[:, :, None]
    valid = (jnp.abs(diff) <= blk) & (k_idx[:, None, :] >= 0) & (k_idx[:, None, :] < L)
    dist = (dilation * jnp.abs(diff)).astype(jnp.float32)
    bias = -slopes[:, None, None, None] * dist[None]
    scores = jnp.where(valid, scores + bias[None, :, None], NEG_INF)
    m = jnp.max(scores, axis=-1, keepdims=True)
    p = jnp.exp(scores - m)
    l = jnp.sum(p, axis=-1, keepdims=True)
    pv = sum(jnp.einsum('bhrnqk,bhrnkd->bhrnqd', p[..., i * blk:(i + 1) * blk], vbs[i])
             for i in range(3))
    out = (pv / l).reshape(Bsz, H, dilation, Lp, dh)[:, :, :, :L]
    lse = (m[..., 0] + jnp.log(l[..., 0])).reshape(Bsz, H, dilation, Lp)[:, :, :, :L]
    out = out.transpose(0, 3, 2, 1, 4).reshape(Bsz, S, H, dh)
    lse = lse.transpose(0, 3, 2, 1).reshape(Bsz, S, H)
    return out, lse

def dilated_attention_branch(qa, ka, va):
    Bsz, S, _ = qa.shape
    shp = (Bsz, S, A_HEADS, A_HEAD_DIM)
    q, k, v = qa.reshape(shp), ka.reshape(shp), va.reshape(shp)
    slopes = alibi_slopes(A_HEADS)
    results = [dilated_window_attention(q, k, v, w, r, slopes) for (w, r) in A_PATTERNS]
    outs = jnp.stack([o for o, _ in results])
    lses = jnp.stack([s for _, s in results])
    wts = jax.nn.softmax(lses, axis=0)
    o = jnp.sum(wts[..., None] * outs, axis=0)
    return o.reshape(Bsz, S, A_WIDTH).astype(qa.dtype)

def centred_depthwise_conv(x, w):
    C = x.shape[-1]
    return lax.conv_general_dilated(
        x, w[:, None, :].astype(x.dtype), window_strides=(1,),
        padding=((CONV_K // 2, CONV_K // 2),),
        dimension_numbers=('NWC', 'WIO', 'NWC'), feature_group_count=C)

def gated_delta_rule_chunked(q, k, v, g, beta):
    Bsz, S, H, dk = q.shape
    dv = v.shape[-1]
    n = S // CHUNK

    def chunks(t):
        return t.astype(jnp.float32).reshape(Bsz, n, CHUNK, H, -1).transpose(0, 3, 1, 2, 4)

    qc, kc, vc = chunks(q), chunks(k), chunks(v)
    gc = jnp.cumsum(chunks(g[..., None])[..., 0], axis=-1)
    bc = chunks(beta[..., None])[..., 0]
    incl = jnp.tril(jnp.ones((CHUNK, CHUNK), dtype=bool))
    strict = jnp.tril(jnp.ones((CHUNK, CHUNK), dtype=bool), -1)
    gdiff = gc[..., :, None] - gc[..., None, :]
    decay = jnp.where(incl, jnp.exp(jnp.where(incl, gdiff, 0.0)), 0.0)
    kb = kc * bc[..., None]
    a_mat = jnp.where(strict, jnp.einsum('bhnid,bhnjd->bhnij', kb, kc) * decay, 0.0)
    rhs = jnp.concatenate([vc * bc[..., None], kb * jnp.exp(gc)[..., None]], axis=-1)
    sol = lax.linalg.triangular_solve(a_mat, rhs, left_side=True, lower=True,
                                      unit_diagonal=True)
    u, w = sol[..., :dv], sol[..., dv:]
    qk = jnp.einsum('bhnid,bhnjd->bhnij', qc, kc) * decay
    q_dec = qc * jnp.exp(gc)[..., None]
    k_dec = kc * jnp.exp(gc[..., -1:] - gc)[..., None]
    g_last = jnp.exp(gc[..., -1])
    to_lead = lambda t: jnp.moveaxis(t, 2, 0)
    xs = (to_lead(u), to_lead(w), to_lead(qk), to_lead(q_dec), to_lead(k_dec), to_lead(g_last))

    def step(state, inp):
        u_i, w_i, qk_i, qd_i, kd_i, gl_i = inp
        v_new = u_i - jnp.einsum('bhcd,bhde->bhce', w_i, state)
        o_i = jnp.einsum('bhcd,bhde->bhce', qd_i, state) + jnp.einsum('bhij,bhje->bhie', qk_i, v_new)
        state = state * gl_i[..., None, None] + jnp.einsum('bhcd,bhce->bhde', kd_i, v_new)
        return state, o_i

    _, o = lax.scan(step, jnp.zeros((Bsz, H, dk, dv), jnp.float32), xs)
    return o.transpose(1, 0, 3, 2, 4).reshape(Bsz, S, H, dv)

def gated_deltanet_branch(qkv, z, a_f, a_b, b_f, b_b, conv_w, a_log_f, a_log_b,
                          dt_bias_f, dt_bias_b, norm_w):
    Bsz, S, _ = qkv.shape
    shp = (Bsz, S, B_HEADS, B_HEAD_DIM)
    qkv = jax.nn.silu(centred_depthwise_conv(qkv, conv_w))
    q, k, v = jnp.split(qkv, 3, axis=-1)
    q = l2_normalize(q.reshape(shp)) * (B_HEAD_DIM ** -0.5)
    k = l2_normalize(k.reshape(shp))
    v = v.reshape(shp).astype(jnp.float32)

    def decay_and_beta(a, b, a_log, dt_bias):
        g = -jnp.exp(a_log.astype(jnp.float32)) * jax.nn.softplus(
            a.astype(jnp.float32) + dt_bias.astype(jnp.float32))
        return g, jax.nn.sigmoid(b.astype(jnp.float32))

    g_f, beta_f = decay_and_beta(a_f, b_f, a_log_f, dt_bias_f)
    g_b, beta_b = decay_and_beta(a_b, b_b, a_log_b, dt_bias_b)
    flip = lambda t: jnp.flip(t, axis=1)
    o_f = gated_delta_rule_chunked(q, k, v, g_f, beta_f)
    o_b = flip(gated_delta_rule_chunked(flip(q), flip(k), flip(v), flip(g_b), flip(beta_b)))
    o = rms_norm(o_f + o_b, norm_w) * jax.nn.silu(z.reshape(shp).astype(jnp.float32))
    return o.reshape(Bsz, S, B_WIDTH).astype(z.dtype)

def moe_ffn(h, router_w, router_b, w_gate_up, b_gate_up, w_down, b_down):
    Bsz, S, D = h.shape
    hf = h.reshape(-1, D)
    n_tok = hf.shape[0]
    logits = (hf @ router_w + router_b).astype(jnp.float32)
    top_logits, top_idx = lax.top_k(logits, TOP_K)
    gates = jax.nn.softmax(top_logits, axis=-1)
    n_assign = n_tok * TOP_K
    flat_e = top_idx.reshape(-1)
    order = jnp.argsort(flat_e)
    e_sorted = flat_e[order]
    tok_sorted = order // TOP_K
    gate_sorted = gates.reshape(-1)[order]
    counts = jnp.bincount(flat_e, length=N_EXPERTS)
    padded = (counts + MOE_BLOCK - 1) // MOE_BLOCK * MOE_BLOCK
    pad_end = jnp.cumsum(padded)
    pad_start = pad_end - padded
    start = jnp.cumsum(counts) - counts
    dest = pad_start[e_sorted] + jnp.arange(n_assign) - start[e_sorted]
    n_blocks = -(-n_assign // MOE_BLOCK) + N_EXPERTS
    slot_tok = jnp.zeros((n_blocks * MOE_BLOCK,), jnp.int32).at[dest].set(tok_sorted)
    block_expert = jnp.clip(
        jnp.searchsorted(pad_end, jnp.arange(n_blocks) * MOE_BLOCK, side='right'),
        0, N_EXPERTS - 1)
    xb = hf[slot_tok].reshape(n_blocks, MOE_BLOCK, D)

    def expert_block(args):
        xe, e = args
        gu = xe @ w_gate_up[e] + b_gate_up[e]
        x_glu = jnp.minimum(gu[:, :D_FF], SWIGLU_LIMIT)
        x_lin = jnp.clip(gu[:, D_FF:], -SWIGLU_LIMIT, SWIGLU_LIMIT)
        act = x_glu * jax.nn.sigmoid(SWIGLU_ALPHA * x_glu) * (x_lin + 1.0)
        return act @ w_down[e] + b_down[e]

    yb = lax.map(expert_block, (xb, block_expert)).reshape(-1, D)
    contrib = (yb[dest].astype(jnp.float32) * gate_sorted[:, None]).astype(h.dtype)
    out = jnp.zeros((n_tok, D), h.dtype).at[tok_sorted].add(contrib)
    return out.reshape(Bsz, S, D)

def setup_inputs(seed: int = 0) -> dict:
    key = jax.random.key(seed)
    ks = jax.random.split(key, 24)
    f32 = jnp.float32

    def normal(k, shape, fan_in):
        return jax.random.normal(k, shape, f32) * (fan_in ** -0.5)

    def gain(k, shape):
        return 1.0 + 0.01 * jax.random.normal(k, shape, f32)

    def dt_bias(k):
        dt = jnp.exp(jax.random.uniform(k, (DEPTH, B_HEADS), f32, math.log(1e-3), math.log(1e-1)))
        return dt + jnp.log(-jnp.expm1(-dt))

    return {
        'x': jax.random.normal(ks[0], (BATCH, SEQ, D_MODEL), f32),
        'norm1_w': gain(ks[1], (DEPTH, D_MODEL)),
        'w_in': normal(ks[2], (DEPTH, D_MODEL, IN_COLS), D_MODEL),
        'conv_w': normal(ks[3], (DEPTH, CONV_K, 3 * B_WIDTH), CONV_K),
        'a_log_f': jnp.log(jax.random.uniform(ks[4], (DEPTH, B_HEADS), f32, 1.0, 16.0)),
        'a_log_b': jnp.log(jax.random.uniform(ks[5], (DEPTH, B_HEADS), f32, 1.0, 16.0)),
        'dt_bias_f': dt_bias(ks[6]),
        'dt_bias_b': dt_bias(ks[7]),
        'gdn_norm_w': gain(ks[8], (DEPTH, B_HEAD_DIM)),
        'w_branch_a': normal(ks[9], (DEPTH, A_WIDTH, D_MODEL), A_WIDTH),
        'w_branch_b': normal(ks[10], (DEPTH, B_WIDTH, D_MODEL), B_WIDTH),
        'w_out': normal(ks[11], (DEPTH, D_MODEL, D_MODEL), D_MODEL),
        'norm2_w': gain(ks[12], (DEPTH, D_MODEL)),
        'router_w': normal(ks[13], (DEPTH, D_MODEL, N_EXPERTS), D_MODEL),
        'router_b': 0.01 * jax.random.normal(ks[14], (DEPTH, N_EXPERTS), f32),
        'w_gate_up': normal(ks[15], (DEPTH, N_EXPERTS, D_MODEL, 2 * D_FF), D_MODEL),
        'b_gate_up': 0.01 * jax.random.normal(ks[16], (DEPTH, N_EXPERTS, 2 * D_FF), f32),
        'w_down': normal(ks[17], (DEPTH, N_EXPERTS, D_FF, D_MODEL), D_FF),
        'b_down': 0.01 * jax.random.normal(ks[18], (DEPTH, N_EXPERTS, D_MODEL), f32),
        'norm_f_w': gain(ks[19], (D_MODEL,)),
    }

def reference(x, norm1_w, w_in, conv_w, a_log_f, a_log_b, dt_bias_f, dt_bias_b,
              gdn_norm_w, w_branch_a, w_branch_b, w_out, norm2_w, router_w, router_b,
              w_gate_up, b_gate_up, w_down, b_down, norm_f_w):
    split_points = [int(s) for s in np.cumsum(IN_SPLITS)[:-1]]
    for layer in range(DEPTH):
        h = rms_norm(x, norm1_w[layer])
        proj = h @ w_in[layer]
        (qa, ka, va, qkv_b, z_b, a_f, a_b, b_f, b_b,
         gate_a, gate_b) = jnp.split(proj, split_points, axis=-1)
        y_a = dilated_attention_branch(qa, ka, va)
        y_b = gated_deltanet_branch(qkv_b, z_b, a_f, a_b, b_f, b_b, conv_w[layer],
                                    a_log_f[layer], a_log_b[layer], dt_bias_f[layer],
                                    dt_bias_b[layer], gdn_norm_w[layer])
        merged = (jax.nn.sigmoid(gate_a) * (y_a @ w_branch_a[layer])
                  + jax.nn.sigmoid(gate_b) * (y_b @ w_branch_b[layer]))
        x = x + merged @ w_out[layer]
        h2 = rms_norm(x, norm2_w[layer])
        x = x + moe_ffn(h2, router_w[layer], router_b[layer], w_gate_up[layer],
                        b_gate_up[layer], w_down[layer], b_down[layer])
    return rms_norm(x, norm_f_w)


_drawn_inputs = setup_inputs


def setup_inputs(seed=0):
    import zlib

    import numpy as np

    out = dict(_drawn_inputs(seed))
    spreads = {}
    factors = {'gdn_norm_w': 4.095, 'b_gate_up': 8.0, 'b_down': 8.0, 'norm_f_w': 5.672}
    for name, (base, spread) in spreads.items():
        noise = np.random.default_rng([zlib.crc32(name.encode()), seed]).standard_normal(out[name].shape)
        drawn = base * np.exp(spread * noise) if base else spread * noise
        out[name] = __import__('jax').numpy.asarray(drawn.astype(out[name].dtype))
    for name, factor in factors.items():
        out[name] = (out[name] * factor).astype(out[name].dtype)
    return out
```

```python
from contextlib import ExitStack
import math

import concourse.bass as bass
from concourse import mybir

F32 = mybir.dt.float32
F16 = mybir.dt.float16
I32 = mybir.dt.int32
U32 = mybir.dt.uint32
ALU = mybir.AluOpType
ACT = mybir.ActivationFunctionType
AX = mybir.AxisListType

P = 128
S = 512
TT = S // P
D = 1024
KD = D // P
AH, ADH = 8, 64
PAIRS = AH // 2
BH, BDH = 8, 128
CK = 5
HALO = CK // 2
NE, TOPK = 32, 4
FF = 1024
FT = FF // P
EPS = 1e-6
MASKED = -1e30
LIMIT, ALPHA = 7.0, 1.702
PATTERNS = ((128, 1), (512, 4), (2048, 16))
SLOPES = [2.0 ** (-8.0 * (h + 1) / AH) for h in range(AH)]
AW, BW = AH * ADH, BH * BDH
COL_QA, COL_KA, COL_VA = 0, AW, 2 * AW
COL_QB = 3 * AW
COL_KB, COL_VB = COL_QB + BW, COL_QB + 2 * BW
COL_Z = COL_QB + 3 * BW
COL_AB = COL_Z + BW
COL_GA = COL_AB + 4 * BH
COL_GB = COL_GA + D
IN_COLS = COL_GB + D
ROUNDS = S // P
FWD, BWD = 0, 1
LEVELS = 6


def build(nc, x, norm1_w, w_in, conv_w, a_log_f, a_log_b, dt_bias_f, dt_bias_b, gdn_norm_w,
          w_branch_a, w_branch_b, w_out, norm2_w, router_w, router_b, w_gate_up, b_gate_up,
          w_down, b_down, norm_f_w, out):
    ds = bass.ds
    x = x[0]
    out = out[0]
    w_in_v = w_in[0].rearrange("(k p) c -> p k c", p=P)
    wa_v = w_branch_a[0].rearrange("(k p) c -> p k c", p=P)
    wb_v = w_branch_b[0].rearrange("(k p) c -> p k c", p=P)
    wo_v = w_out[0].rearrange("(k p) c -> p k c", p=P)
    h2_dram = nc.dram_tensor("h2_rows", [S, D], F32).ap()
    y_dram = nc.dram_tensor("expert_rows", [NE * S, D], F32).ap()

    with ExitStack() as ctx:
        def sb(name, shape, dt=F32):
            return ctx.enter_context(nc.sbuf_tensor(name, shape, dt))

        def sem(name):
            return ctx.enter_context(nc.semaphore(name))

        ps = ctx.enter_context(nc.psum_tensor("ps", [P, 8, 512], F32))

        def bank(b):
            return ps[:, b, :]


        def split(v, shape):
            names = "abcd"[:len(shape)]
            dims = dict(zip(names, shape))
            return v.rearrange(f"p ({' '.join(names)}) -> p {' '.join(names)}", **dims)

        class Area:

            def __init__(self, whole, floats):
                self.whole, self.floats, self.at = whole, floats, 0

            def take(self, *shape):
                n = math.prod(shape)
                v = self.whole[:, self.at:self.at + n]
                self.at += n
                assert self.at <= self.floats, (self.at, self.floats)
                return split(v, shape)

        def wide(ap, shape):
            return ap.to_broadcast(shape)

        xs = sb("xs", [P, TT, D])

        MIXER_FLOATS = 2 * KD * S + PAIRS * S + 2 * 4 * KD * P
        mixer = Area(sb("mixer_area", [P, MIXER_FLOATS]), MIXER_FLOATS)
        hT = mixer.take(KD, S)
        ybT = mixer.take(BH, S)
        yaT = mixer.take(PAIRS, S)
        wcols = [mixer.take(4, KD, P) for _ in range(2)]

        RING = 12
        SLOT = 2 * FF
        WORK_FLOATS = 10 * SLOT + 64
        work = Area(sb("work_area", [P, WORK_FLOATS]), WORK_FLOATS)
        ring_head = sb("ring_head", [P, 2, SLOT])
        slots = [ring_head[:, i, :] if i < 2 else work.whole[:, (i - 2) * SLOT:(i - 1) * SLOT]
                 for i in range(RING)]

        ident = sb("ident", [P, P])
        ones = sb("ones", [P, P])
        upper_incl = sb("upper_incl", [P, P])
        upper_strict = sb("upper_strict", [P, P])
        lower_incl = sb("lower_incl", [P, P])
        lower_strict = sb("lower_strict", [P, P])
        vec_rows = sb("vec_rows", [P, P])
        vecT = sb("vecT", [P, P])
        CONVS = CK * 3 * BH
        gnw = sb("gnw", [P, 1])
        wab = sb("wab", [P, KD, 4 * BH])
        gate_c = sb("gate_c", [P, 4, BH])
        ab = sb("ab", [P, 4 * BH, TT])
        soft = sb("soft", [P, 2 * BH, TT])
        gk = sb("gk", [P, 10, BH, TT])
        EG, KDEC, GLAST, BETA, GATE = 0, 2, 4, 6, 8
        ms = sb("ms", [P, 3, TT])

        work.at = 0
        hrow = work.take(2, D)
        junk = work.take(D)

        work.at = 0
        raw = work.take(3, S + 2 * HALO)
        cv = work.take(3, S)
        sg = work.take(3, S)
        qkv = [work.take(3, S) for _ in range(2)]
        sq = work.take(2, S)
        zr = work.take(S)
        sz = [work.take(S) for _ in range(2)]
        k_tok = work.take(TT, P)
        v_r = work.take(TT, P)
        gmask = work.take(2, TT, P)
        decay = work.take(2, TT, P)
        d_strict = work.take(2, TT, P)
        d_incl = work.take(2, TT, P)
        qkd = work.take(2, TT, P)
        pw = work.take(2, TT, P)
        pwT = work.take(2, TT, P)
        tT = work.take(2, TT, P)
        res = work.take(2, P)
        vn = work.take(2, P)
        vs = work.take(2, P)
        state = work.take(2, P)
        o_dir = gmask
        yb = decay[:, 0, :, :]
        yb_sq = decay[:, 1, :, :]
        hs = sb("head_scalars", [P, 10, TT])
        taps = sb("taps", [P, CK, 3])
        c1 = sb("c1", [P, 2, TT])
        nc1 = sb("nc1", [P, 2, TT])
        c2 = sb("c2", [P, 2, TT])
        neg_eg = sb("neg_eg", [P, 2, TT])
        ss = sb("ss", [P, 2, TT])
        rt = sb("rt", [P, 2, TT])
        rq = sb("rq", [P, TT])
        r2 = sb("r2", [P, TT])
        oms = sb("oms", [P, 3, TT])

        DW = S + (TT - 1) * P
        work.at = 0
        dist = work.take(DW)
        lnc = work.take(DW)
        t_i = work.take(DW).bitcast(I32)
        t_j = work.take(DW).bitcast(I32)
        t_a, t_b, t_c = work.take(DW), work.take(DW), work.take(DW)
        bias = [work.take(DW) for _ in range(2)]
        qa = [work.take(S) for _ in range(2)]
        ka = [work.take(S) for _ in range(2)]
        va = [work.take(TT, P) for _ in range(2)]
        sc = [work.take(S) for _ in range(2)]
        pr = [work.take(S) for _ in range(2)]
        pn = [work.take(S) for _ in range(2)]
        prT = [work.take(TT, S)]
        slope = sb("slope", [P, AH])
        nmx = sb("nmx", [P, 2 * TT])
        mx = sb("mx", [P, 2 * TT])
        lsum = sb("lsum", [P, 2 * TT])
        rl = sb("rl", [P, 2 * TT])

        work.at = 0
        mT = work.take(KD, S)
        sig = [work.take(2, S) for _ in range(2)]
        mab = [work.take(2, S) for _ in range(2)]
        wout = work.take(KD, D)

        mixer.at = 0
        mixer.take(KD, S)
        nw2 = mixer.take(D)
        h2 = mixer.take(2, D)
        hot_f32 = mixer.take(2, NE * P // 2)
        hot = [hot_f32[:, i, :].bitcast(F16).rearrange("p (e s) -> p e s", e=NE) for i in range(2)]
        bgu_rows = mixer.take(2 * FF)
        bd_rows = mixer.take(D)
        guT = mixer.take(2 * FT, NE)
        nwf = mixer.take(D)
        sgm = mixer.take(FT, P)
        actT = mixer.take(FT, P)
        mixer.at = 0
        xg = mixer.take(D)
        xgT = mixer.take(KD, P)
        glu = mixer.take(FT, P)
        lin = mixer.take(FT, P)
        yrow = h2[:, 0, :]
        orow = [h2[:, 0, :], h2[:, 1, :]]
        yg = [hot_f32[:, 0, 0:D], hot_f32[:, 0, D:2 * D], hot_f32[:, 1, 0:D], hot_f32[:, 1, D:2 * D]]
        rw = sb("rw", [P, KD, NE])
        rb = sb("rb", [P, NE])
        lg = sb("lg", [P, TT, NE])
        mx8 = sb("mx8", [P, TT, 8])
        ix8 = sb("ix8", [P, TT, 8], U32)
        idxf = sb("idxf", [P, TT, TOPK])
        ngt = sb("ngt", [P, TT])
        gsum = sb("gsum", [P, TT])
        gate = sb("gate", [P, TT, TOPK])
        i_slot = sb("i_slot", [P, P])
        i_slot_i = sb("i_slot_i", [P, P], I32)
        one_v, tmp_v = (a.rearrange("p f d -> p (f d)")[:, 0:TT * TOPK * NE] for a in (actT, sgm))
        onehot, tmp_hot = (v.rearrange("p (t j e) -> p t j e", t=TT, j=TOPK) for v in (one_v, tmp_v))
        m4 = sb("m4", [P, TT, NE])
        gmat = sb("gmat", [P, TT, NE])
        gmatT = sb("gmatT", [P, TT, P])
        rk = sb("rk", [P, TT, NE])
        rm = sb("rm", [P, TT, NE])
        rmr = sb("rmr", [P, TT, NE])
        posf = sb("posf", [P, TT, TOPK])
        rowf = sb("rowf", [P, TT, TOPK])
        later = sb("later", [P, TT, TOPK])
        pos = sb("pos", [P, TT * TOPK], I32)
        cnt_f = sb("cnt_f", [P, 1])
        cnt = sb("cnt", [P, 1], I32)
        tokid_i = sb("tokid_i", [P, TT], I32)
        tokid = sb("tokid", [P, TT], F16)
        tok_of = sb("tok_of", [P, NE], I32)
        idx_col = sb("idx_col", [P, 1], I32)
        waited = sb("waited", [P, 1])

        sems = {}

        def s(name):
            if name not in sems:
                sems[name] = sem(name)
            return sems[name]

        block = ctx.enter_context(nc.Block())

        def tiles_of(b):
            return bank(b).rearrange("p (t d) -> p t d", t=TT)

        def heads(eng, step):
            last = BH // 2 - 1
            with eng.Fori(0, last) as i:
                step(2 * i, i, 0, True)
                step(2 * i + 1, i, 1, True)
            step(BH - 2, last, 0, True)
            step(BH - 1, last, 1, False)

        def pairs(eng, step):
            for p in range(PAIRS):
                step(p, p // 2, p % 2, p < PAIRS - 1)

        def mixer_over(eng):
            eng.wait_ge(s("x1_added"), 2 * TT)

        def deltanet_over(eng):
            eng.wait_ge(s("ybT_ready"), BH)
            eng.wait_ge(s("silu_z"), BH)

        def attention_over(eng):
            eng.wait_ge(s("yaT_ready"), 2 * PAIRS)


        def head_cols(i):
            return 64 * (i + 1)

        def pair_cols(i):
            return head_cols(BH // 2 - 1) + 48 * (i + 1)

        def merge_cols(i):
            return pair_cols(PAIRS // 2 - 1) + 64 * (i + 1)

        def more_rounds(eng, one_round):
            eng.wait_ge(s("cnt_ready"), 1)
            largest = eng.value_load(cnt[0:1, 0:1], min_val=0, max_val=S)
            with eng.If(largest > P):
                with eng.Fori(1, ROUNDS) as r:
                    with eng.If(largest > r * P):
                        one_round(r)
                        eng.nop()
                    with eng.Else():
                        eng.nop()
                eng.nop()
            with eng.Else():
                eng.nop()

        gu_v = w_gate_up[0].rearrange("e (k p) c -> e k p c", p=P)
        dn_v = w_down[0].rearrange("e (c f p) d -> e c p f d", f=2, p=P)

        @block.sync
        def _(sp):
            for t in range(TT):
                sp.dma_start(xs[:, t, :], x[t * P:(t + 1) * P, :]).then_inc(s("x_loaded"), 16)
            sp.dma_start(vec_rows[0:CONVS, :], conv_w[0].rearrange("k (c p) -> (k c) p", p=P))\
                .then_inc(s("params_loaded"), 16)
            sp.dma_start(vec_rows[CONVS:P, :], norm1_w[0].rearrange("(k p) -> k p", p=P))\
                .then_inc(s("params_loaded"), 16)
            sp.dma_start(wab[:, :, :], w_in_v[:, :, COL_AB:COL_AB + 4 * BH]).then_inc(s("params_loaded"), 16)
            for i, v in enumerate((dt_bias_f, dt_bias_b, a_log_f, a_log_b)):
                sp.dma_start(gate_c[:, i, :], v[0].partition_broadcast(P)).then_inc(s("params_loaded"), 16)
            sp.dma_start(gnw[:, :], gdn_norm_w[0].rearrange("(p a) -> p a", a=1)).then_inc(s("params_loaded"), 16)

            def load_cols(b, parts):
                for i, (view, tiles, col) in enumerate(parts):
                    sp.dma_start(wcols[b][:, i, 0:tiles, :], view[:, :, ds(col, P)])\
                        .then_inc(s(f"wcols_loaded{b}"), 16)

            def load_head(h, b):
                load_cols(b, [(w_in_v, KD, c + h * P) for c in (COL_QB, COL_KB, COL_VB, COL_Z)])

            def load_pair(p, b):
                load_cols(b, [(w_in_v, KD, c + p * P) for c in (COL_QA, COL_KA, COL_VA)])

            def load_merge(n, b):
                load_cols(b, [(w_in_v, KD, COL_GA + n * P), (w_in_v, KD, COL_GB + n * P),
                              (wa_v, PAIRS, n * P), (wb_v, KD, n * P)])

            load_head(0, 0)
            load_head(1, 1)
            with sp.Fori(0, BH // 2 - 1) as i:
                for b in range(2):
                    sp.wait_ge(s("proj_z"), 2 * i + b + 1)
                    load_head(2 * i + b + 2, b)
            for p in range(PAIRS):
                if p < 2:
                    sp.wait_ge(s("proj_z"), BH - 1 + p)
                else:
                    sp.wait_ge(s("proj_va"), p - 1)
                load_pair(p, p % 2)
            for n in range(2):
                sp.wait_ge(s("proj_va"), PAIRS - 1 + n)
                load_merge(n, n)
            attention_over(sp)
            sp.dma_start(wout, wo_v).then_inc(s("wout_loaded"), 16)
            with sp.Fori(0, KD // 2 - 1) as i:
                for b in range(2):
                    sp.wait_ge(s("merge_ps"), 2 * i + b + 1)
                    load_merge(2 * i + b + 2, b)
            mixer_over(sp)
            sp.dma_start(nw2, norm2_w[0].partition_broadcast(P)).then_inc(s("late_params_loaded"), 16)
            sp.dma_start(rw[:, :, :], router_w[0].rearrange("(k p) e -> p k e", p=P)).then_inc(s("late_params_loaded"), 16)
            sp.dma_start(rb[:, :], router_b[0].partition_broadcast(P)).then_inc(s("late_params_loaded"), 16)
            sp.dma_start(bgu_rows[0:NE, :], b_gate_up[0]).then_inc(s("late_params_loaded"), 16)
            sp.dma_start(bd_rows[0:NE, :], b_down[0]).then_inc(s("late_params_loaded"), 16)
            sp.dma_start(nwf, norm_f_w.partition_broadcast(P)).then_inc(s("late_params_loaded"), 16)

            def load_gate_up(n, e):
                for c in range(KD):
                    if not (isinstance(n, int) and n == 0):
                        sp.wait_ge(s("gu_used"), KD * (n - 1) + c + 1)
                    sp.dma_start(slots[c], gu_v[ds(e, 1), c]).then_inc(s(f"slot_loaded{c}"), 16)

            def load_down(n, e):
                for c in range(FT // 2):
                    if not (isinstance(n, int) and n == 0):
                        sp.wait_ge(s("down_used"), FT // 2 * (n - 1) + c + 1)
                    sp.dma_start(slots[KD + c].rearrange("p (f d) -> p f d", f=2), dn_v[ds(e, 1), c])\
                        .then_inc(s(f"slot_loaded{KD + c}"), 16)

            load_gate_up(0, 0)
            load_down(0, 0)
            for t in range(TT):
                sp.wait_ge(s("h2_ready"), t + 1)
                sp.dma_start(h2_dram[t * P:(t + 1) * P, :], h2[:, t % 2, :]).then_inc(s(f"h2_stored{t % 2}"), 16)

            def sp_rest(n0):
                load_gate_up(n0 + 1, 1)
                with sp.Fori(1, NE - 1) as e:
                    load_gate_up(n0 + e + 1, e + 1)
                    load_down(n0 + e, e)
                load_down(n0 + NE - 1, NE - 1)

            sp_rest(0)

            def sp_round(r):
                load_gate_up(r * NE, 0)
                load_down(r * NE, 0)
                sp_rest(r * NE)

            more_rounds(sp, sp_round)
            for t in range(TT):
                sp.wait_ge(s("out_ready"), t + 1)
                sp.dma_start(out[t * P:(t + 1) * P, :], orow[t % 2]).then_inc(s(f"out_stored{t % 2}"), 16)
            for b in range(2):
                sp.wait_ge(s(f"out_stored{b}"), 16 * TT // 2)

        @block.gpsimd
        def _(pool):
            pool.memset(ones[:, :], 1.0).then_inc(s("pool_setup"), 1)
            pool.wait_ge(s("pool_setup"), 1)
            for m, base, per_col, per_row in ((upper_incl, 0, 1, -1), (upper_strict, -1, 1, -1),
                                              (lower_incl, 0, -1, 1), (lower_strict, -1, -1, 1)):
                pool.affine_select(out=m[:, :], in_=ones[:, :], pattern=[[per_col, P]], base=base,
                                   channel_multiplier=per_row, compare_op=ALU.is_ge, fill=0.0)\
                    .then_inc(s("pool_setup"), 1)
            pool.wait_ge(s("pool_setup"), 5)
            pool.tensor_tensor(ident[:, :], upper_incl[:, :], upper_strict[:, :], ALU.subtract)\
                .then_inc(s("pool_setup"), 1)
            pool.iota(i_slot_i[:, :], [[1, P]], base=0, channel_multiplier=0).then_inc(s("pool_setup"), 1)
            pool.iota(tokid_i[:, :], [[P, TT]], base=0, channel_multiplier=1).then_inc(s("pool_setup"), 1)
            pool.wait_ge(s("pool_setup"), 8)
            pool.tensor_copy(i_slot[:, :], i_slot_i[:, :]).then_inc(s("pool_setup"), 1)
            pool.tensor_copy(tokid[:, :], tokid_i[:, :]).then_inc(s("pool_setup"), 1)
            for h in range(AH):
                pool.memset(slope[:, h:h + 1], -SLOPES[h]).then_inc(s("pool_setup"), 1)

            def head(h, i, b, nxt):
                pool.wait_ge(s("hs_ready"), h + 1)
                for d, m in ((FWD, upper_incl), (BWD, lower_incl)):
                    pool.tensor_tensor(gmask[:, d], wide(m[:, :].unsqueeze(1), [P, TT, P]),
                                       wide(hs[:, GATE + d, :].unsqueeze(2), [P, TT, P]), ALU.mult)\
                        .then_inc(s("gmask_ready"), 1)
                for d, strict, incl in ((FWD, upper_strict, upper_incl), (BWD, lower_strict, lower_incl)):
                    pool.wait_ge(s("decay_ready"), 2 * h + d + 1)
                    pool.tensor_tensor(d_strict[:, d], decay[:, d], wide(strict[:, :].unsqueeze(1), [P, TT, P]),
                                       ALU.mult).then_inc(s("masked"), 1)
                    pool.tensor_tensor(d_incl[:, d], decay[:, d], wide(incl[:, :].unsqueeze(1), [P, TT, P]),
                                       ALU.mult).then_inc(s("masked"), 1)

            pool.wait_ge(s("hT_ready"), TT)
            pool.memset(raw[:, :, 0:HALO], 0.0).then_inc(s("pool_setup"), 1)
            pool.memset(raw[:, :, HALO + S:], 0.0).then_inc(s("pool_setup"), 1)
            heads(pool, head)

            deltanet_over(pool)
            pool.iota(t_i, [[1, DW]], base=-(TT - 1) * P, channel_multiplier=-1).then_inc(s("pool_setup"), 1)
            pool.iota(t_j, [[1, DW]], base=P, channel_multiplier=-1).then_inc(s("pool_setup"), 1)

            def take_wait():
                pool.tensor_tensor(waited[:, :], ones[:, 0:1], ones[:, 0:1], ALU.mult)

            def gathers(n, e):
                if not (isinstance(n, int) and n == 0):
                    pool.wait_ge(s("xgT_ps"), n)
                    pool.wait_ge(s("xg_loaded"), 16 * n)
                pool.tensor_copy(idx_col[:, :], tok_of[:, ds(e, 1)]).then_inc(s("idx_ready"), 1)
                pool.wait_ge(s("idx_ready"), n + 1)
                take_wait()
                pool.indirect_dma_start(xg, None, h2_dram, bass.IndirectOffsetOnAxis(ap=idx_col[:, 0:1], axis=0))\
                    .then_inc(s("xg_loaded"), 16)

            def pool_round(r):
                pool.wait_ge(s("tok_of_ready"), r + 1)
                take_wait()
                if isinstance(r, int):
                    gathers(0, 0)
                    with pool.Fori(1, NE) as e:
                        gathers(e, e)
                else:
                    with pool.Fori(0, NE) as e:
                        gathers(r * NE + e, e)
                pool.wait_ge(s("y_stored"), (r * NE + NE) * 16)

            for b in range(2):
                pool.wait_ge(s(f"h2_stored{b}"), 16 * TT // 2)
            pool_round(0)
            more_rounds(pool, pool_round)

            def results(rounds):
                for t in range(TT):
                    for j in range(TOPK):
                        k = t * TOPK + j
                        if t:
                            pool.wait_ge(s("y_added"), k - TOPK + 1)
                        pool.indirect_dma_start(yg[j], None, y_dram[0:rounds * NE * P, :],
                                                bass.IndirectOffsetOnAxis(ap=pos[:, k:k + 1], axis=0))\
                            .then_inc(s(f"yg_loaded{j}"), 16)

            def results_of(rounds, largest):
                if rounds == ROUNDS:
                    results(rounds)
                    return
                with pool.If(largest > rounds * P):
                    results_of(rounds + 1, largest)
                    pool.nop()
                with pool.Else():
                    results(rounds)

            pool.wait_ge(s("pos_ready"), 1)
            results_of(1, pool.value_load(cnt[0:1, 0:1], min_val=0, max_val=S))

        @block.tensor
        def _(pe):
            def mm(o, lhsT, rhs, start=True, stop=True, **kw):
                return nc.tensor.matmul(o, lhsT, rhs, start=start, stop=stop, **kw)

            pe.wait_ge(s("pool_setup"), 6)
            pe.wait_ge(s("params_loaded"), 128)
            nc.tensor.transpose(bank(6)[:, 0:P], vec_rows[:, :], ident[:, :]).then_inc(s("vecT_ps"), 1)

            def to_features(t, source, ready, free, name):
                pe.wait_ge(s(ready), t + 1)
                if t >= 2:
                    pe.wait_ge(s(free), t - 1)
                two = ps[:, 2 * (t % 2):2 * (t % 2) + 2, :].rearrange("p b (u d) -> p (b u) d", d=P)
                for k in range(KD):
                    last = nc.tensor.transpose(two[:, k, :], source[:, t % 2, k * P:(k + 1) * P], ident[:, :])
                last.then_inc(s(name), 1)

            for t in range(TT):
                to_features(t, hrow, "hrow_ready", "hT_ready", "hT_ps")

            pe.wait_ge(s("params_loaded"), 128)
            pe.wait_ge(s("hT_ready"), TT)
            for t in range(TT):
                for k in range(KD):
                    last = mm(bank(4)[:, t * 4 * BH:(t + 1) * 4 * BH], hT[:, k, t * P:(t + 1) * P],
                              wab[:, k, :], k == 0, k == KD - 1)
            last.then_inc(s("ab_ps"), 1)
            pe.wait_ge(s("gates_dve"), 10)
            W = BH * TT
            for j, (m, d) in enumerate(((upper_incl, FWD), (lower_incl, BWD), (lower_strict, FWD),
                                        (upper_strict, BWD), (ones, FWD), (ones, BWD))):
                last = mm(bank(5)[:, j * W:(j + 1) * W], m[:, :],
                          gk[:, GATE + d].rearrange("p h t -> p (h t)"))
            last.then_inc(s("cum_ps"), 1)

            def proj_qkv(h, i, b, part):
                if part == 0:
                    pe.wait_ge(s(f"wcols_loaded{b}"), head_cols(i))
                if not (isinstance(h, int) and h == 0 and part < 2):
                    if part == 0:
                        pe.wait_ge(s("raw_ready"), 3 * h)
                    elif part == 1:
                        pe.wait_ge(s("z_raw"), h)
                        pe.wait_ge(s("scalars_ready"), 9 * (h - 1) + 1)
                    else:
                        pe.wait_ge(s("raw_ready"), 3 * h + 1)
                for k in range(KD):
                    last = mm(bank(part % 2), wcols[b][:, part, k, :], hT[:, k, :], k == 0, k == KD - 1)
                last.then_inc(s("proj_qkv"), 1)

            def proj_z(h, b):
                pe.wait_ge(s("raw_ready"), 3 * h + 2)
                for t in range(TT):
                    for k in range(KD):
                        last = mm(tiles_of(1)[:, t, :], hT[:, k, t * P:(t + 1) * P], wcols[b][:, 3, k, :],
                                  k == 0, k == KD - 1)
                last.then_inc(s("proj_z"), 1)

            kq = ps[:, 4:6, :].rearrange("p b (u w i) -> p (b u) w i", u=2, w=2)

            def head(h, i, b, nxt):
                hn, bn = h + 1, 1 - b
                i_n = i + b
                q, k, v = qkv[b][:, 0, :], qkv[b][:, 1, :], qkv[b][:, 2, :]

                def tile(a, t):
                    return a[:, t * P:(t + 1) * P]

                pe.wait_ge(s("sq_ready"), h + 1)
                pe.wait_ge(s("z_raw"), h + 1)
                for w in range(2):
                    for t in range(TT):
                        last = mm(bank(1)[:, w * TT + t:w * TT + t + 1], tile(sq[:, w, :], t), ones[:, 0:1])
                last.then_inc(s("ss_ps"), 1)
                for d, m in ((FWD, lower_strict), (BWD, upper_strict)):
                    pe.wait_ge(s("gmask_ready"), 2 * h + d + 1)
                    mm(bank(6 + d), m[:, :], gmask[:, d].rearrange("p t i -> p (t i)")).then_inc(s("decay_ps"), 1)
                for t in range(TT):
                    nc.tensor.transpose(tiles_of(2)[:, t, :], tile(k, t), ident[:, :])
                for t in range(TT):
                    last = nc.tensor.transpose(tiles_of(3)[:, t, :], tile(v, t), ident[:, :])
                last.then_inc(s("kv_tok_ps"), 1)
                qk = qkv[b][:, 0:2, :].rearrange("p w (t i) -> p w t i", t=TT)
                for t in range(TT):
                    last = mm(kq[:, t], tile(k, t), qk[:, :, t, :])
                last.then_inc(s("kq_ps"), 1)
                if nxt:
                    proj_qkv(hn, i_n, bn, 0)

                for d in (FWD, BWD):
                    pe.wait_ge(s("pT_made"), 2 * h + d + 1)
                    if d == FWD:
                        pe.wait_ge(s("k_tok_ready"), h + 1)
                    else:
                        pe.wait_ge(s("scalars_ready"), 9 * h + 7)
                    for t in range(TT):
                        last = nc.tensor.transpose(tiles_of(2 + d)[:, t, :], pwT[:, d, t, :], ident[:, :])
                    last.then_inc(s(f"pw_ps{d}"), 1)

                def squares(d, n):
                    pe.wait_ge(s(f"pw_ready{d}"), h * (LEVELS + 1) + n)
                    if n > 1:
                        pe.wait_ge(s(f"pwT_ready{d}"), h * (LEVELS - 1) + n - 1)
                    for t in range(TT):
                        last = mm(tiles_of(2 + d)[:, t, :], pwT[:, d, t, :], pw[:, d, t, :])
                    last.then_inc(s(f"pw_ps{d}"), 1)
                    if n < LEVELS:
                        if n == 1:
                            pe.wait_ge(s("qkd_ready"), 2 * h + 2)
                        for t in range(TT):
                            last = mm(tiles_of(4 + d)[:, t, :], pw[:, d, t, :], pwT[:, d, t, :])
                        last.then_inc(s(f"pwT_ps{d}"), 1)

                def grow(d, n):
                    pe.wait_ge(s(f"pw_ready{d}"), h * (LEVELS + 1) + n + 1)
                    pe.wait_ge(s(f"tT_ready{d}"), h * (LEVELS + 1) + n)
                    for t in range(TT):
                        last = mm(tiles_of(6 + d)[:, t, :], pw[:, d, t, :], tT[:, d, t, :])
                    last.then_inc(s(f"tT_ps{d}"), 1)

                for d in (FWD, BWD):
                    squares(d, 1)
                for n in range(1, LEVELS + 1):
                    if n == 3 and nxt:
                        proj_qkv(hn, i_n, bn, 1)
                    for d in (FWD, BWD):
                        grow(d, n)
                        if n < LEVELS:
                            squares(d, n + 1)

                def scan(step):
                    for d in (FWD, BWD):
                        t = step if d == FWD else TT - 1 - step
                        bk = bank(2 + d)
                        if step:
                            pe.wait_ge(s("state_ready"), 2 * ((TT - 1) * h + step - 1) + d + 1)
                            mm(bk[:, 0:P], tile(k, t), state[:, d, :])
                            if step > 1:
                                pe.wait_ge(s("qs_ready"), 2 * ((TT - 1) * h + step - 2) + d + 1)
                            mm(bank(6 + d)[:, 0:P], tile(q, t), state[:, d, :]).then_inc(s("ks_ps"), 1)
                    for d in (FWD, BWD):
                        t = step if d == FWD else TT - 1 - step
                        if step:
                            pe.wait_ge(s("res_ready"), 2 * ((TT - 1) * h + step - 1) + d + 1)
                        else:
                            pe.wait_ge(s(f"tT_ready{d}"), (h + 1) * (LEVELS + 1))
                            pe.wait_ge(s(f"pw_ready{d}"), (h + 1) * (LEVELS + 1))
                        mm(bank(2 + d)[:, 2 * P:3 * P], tT[:, d, t, :], res[:, d, :] if step else v_r[:, t, :])\
                            .then_inc(s("y_ps"), 1)
                    for d in (FWD, BWD):
                        t = step if d == FWD else TT - 1 - step
                        pe.wait_ge(s("vn_ready"), 2 * (TT * h + step) + d + 1)
                        last = mm(bank(4 + d)[:, 0:P], qkd[:, d, t, :], vn[:, d, :])
                        if step < TT - 1:
                            pe.wait_ge(s("vs_ready"), 2 * ((TT - 1) * h + step) + d + 1)
                            last = mm(bank(4 + d)[:, P:2 * P], k_tok[:, t, :], vs[:, d, :])
                        last.then_inc(s("os_ps"), 1)

                scan(0)
                scan(1)
                if nxt:
                    proj_qkv(hn, i_n, bn, 2)
                scan(2)
                scan(3)
                if nxt:
                    proj_z(hn, bn)
                pe.wait_ge(s("tail"), 8 * h + 8)
                for t in range(TT):
                    last = nc.tensor.transpose(tiles_of(6)[:, t, :], yb[:, t, :], ident[:, :])
                last.then_inc(s("ybT_ps"), 1)

            proj_qkv(0, 0, 0, 0)
            proj_qkv(0, 0, 0, 1)
            proj_qkv(0, 0, 0, 2)
            proj_z(0, 0)
            heads(pe, head)

            def proj_pair(p, i, b):
                pe.wait_ge(s(f"wcols_loaded{b}"), pair_cols(i))
                for part in range(2):
                    if p:
                        pe.wait_ge(s("qkva_ready"), 3 * p - (2 if part == 0 else 1))
                        if part == 0:
                            pe.wait_ge(s("qkva_ready"), 3 * p)
                    else:
                        pe.wait_ge(s("z_raw"), BH)
                    for k in range(KD):
                        last = mm(bank(part), wcols[b][:, part, k, :], hT[:, k, :], k == 0, k == KD - 1)
                    last.then_inc(s("proj_qka"), 1)
                pe.wait_ge(s("qkva_ready"), 3 * p + 1)
                for t in range(TT):
                    for k in range(KD):
                        last = mm(tiles_of(0)[:, t, :], hT[:, k, t * P:(t + 1) * P], wcols[b][:, 2, k, :],
                                  k == 0, k == KD - 1)
                last.then_inc(s("proj_va"), 1)

            deltanet_over(pe)
            proj_pair(0, 0, 0)
            U = 2 * TT

            def scores(p, b, u):
                hh, t = divmod(u, TT)
                n = U * p + u
                rows = slice(ADH * hh, ADH * hh + ADH)
                if n >= 2:
                    pe.wait_ge(s("sc_ready"), n - 1)
                mm(bank(2 + u % 2), qa[b][rows, t * P:(t + 1) * P], ka[b][rows, :]).then_inc(s("sc_ps"), 1)

            def pair(p, i, b, nxt):
                pe.wait_ge(s("qkva_ready"), 3 * p + 3)
                scores(p, b, 0)
                scores(p, b, 1)
                for u in range(U):
                    hh, t = divmod(u, TT)
                    n = U * p + u
                    pe.wait_ge(s("pn_ready"), n + 1)
                    if n >= 2:
                        pe.wait_ge(s("prT_ready"), n - 1)
                    for j in range(TT):
                        last = nc.tensor.transpose(tiles_of(4 + u % 2)[:, j, :], pn[u % 2][:, j * P:(j + 1) * P],
                                                   ident[:, :])
                    last.then_inc(s("prT_ps"), 1)
                    if u + 2 < U:
                        scores(p, b, u + 2)
                    if u == 5 and nxt:
                        proj_pair(p + 1, i + b, 1 - b)
                    if t == TT - 1:
                        pe.wait_ge(s("prT_ready"), n + 1)
                        if 2 * p + hh >= 2:
                            pe.wait_ge(s("yaT_ready"), 2 * p + hh - 1)
                        for j in range(TT):
                            last = mm(ps[ADH * hh:ADH * hh + ADH, 6 + hh, :], va[b][:, j, ADH * hh:ADH * hh + ADH],
                                      prT[0][:, j, :], j == 0, j == TT - 1)
                        last.then_inc(s("pv_ps"), 1)

            pairs(pe, pair)

            attention_over(pe)

            def merge(n, i, b):
                pe.wait_ge(s(f"wcols_loaded{b}"), merge_cols(i))
                if not (isinstance(i, int) and i == 0):
                    pe.wait_ge(s("mT_ready"), n - 1)
                for j, (tiles, rhs) in enumerate(((KD, hT), (KD, hT), (PAIRS, yaT), (KD, ybT))):
                    for k in range(tiles):
                        last = mm(bank(4 * b + j), wcols[b][:, j, k, :], rhs[:, k, :], k == 0, k == tiles - 1)
                last.then_inc(s("merge_ps"), 1)

            merge(0, 0, 0)
            merge(1, 0, 1)
            with pe.Fori(1, KD // 2) as i:
                merge(2 * i, i, 0)
                merge(2 * i + 1, i, 1)
            pe.wait_ge(s("mT_ready"), KD)
            pe.wait_ge(s("wout_loaded"), 16)
            for t in range(TT):
                for half in range(2):
                    for k in range(KD):
                        last = mm(bank(2 * t + half), mT[:, k, t * P:(t + 1) * P],
                                  wout[:, k, half * 512:(half + 1) * 512], k == 0, k == KD - 1)
                    last.then_inc(s("x1_ps"), 1)
            pe.wait_ge(s("x1_added"), 2 * TT)
            for t in range(TT):
                to_features(t, h2, "h2_ready", "h2T_ready", "h2T_ps")
            pe.wait_ge(s("h2T_ready"), TT)
            pe.wait_ge(s("late_params_loaded"), 96)
            for t in range(TT):
                for k in range(KD):
                    last = mm(bank(4)[:, t * NE:(t + 1) * NE], hT[:, k, t * P:(t + 1) * P], rw[:, k, :],
                              k == 0, k == KD - 1)
            last.then_inc(s("logits_ps"), 1)
            pe.wait_ge(s("late_params_loaded"), 96)
            for f in range(2 * FT):
                last = nc.tensor.transpose(bank(5)[:, f * NE:(f + 1) * NE], bgu_rows[0:NE, f * P:(f + 1) * P],
                                           ident[0:NE, 0:NE])
            last.then_inc(s("guT_ps"), 1)
            pe.wait_ge(s("m4_ready"), 1)
            for t in range(TT):
                for u in range(t + 1):
                    last = mm(bank(6)[:, t * NE:(t + 1) * NE], (upper_strict if u == t else ones)[:, :],
                              m4[:, u, :], u == 0, u == t)
            for t in range(TT):
                last = mm(bank(7)[:, 0:NE], ones[:, :], m4[:, t, :], t == 0, t == TT - 1)
            last.then_inc(s("rank_ps"), 1)
            pe.wait_ge(s("gmat_ready"), 1)
            for t in range(TT):
                last = nc.tensor.transpose(ps[0:NE, 4, t * P:(t + 1) * P], gmat[:, t, :], ident[:, :])
            last.then_inc(s("gmatT_ps"), 1)

            def slot_tokens(r):
                for t in range(TT):
                    pe.wait_ge(s("hot_ready"), r * TT + t + 1)
                    for e in range(NE):
                        last = mm(bank(7)[:, e:e + 1], hot[t % 2][:, e, :], tokid[:, t:t + 1],
                                  t == 0 and e == 0, t == TT - 1, skip_group_check=True)
                    last.then_inc(s("tok_ps"), 1)

            def xg_to_features(n):
                pe.wait_ge(s("xg_loaded"), 16 * n + 16)
                for k in range(KD):
                    last = nc.tensor.transpose(ps[:, 4 + k // 4, (k % 4) * P:(k % 4 + 1) * P],
                                               xg[:, k * P:(k + 1) * P], ident[:, :])
                last.then_inc(s("xgT_ps"), 1)

            def gate_up(n):
                pe.wait_ge(s("xgT_ready"), n + 1)
                if not (isinstance(n, int) and n == 0):
                    pe.wait_ge(s("gu_read"), 2 * n)
                for k in range(KD):
                    pe.wait_ge(s(f"slot_loaded{k}"), 16 * n + 16)
                    for f in range(2 * FT):
                        last = mm(tiles_of(f // 4)[:, f % 4, :], slots[k][:, f * P:(f + 1) * P], xgT[:, k, :],
                                  k == 0 and f % 4 == 0, k == KD - 1, skip_group_check=True)
                    last.then_inc(s("gu_used"), 1)

            def down(n):
                pe.wait_ge(s("act_ready"), n + 1)
                if not (isinstance(n, int) and n == 0):
                    pe.wait_ge(s("y_read"), n)
                for c in range(FT // 2):
                    pe.wait_ge(s(f"slot_loaded{KD + c}"), 16 * n + 16)
                    w = slots[KD + c].rearrange("p (f d) -> p f d", f=2)
                    for f in (2 * c, 2 * c + 1):
                        for half in range(2):
                            last = mm(bank(6 + half), actT[:, f, :], w[:, f % 2, half * 512:(half + 1) * 512],
                                      f == 0, f == FT - 1)
                    last.then_inc(s("down_used"), 1)

            def pe_round(r):
                n0 = r * NE
                slot_tokens(r)
                pe.wait_ge(s("tok_of_ready"), r + 1)
                if isinstance(r, int):
                    pe.wait_ge(s("gmatT_ready"), 1)
                xg_to_features(n0)
                gate_up(n0)
                xg_to_features(n0 + 1)
                with pe.Fori(1, NE - 1) as e:
                    gate_up(n0 + e)
                    xg_to_features(n0 + e + 1)
                    down(n0 + e - 1)
                gate_up(n0 + NE - 1)
                down(n0 + NE - 2)
                down(n0 + NE - 1)

            pe_round(0)
            more_rounds(pe, pe_round)
            pe.wait_ge(s("y_all_read"), 1)
            for t in range(TT):
                for half in range(2):
                    mm(bank(2 * t + half), gmatT[0:NE, t, :], bd_rows[0:NE, half * 512:(half + 1) * 512])\
                        .then_inc(s("bd_ps"), 1)

        @block.scalar
        def _(act):
            A = nc.scalar.activation

            act.wait_ge(s("x_loaded"), 16 * TT)
            for t in range(TT):
                if t:
                    act.wait_ge(s("ms_sum"), t)
                A(junk, xs[:, t, :], ACT.Square, accum_out=ms[:, 0, t:t + 1]).then_inc(s("ms_sum"), 1)
            act.wait_ge(s("ms_eps"), 1)
            A(ms[:, 1, :], ms[:, 0, :], ACT.Sqrt).then_inc(s("ms_root"), 1)
            act.wait_ge(s("ms_inv"), 1)
            for t in range(TT):
                if t >= 2:
                    act.wait_ge(s("hT_ps"), t - 1)
                A(hrow[:, t % 2, :], xs[:, t, :], ACT.Copy, scale=ms[:, 2, t:t + 1]).then_inc(s("hrow_ready"), 1)

            act.wait_ge(s("gates_dve"), 4)
            act.wait_ge(s("params_loaded"), 128)
            A(soft[:, :, :], soft[:, :, :], ACT.Exp, scale=-1.0).then_inc(s("gates_act"), 1)
            A(gate_c[:, 2:4, :], gate_c[:, 2:4, :], ACT.Exp).then_inc(s("gates_act"), 1)
            A(ab[:, 2 * BH:4 * BH, :], ab[:, 2 * BH:4 * BH, :], ACT.Exp, scale=-1.0).then_inc(s("gates_act"), 1)
            act.wait_ge(s("gates_dve"), 5)
            A(soft[:, :, :], soft[:, :, :], ACT.Ln).then_inc(s("gates_act"), 1)
            act.wait_ge(s("cum_ps"), 1)
            A(gk[:, 0:GLAST + 2].rearrange("p k h t -> p (k h t)"), bank(5)[:, 0:6 * BH * TT], ACT.Exp)\
                .then_inc(s("gates_act"), 1)

            def evac_raw(h, part):
                act.wait_ge(s("proj_qkv"), 3 * h + part + 1)
                if not (isinstance(h, int) and h == 0):
                    act.wait_ge(s("tap"), CK * (3 * (h - 1) + part + 1))
                elif part == 0:
                    act.wait_ge(s("pool_setup"), 20)
                A(raw[:, part, HALO:HALO + S], bank(part % 2), ACT.Copy).then_inc(s("raw_ready"), 1)

            def evac_z(h):
                act.wait_ge(s("proj_z"), h + 1)
                if not (isinstance(h, int) and h == 0):
                    act.wait_ge(s("silu_z"), h)
                A(zr, bank(1), ACT.Copy).then_inc(s("z_raw"), 1)

            def silus(h, b):
                act.wait_ge(s("tap"), 3 * CK * (h + 1))
                act.wait_ge(s("silu_z"), h)
                A(sg, cv, ACT.Sigmoid).then_inc(s("sig_qkv"), 1)
                act.wait_ge(s("silu_qkv"), h + 1)
                act.wait_ge(s("z_raw"), h + 1)
                A(sg[:, 0, :], zr, ACT.Sigmoid).then_inc(s("sig_z"), 1)
                A(sq, qkv[b][:, 0:2, :], ACT.Square).then_inc(s("sq_ready"), 1)

            def head(h, i, b, nxt):
                hn, bn = h + 1, 1 - b
                act.wait_ge(s("scalars_ready"), 9 * h + 1)
                A(rt[:, :, :], ss[:, :, :], ACT.Sqrt).then_inc(s("rt_ready"), 1)
                for d in (FWD, BWD):
                    act.wait_ge(s("decay_ps"), 2 * h + d + 1)
                    A(decay[:, d].rearrange("p t i -> p (t i)"), bank(6 + d), ACT.Exp).then_inc(s("decay_ready"), 1)
                act.wait_ge(s("kv_tok_ps"), h + 1)
                A(k_tok.rearrange("p t d -> p (t d)"), bank(2), ACT.Copy).then_inc(s("k_tok_ready"), 1)
                if nxt:
                    evac_raw(hn, 0)

                def evac_pw(d, n):
                    act.wait_ge(s(f"pw_ps{d}"), h * (LEVELS + 1) + n + 1)
                    if 0 < n < LEVELS:
                        act.wait_ge(s(f"pwT_ps{d}"), h * (LEVELS - 1) + n)
                    A(pw[:, d].rearrange("p t i -> p (t i)"), bank(2 + d), ACT.Copy).then_inc(s(f"pw_ready{d}"), 1)
                    if n == 1:
                        act.wait_ge(s(f"tT_ready{d}"), h * (LEVELS + 1) + 1)
                    if 0 < n < LEVELS:
                        A(pwT[:, d].rearrange("p t i -> p (t i)"), bank(4 + d), ACT.Copy)\
                            .then_inc(s(f"pwT_ready{d}"), 1)

                for d in (FWD, BWD):
                    evac_pw(d, 0)
                for n in range(1, LEVELS + 1):
                    if n == 4 and nxt:
                        evac_raw(hn, 1)
                    for d in (FWD, BWD):
                        evac_pw(d, n)

                def scan(step):
                    for d in (FWD, BWD):
                        t = step if d == FWD else TT - 1 - step
                        if step:
                            act.wait_ge(s("ks_ps"), 2 * ((TT - 1) * h + step - 1) + d + 1)
                            A(o_dir[:, d, t, :], bank(6 + d)[:, 0:P], ACT.Copy, scale=hs[:, EG + d, t:t + 1])\
                                .then_inc(s("qs_ready"), 1)

                scan(1)
                scan(2)
                if nxt:
                    evac_raw(hn, 2)
                scan(3)
                if nxt:
                    evac_z(hn)
                act.wait_ge(s("tail"), 8 * h + 5)
                A(oms[:, 1, :], oms[:, 0, :], ACT.Sqrt).then_inc(s("oms_root"), 1)
                act.wait_ge(s("ybT_ps"), h + 1)
                A(ybT[:, ds(h, 1), :].rearrange("p a i -> p (a i)"), bank(6), ACT.Copy, scale=gnw[:, 0:1])\
                    .then_inc(s("ybT_ready"), 1)
                if nxt:
                    silus(hn, bn)

            act.wait_ge(s("params_loaded"), 128)
            for part in range(3):
                evac_raw(0, part)
            evac_z(0)
            silus(0, 0)
            heads(act, head)

            def evac_pair(p, b):
                act.wait_ge(s("proj_qka"), 2 * p + 1)
                A(qa[b], bank(0), ACT.Copy, scale=ADH ** -0.5).then_inc(s("qkva_ready"), 1)
                act.wait_ge(s("proj_qka"), 2 * p + 2)
                A(ka[b], bank(1), ACT.Copy).then_inc(s("qkva_ready"), 1)
                act.wait_ge(s("proj_va"), p + 1)
                A(va[b].rearrange("p t d -> p (t d)"), bank(0), ACT.Copy).then_inc(s("qkva_ready"), 1)

            evac_pair(0, 0)

            def pair(p, i, b, nxt):
                for u in range(2 * TT):
                    hh, t = divmod(u, TT)
                    n = 2 * TT * p + u
                    act.wait_ge(s("nmx_ready"), n + 1)
                    if n >= 2:
                        act.wait_ge(s("pn_ready"), n - 1)
                    A(pr[u % 2], sc[u % 2], ACT.Exp, bias=nmx[:, u:u + 1], accum_out=lsum[:, u:u + 1])\
                        .then_inc(s("pr_ready"), 1)
                    if u:
                        evac_prT(p, u - 1)
                    if u == 6 and nxt:
                        evac_pair(p + 1, 1 - b)
                evac_prT(p, 2 * TT - 1)

            def evac_prT(p, u):
                hh, t = divmod(u, TT)
                n = 2 * TT * p + u
                act.wait_ge(s("prT_ps"), n + 1)
                if t == 0 and n:
                    act.wait_ge(s("pv_ps"), 2 * p + hh)
                A(prT[0][:, :, t * P:(t + 1) * P], tiles_of(4 + u % 2), ACT.Copy).then_inc(s("prT_ready"), 1)

            pairs(act, pair)

            attention_over(act)

            def merge(n, i, b):
                act.wait_ge(s("merge_ps"), n + 1)
                A(sig[b].rearrange("p a i -> p (a i)"), ps[:, 4 * b:4 * b + 2, :].rearrange("p a i -> p (a i)"),
                  ACT.Sigmoid).then_inc(s("sig_ready"), 1)

            merge(0, 0, 0)
            merge(1, 0, 1)
            with act.Fori(1, KD // 2) as i:
                for b in range(2):
                    act.wait_ge(s("mab_ready"), 2 * i + b - 1)
                    merge(2 * i + b, i, b)

            for t in range(TT):
                act.wait_ge(s("x1_added"), 2 * t + 2)
                act.wait_ge(s("ms_sum"), TT + t)
                A(sgm.rearrange("p f d -> p (f d)"), xs[:, t, :], ACT.Square, accum_out=ms[:, 0, t:t + 1])\
                    .then_inc(s("ms_sum"), 1)
            act.wait_ge(s("ms_eps"), 2)
            A(ms[:, 1, :], ms[:, 0, :], ACT.Sqrt).then_inc(s("ms_root"), 1)
            for t in range(TT):
                act.wait_ge(s("h2T_ps"), t + 1)
                A(hT[:, :, t * P:(t + 1) * P], ps[:, 2 * (t % 2):2 * (t % 2) + 2, :]
                  .rearrange("p b (u d) -> p (b u) d", d=P), ACT.Copy).then_inc(s("h2T_ready"), 1)
            act.wait_ge(s("ngt_ready"), 1)
            for t in range(TT):
                A(gate[:, t, :], mx8[:, t, 0:TOPK], ACT.Exp, bias=ngt[:, t:t + 1], accum_out=gsum[:, t:t + 1])\
                    .then_inc(s("gate_exp"), 1)
            act.wait_ge(s("guT_ps"), 1)
            A(guT.rearrange("p f e -> p (f e)"), bank(5), ACT.Copy).then_inc(s("guT_ready"), 1)
            act.wait_ge(s("gmatT_ps"), 1)
            A(gmatT[0:NE, :, :], ps[0:NE, 4, :].rearrange("p (t d) -> p t d", t=TT), ACT.Copy)\
                .then_inc(s("gmatT_ready"), 1)

            def evac_xgT(n, first=False):
                act.wait_ge(s("xgT_ps"), n + 1)
                if not first:
                    act.wait_ge(s("gu_used"), KD * n)
                A(xgT.rearrange("p k d -> p (k d)"), ps[:, 4:6, :].rearrange("p b d -> p (b d)"), ACT.Copy)\
                    .then_inc(s("xgT_ready"), 1)

            def swish(n):
                act.wait_ge(s("swiglu"), 3 * n + 1)
                A(sgm, glu, ACT.Sigmoid, scale=ALPHA).then_inc(s("sgm_ready"), 1)

            def y_out(n, e, first=False):
                act.wait_ge(s("down_used"), FT // 2 * (n + 1))
                if not first:
                    act.wait_ge(s("y_stored"), 16 * n)
                A(yrow, ps[:, 6:8, :].rearrange("p b d -> p (b d)"), ACT.Copy).then_inc(s("y_read"), 1)
                act.wait_ge(s("y_read"), n + 1)
                act.dma_start(y_v[r_of[0], ds(e, 1)], yrow).then_inc(s("y_stored"), 16)

            y_v = y_dram.rearrange("(r e p) d -> r e p d", r=ROUNDS, p=P)
            r_of = [0]

            def act_round(r):
                n0 = r * NE
                r_of[0] = ds(r, 1)
                first = isinstance(r, int)
                if first:
                    for b in range(2):
                        act.wait_ge(s(f"h2_stored{b}"), 16 * TT // 2)
                evac_xgT(n0, first)
                evac_xgT(n0 + 1)
                swish(n0)
                evac_xgT(n0 + 2)
                swish(n0 + 1)
                y_out(n0, 0, first)
                with act.Fori(2, NE - 1) as e:
                    evac_xgT(n0 + e + 1)
                    swish(n0 + e)
                    y_out(n0 + e - 1, e - 1)
                swish(n0 + NE - 1)
                y_out(n0 + NE - 2, NE - 2)
                y_out(n0 + NE - 1, NE - 1)

            act_round(0)
            more_rounds(act, act_round)
            act.nop().then_inc(s("y_all_read"), 1)
            for t in range(TT):
                act.wait_ge(s("y_added"), TOPK * (t + 1))
                act.wait_ge(s("ms_sum"), 2 * TT + t)
                A(glu.rearrange("p k d -> p (k d)"), xs[:, t, :], ACT.Square, accum_out=ms[:, 0, t:t + 1])\
                    .then_inc(s("ms_sum"), 1)
                act.wait_ge(s("ms_eps"), 3 + t)
                A(ms[:, 1, t:t + 1], ms[:, 0, t:t + 1], ACT.Sqrt).then_inc(s("ms_root"), 1)

        @block.vector
        def _(dve):
            V = nc.vector

            def eps_and_inverse(k, view=slice(0, TT)):
                V.tensor_scalar(ms[:, 0, view], ms[:, 0, view], 1.0 / D, EPS, ALU.mult, ALU.add)\
                    .then_inc(s("ms_eps"), 1)
                dve.wait_ge(s("ms_root"), k)
                V.reciprocal(ms[:, 2, view], ms[:, 1, view]).then_inc(s("ms_inv"), 1)

            dve.wait_ge(s("vecT_ps"), 1)
            V.tensor_copy(vecT[:, :], bank(6)[:, 0:P]).then_inc(s("vecT_ready"), 1)
            dve.wait_ge(s("ms_sum"), TT)
            eps_and_inverse(1)
            dve.wait_ge(s("vecT_ready"), 1)
            for t in range(TT):
                dve.wait_ge(s("hT_ps"), t + 1)
                V.tensor_tensor(hT[:, :, t * P:(t + 1) * P],
                                ps[:, 2 * (t % 2):2 * (t % 2) + 2, :].rearrange("p b (u d) -> p (b u) d", d=P),
                                wide(vecT[:, CONVS:P].unsqueeze(2), [P, KD, P]), ALU.mult)\
                    .then_inc(s("hT_ready"), 1)

            dve.wait_ge(s("ab_ps"), 1)
            V.tensor_copy(ab[:, :, :], bank(4)[:, 0:TT * 4 * BH].rearrange("p (t c) -> p c t", t=TT))\
                .then_inc(s("gates_dve"), 1)
            dve.wait_ge(s("gates_dve"), 1)
            dve.wait_ge(s("params_loaded"), 128)
            a_part, b_part = ab[:, 0:2 * BH, :], ab[:, 2 * BH:4 * BH, :]
            V.tensor_tensor(a_part, a_part,
                            wide(gate_c[:, 0:2, :].rearrange("p a h -> p (a h)").unsqueeze(2), [P, 2 * BH, TT]),
                            ALU.add).then_inc(s("gates_dve"), 1)
            dve.wait_ge(s("gates_dve"), 2)
            V.tensor_scalar(soft[:, :, :], a_part, -1.0, None, ALU.mult).then_inc(s("gates_dve"), 1)
            dve.wait_ge(s("gates_dve"), 3)
            V.tensor_tensor(soft[:, :, :], soft[:, :, :], a_part, ALU.max).then_inc(s("gates_dve"), 1)
            dve.wait_ge(s("gates_act"), 3)
            V.tensor_scalar(soft[:, :, :], soft[:, :, :], 1.0, None, ALU.add).then_inc(s("gates_dve"), 1)
            V.tensor_scalar(b_part, b_part, 1.0, None, ALU.add).then_inc(s("gates_dve"), 1)
            dve.wait_ge(s("gates_dve"), 6)
            V.reciprocal(gk[:, BETA:BETA + 2].rearrange("p k h t -> p (k h) t"), b_part).then_inc(s("gates_dve"), 1)
            V.tensor_scalar(a_part, a_part, 0.0, None, ALU.max).then_inc(s("gates_dve"), 1)
            dve.wait_ge(s("gates_dve"), 8)
            dve.wait_ge(s("gates_act"), 4)
            V.tensor_tensor(soft[:, :, :], soft[:, :, :], a_part, ALU.add).then_inc(s("gates_dve"), 1)
            dve.wait_ge(s("gates_dve"), 9)
            V.scalar_tensor_tensor(out=gk[:, GATE:GATE + 2].rearrange("p k h t -> p (k h) t"), in0=soft[:, :, :],
                                   scalar=-1.0,
                                   in1=wide(gate_c[:, 2:4, :].rearrange("p a h -> p (a h)").unsqueeze(2),
                                            [P, 2 * BH, TT]),
                                   op0=ALU.mult, op1=ALU.mult).then_inc(s("gates_dve"), 1)

            def conv(h, part):
                n0 = CK * (3 * h + part)
                dve.wait_ge(s("raw_ready"), 3 * h + part + 1)
                if part == 0:
                    if not (isinstance(h, int) and h == 0):
                        dve.wait_ge(s("sig_qkv"), h)
                    V.tensor_copy(taps[:, :, :].rearrange("p k w -> p (k w)").unsqueeze(2),
                                  vecT[:, 0:CONVS].rearrange("p (k h) -> p k h", h=BH)[:, :, ds(h, 1)])\
                        .then_inc(s("taps_ready"), 1)
                    dve.wait_ge(s("taps_ready"), h + 1)
                V.tensor_scalar(cv[:, part, :], raw[:, part, 0:S], taps[:, 0, part:part + 1], None, ALU.mult)\
                    .then_inc(s("tap"), 1)
                for k in range(1, CK):
                    dve.wait_ge(s("tap"), n0 + k)
                    V.scalar_tensor_tensor(out=cv[:, part, :], in0=raw[:, part, k:k + S],
                                           scalar=taps[:, k, part:part + 1], in1=cv[:, part, :],
                                           op0=ALU.mult, op1=ALU.add).then_inc(s("tap"), 1)

            def silus(h, b):
                dve.wait_ge(s("sig_qkv"), h + 1)
                V.tensor_tensor(qkv[b], cv, sg, ALU.mult).then_inc(s("silu_qkv"), 1)
                dve.wait_ge(s("sig_z"), h + 1)
                V.tensor_tensor(sz[b], zr, sg[:, 0, :], ALU.mult).then_inc(s("silu_z"), 1)

            kq = ps[:, 4:6, :].rearrange("p b (u w i) -> p (b u) w i", u=2, w=2)

            def head_scalars(h):
                V.tensor_copy(hs[:, :, :].unsqueeze(2), gk[:, :, ds(h, 1), :]).then_inc(s("hs_ready"), 1)

            def head(h, i, b, nxt):
                hn, bn = h + 1, 1 - b
                dve.wait_ge(s("ss_ps"), h + 1)
                V.tensor_scalar(ss[:, :, :].rearrange("p w t -> p (w t)"), bank(1)[:, 0:2 * TT], EPS, None, ALU.add)\
                    .then_inc(s("scalars_ready"), 1)
                dve.wait_ge(s("scalars_ready"), 9 * h + 1)
                V.reciprocal(r2[:, :], ss[:, 1, :]).then_inc(s("scalars_ready"), 1)
                dve.wait_ge(s("scalars_ready"), 9 * h + 2)
                dve.wait_ge(s("hs_ready"), h + 1)
                V.tensor_tensor(c1[:, :, :], hs[:, BETA:BETA + 2, :], wide(r2[:, :].unsqueeze(1), [P, 2, TT]),
                                ALU.mult).then_inc(s("scalars_ready"), 1)
                V.tensor_scalar(neg_eg[:, :, :], hs[:, EG:EG + 2, :], -1.0, None, ALU.mult)\
                    .then_inc(s("scalars_ready"), 1)
                dve.wait_ge(s("scalars_ready"), 9 * h + 3)
                V.tensor_scalar(nc1[:, :, :], c1[:, :, :], -1.0, None, ALU.mult).then_inc(s("scalars_ready"), 1)
                V.tensor_tensor(c2[:, :, :], c1[:, :, :], hs[:, KDEC:KDEC + 2, :], ALU.mult).then_inc(s("scalars_ready"), 1)
                dve.wait_ge(s("rt_ready"), h + 1)
                dve.wait_ge(s("kv_tok_ps"), h + 1)
                V.tensor_tensor(v_r, tiles_of(3), wide(rt[:, 1, :].unsqueeze(2), [P, TT, P]), ALU.mult)\
                    .then_inc(s("scalars_ready"), 1)
                V.reciprocal(rq[:, :], rt[:, 0, :]).then_inc(s("scalars_ready"), 1)
                dve.wait_ge(s("scalars_ready"), 9 * h + 8)
                V.tensor_scalar(rq[:, :], rq[:, :], BDH ** -0.5, None, ALU.mult).then_inc(s("scalars_ready"), 1)
                dve.wait_ge(s("kq_ps"), h + 1)
                dve.wait_ge(s("scalars_ready"), 9 * h + 5)
                for d in (FWD, BWD):
                    dve.wait_ge(s("masked"), 4 * h + 2 * d + 1)
                    for t in range(TT):
                        last = V.scalar_tensor_tensor(out=pwT[:, d, t, :], in0=kq[:, t, 1, :],
                                                      scalar=nc1[:, d, t:t + 1], in1=d_strict[:, d, t, :],
                                                      op0=ALU.mult, op1=ALU.mult)
                    last.then_inc(s("pT_made"), 1)
                for d in (FWD, BWD):
                    dve.wait_ge(s("masked"), 4 * h + 2 * d + 2)
                    V.tensor_tensor(qkd[:, d], kq[:, :, 0, :], d_incl[:, d], ALU.mult).then_inc(s("qkd_ready"), 1)
                dve.wait_ge(s("pT_made"), 2 * h + 2)
                for d in (FWD, BWD):
                    V.tensor_tensor(tT[:, d], pwT[:, d], wide(ident[:, :].unsqueeze(1), [P, TT, P]), ALU.add)\
                        .then_inc(s(f"tT_ready{d}"), 1)
                if nxt:
                    conv(hn, 0)

                for n in range(1, LEVELS + 1):
                    for d in (FWD, BWD):
                        dve.wait_ge(s(f"tT_ps{d}"), h * LEVELS + n)
                        dve.wait_ge(s(f"tT_ready{d}"), h * (LEVELS + 1) + n)
                        V.tensor_tensor(tT[:, d], tT[:, d], tiles_of(6 + d), ALU.add).then_inc(s(f"tT_ready{d}"), 1)
                    if n == 4 and nxt:
                        conv(hn, 1)

                def scan(step):
                    for d in (FWD, BWD):
                        t = step if d == FWD else TT - 1 - step
                        if step:
                            dve.wait_ge(s("ks_ps"), 2 * ((TT - 1) * h + step - 1) + d + 1)
                            dve.wait_ge(s("scalars_ready"), 9 * h + 4)
                            V.scalar_tensor_tensor(out=res[:, d, :], in0=bank(2 + d)[:, 0:P],
                                                   scalar=neg_eg[:, d, t:t + 1], in1=v_r[:, t, :],
                                                   op0=ALU.mult, op1=ALU.add).then_inc(s("res_ready"), 1)
                    for d in (FWD, BWD):
                        t = step if d == FWD else TT - 1 - step
                        dve.wait_ge(s("y_ps"), 2 * (TT * h + step) + d + 1)
                        V.tensor_scalar(vn[:, d, :], bank(2 + d)[:, 2 * P:3 * P], c1[:, d, t:t + 1], None,
                                        ALU.mult).then_inc(s("vn_ready"), 1)
                        if step < TT - 1:
                            dve.wait_ge(s("scalars_ready"), 9 * h + 6)
                            V.tensor_scalar(vs[:, d, :], bank(2 + d)[:, 2 * P:3 * P], c2[:, d, t:t + 1], None,
                                            ALU.mult).then_inc(s("vs_ready"), 1)
                    for d in (FWD, BWD):
                        t = step if d == FWD else TT - 1 - step
                        dve.wait_ge(s("os_ps"), 2 * (TT * h + step) + d + 1)
                        if step == 0:
                            V.tensor_copy(state[:, d, :], bank(4 + d)[:, P:2 * P]).then_inc(s("state_ready"), 1)
                            V.tensor_copy(o_dir[:, d, t, :], bank(4 + d)[:, 0:P]).then_inc(s("o_done"), 1)
                        else:
                            if step < TT - 1:
                                V.scalar_tensor_tensor(out=state[:, d, :], in0=state[:, d, :],
                                                       scalar=hs[:, GLAST + d, t:t + 1],
                                                       in1=bank(4 + d)[:, P:2 * P], op0=ALU.mult, op1=ALU.add)\
                                    .then_inc(s("state_ready"), 1)
                            dve.wait_ge(s("qs_ready"), 2 * ((TT - 1) * h + step - 1) + d + 1)
                            V.tensor_tensor(o_dir[:, d, t, :], o_dir[:, d, t, :], bank(4 + d)[:, 0:P], ALU.add)\
                                .then_inc(s("o_done"), 1)

                scan(0)
                scan(1)
                scan(2)
                scan(3)
                dve.wait_ge(s("o_done"), 2 * TT * (h + 1))
                V.tensor_tensor(yb, o_dir[:, FWD], o_dir[:, BWD], ALU.add).then_inc(s("tail"), 1)
                dve.wait_ge(s("tail"), 8 * h + 1)
                dve.wait_ge(s("scalars_ready"), 9 * h + 9)
                V.tensor_tensor(yb, yb, wide(rq[:, :].unsqueeze(2), [P, TT, P]), ALU.mult).then_inc(s("tail"), 1)
                dve.wait_ge(s("tail"), 8 * h + 2)
                V.tensor_tensor(yb_sq, yb, yb, ALU.mult).then_inc(s("tail"), 1)
                dve.wait_ge(s("tail"), 8 * h + 3)
                V.tensor_reduce(oms[:, 2, :], yb_sq, AX.X, ALU.add).then_inc(s("tail"), 1)
                dve.wait_ge(s("tail"), 8 * h + 4)
                V.tensor_scalar(oms[:, 0, :], oms[:, 2, :], 1.0 / BDH, EPS, ALU.mult, ALU.add)\
                    .then_inc(s("tail"), 1)
                if nxt:
                    head_scalars(hn)
                    conv(hn, 2)
                dve.wait_ge(s("oms_root"), h + 1)
                V.reciprocal(oms[:, 2, :], oms[:, 1, :]).then_inc(s("tail"), 1)
                dve.wait_ge(s("tail"), 8 * h + 6)
                V.tensor_tensor(yb, yb, wide(oms[:, 2, :].unsqueeze(2), [P, TT, P]), ALU.mult)\
                    .then_inc(s("tail"), 1)
                dve.wait_ge(s("tail"), 8 * h + 7)
                dve.wait_ge(s("silu_z"), h + 1)
                V.tensor_tensor(yb, yb, sz[b].rearrange("p (t d) -> p t d", t=TT), ALU.mult)\
                    .then_inc(s("tail"), 1)
                if nxt:
                    silus(hn, bn)

            dve.wait_ge(s("gates_act"), 5)
            dve.wait_ge(s("gates_dve"), 7)
            dve.wait_ge(s("gates_dve"), 10)
            head_scalars(0)
            for part in range(3):
                conv(0, part)
            silus(0, 0)
            heads(dve, head)

            deltanet_over(dve)
            dve.wait_ge(s("pool_setup"), 22)
            V.tensor_copy(dist, t_i).then_inc(s("mk"), 1)
            made = [1]

            def mk(ins):
                ins.then_inc(s("mk"), 1)
                made[0] += 1
                dve.wait_ge(s("mk"), made[0])

            dve.wait_ge(s("mk"), 1)
            mk(V.tensor_scalar(t_a, dist, -1.0, None, ALU.mult))
            mk(V.tensor_tensor(dist, dist, t_a, ALU.max))
            for gi, (window, dilation) in enumerate(PATTERNS):
                reach = (window // (2 * dilation)) * dilation
                dst = lnc if gi == 0 else t_b
                mk(V.tensor_scalar(dst, dist, float(reach), None, ALU.is_le))
                if dilation > 1:
                    mk(V.tensor_scalar(t_i, t_j, dilation - 1, None, ALU.bitwise_and))
                    mk(V.tensor_copy(t_a, t_i))
                    mk(V.tensor_scalar(t_a, t_a, 0.0, None, ALU.is_equal))
                    mk(V.tensor_tensor(t_b, t_b, t_a, ALU.mult))
                    mk(V.tensor_tensor(lnc, lnc, t_b, ALU.add))
            mk(V.tensor_scalar(t_a, lnc, 2.0, math.log(2.0), ALU.is_equal, ALU.mult))
            mk(V.tensor_scalar(t_b, lnc, 3.0, math.log(3.0), ALU.is_equal, ALU.mult))
            mk(V.tensor_scalar(t_c, lnc, 0.0, MASKED, ALU.is_equal, ALU.mult))
            mk(V.tensor_tensor(t_a, t_a, t_b, ALU.add))
            mk(V.tensor_tensor(lnc, t_a, t_c, ALU.add))
            dve.wait_ge(s("pool_setup"), 18)

            def pair(p, i, b, nxt):
                for u in range(2 * TT):
                    hh, t = divmod(u, TT)
                    n = 2 * TT * p + u
                    if t == 0:
                        if n:
                            dve.wait_ge(s("sc_made"), n)
                        V.scalar_tensor_tensor(out=bias[hh], in0=dist, scalar=slope[:, 2 * p + hh:2 * p + hh + 1],
                                               in1=lnc, op0=ALU.mult, op1=ALU.add).then_inc(s("bias_ready"), 1)
                        dve.wait_ge(s("bias_ready"), 2 * p + hh + 1)
                    dve.wait_ge(s("sc_ps"), n + 1)
                    if n >= 2:
                        dve.wait_ge(s("pr_ready"), n - 1)
                    c0 = (TT - 1 - t) * P
                    V.tensor_tensor(sc[u % 2], bank(2 + u % 2), bias[hh][:, c0:c0 + S], ALU.add)\
                        .then_inc(s("sc_ready"), 1)
                    dve.wait_ge(s("sc_ready"), n + 1)
                    V.tensor_reduce(mx[:, u:u + 1], sc[u % 2], AX.X, ALU.max).then_inc(s("sc_made"), 1)
                    dve.wait_ge(s("sc_made"), n + 1)
                    V.tensor_scalar(nmx[:, u:u + 1], mx[:, u:u + 1], -1.0, None, ALU.mult).then_inc(s("nmx_ready"), 1)
                    if u:
                        normalise(p, u - 1)
                    if u in (TT, ):
                        pv_out(p, 0)
                normalise(p, 2 * TT - 1)
                pv_out(p, 1)

            def normalise(p, u):
                n = 2 * TT * p + u
                dve.wait_ge(s("pr_ready"), n + 1)
                V.reciprocal(rl[:, u:u + 1], lsum[:, u:u + 1]).then_inc(s("rl_ready"), 1)
                dve.wait_ge(s("rl_ready"), n + 1)
                if n >= 2:
                    dve.wait_ge(s("prT_ps"), n - 1)
                V.tensor_scalar(pn[u % 2], pr[u % 2], rl[:, u:u + 1], None, ALU.mult).then_inc(s("pn_ready"), 1)

            def pv_out(p, hh):
                rows = slice(ADH * hh, ADH * hh + ADH)
                dve.wait_ge(s("pv_ps"), 2 * p + hh + 1)
                V.tensor_copy(yaT[rows, p, :], ps[rows, 6 + hh, :]).then_inc(s("yaT_ready"), 1)

            pairs(dve, pair)

            attention_over(dve)

            def merge(n, i, b):
                dve.wait_ge(s("sig_ready"), n + 1)
                V.tensor_tensor(mab[b], sig[b], ps[:, 4 * b + 2:4 * b + 4, :], ALU.mult).then_inc(s("mab_ready"), 1)
                dve.wait_ge(s("mab_ready"), n + 1)
                V.tensor_tensor(mT[:, ds(n, 1), :].rearrange("p a i -> p (a i)"), mab[b][:, 0, :], mab[b][:, 1, :],
                                ALU.add).then_inc(s("mT_ready"), 1)

            with dve.Fori(0, KD // 2) as i:
                merge(2 * i, i, 0)
                merge(2 * i + 1, i, 1)
            for t in range(TT):
                for half in range(2):
                    dve.wait_ge(s("x1_ps"), 2 * t + half + 1)
                    cols = slice(half * 512, (half + 1) * 512)
                    V.tensor_tensor(xs[:, t, cols], xs[:, t, cols], bank(2 * t + half), ALU.add)\
                        .then_inc(s("x1_added"), 1)

            dve.wait_ge(s("ms_sum"), 2 * TT)
            eps_and_inverse(2)
            dve.wait_ge(s("ms_inv"), 2)
            dve.wait_ge(s("late_params_loaded"), 96)
            for t in range(TT):
                if t >= 2:
                    dve.wait_ge(s("h2T_ps"), t - 1)
                    dve.wait_ge(s(f"h2_stored{t % 2}"), 16)
                V.scalar_tensor_tensor(out=h2[:, t % 2, :], in0=xs[:, t, :], scalar=ms[:, 2, t:t + 1], in1=nw2,
                                       op0=ALU.mult, op1=ALU.mult).then_inc(s("h2_ready"), 1)
            made_r = [0]

            def rt_step(ins):
                ins.then_inc(s("routing"), 1)
                made_r[0] += 1
                dve.wait_ge(s("routing"), made_r[0])

            dve.wait_ge(s("logits_ps"), 1)
            rt_step(V.tensor_tensor(lg[:, :, :], bank(4)[:, 0:TT * NE].rearrange("p (t e) -> p t e", t=TT),
                                    wide(rb[:, :].unsqueeze(1), [P, TT, NE]), ALU.add))
            for t in range(TT):
                rt_step(V.max(mx8[:, t, :], lg[:, t, :]))
                rt_step(V.max_index(ix8[:, t, :], mx8[:, t, :], lg[:, t, :]))
            V.tensor_scalar(ngt[:, :].unsqueeze(2), mx8[:, :, 0:1], -1.0, None, ALU.mult).then_inc(s("ngt_ready"), 1)
            rt_step(V.tensor_copy(idxf[:, :, :], ix8[:, :, 0:TOPK]))
            dve.wait_ge(s("pool_setup"), 10)
            n_rep = TT * TOPK
            oh = onehot[:, :, :, :].rearrange("p t j e -> p (t j) e")
            th = tmp_hot[:, :, :, :].rearrange("p t j e -> p (t j) e")

            def each(a):
                return wide(a[:, :, :].rearrange("p t j -> p (t j)").unsqueeze(2), [P, n_rep, NE])

            rt_step(V.tensor_tensor(oh, wide(i_slot[:, 0:NE].unsqueeze(1), [P, n_rep, NE]), each(idxf), ALU.is_equal))
            V.tensor_reduce(m4[:, :, :], onehot[:, :, :, :].rearrange("p t j e -> p t e j"), AX.X, ALU.add)\
                .then_inc(s("m4_ready"), 1)
            dve.wait_ge(s("gate_exp"), TT)
            rt_step(V.reciprocal(gsum[:, :], gsum[:, :]))
            rt_step(V.tensor_tensor(gate[:, :, :], gate[:, :, :], wide(gsum[:, :].unsqueeze(2), [P, TT, TOPK]),
                                    ALU.mult))
            rt_step(V.tensor_tensor(th, oh, each(gate), ALU.mult))
            rt_step(V.tensor_reduce(gmat[:, :, :], tmp_hot[:, :, :, :].rearrange("p t j e -> p t e j"), AX.X, ALU.add))
            V.nop().then_inc(s("gmat_ready"), 1)
            dve.wait_ge(s("rank_ps"), 1)
            dve.wait_ge(s("m4_ready"), 1)
            rt_step(V.tensor_copy(rk[:, :, :].rearrange("p t e -> p (t e)"), bank(6)[:, 0:TT * NE]))
            rt_step(V.tensor_reduce(cnt_f[:, :], bank(7)[:, 0:NE], AX.X, ALU.max))
            V.tensor_copy(cnt[:, :], cnt_f[:, :]).then_inc(s("cnt_ready"), 1)
            rt_step(V.scalar_tensor_tensor(out=rm[:, :, :].rearrange("p t e -> p (t e)"),
                                           in0=rk[:, :, :].rearrange("p t e -> p (t e)"), scalar=1.0,
                                           in1=m4[:, :, :].rearrange("p t e -> p (t e)"),
                                           op0=ALU.add, op1=ALU.mult))
            rt_step(V.tensor_scalar(rm[:, :, :], rm[:, :, :], -1.0, None, ALU.add))
            for t in range(TT):
                rt_step(V.tensor_tensor(tmp_hot[:, t], onehot[:, t], wide(rk[:, t, :].unsqueeze(1), [P, TOPK, NE]),
                                        ALU.mult))
            rt_step(V.tensor_reduce(posf[:, :, :].rearrange("p t j -> p (t j)"), th, AX.X, ALU.add))
            rt_step(V.scalar_tensor_tensor(out=rowf[:, :, :], in0=idxf[:, :, :], scalar=float(P), in1=posf[:, :, :],
                                           op0=ALU.mult, op1=ALU.add))
            for r in range(1, ROUNDS):
                rt_step(V.tensor_scalar(later[:, :, :], posf[:, :, :], float(r * P), float((NE - 1) * P),
                                        ALU.is_ge, ALU.mult))
                rt_step(V.tensor_tensor(rowf[:, :, :], rowf[:, :, :], later[:, :, :], ALU.add))
            V.tensor_copy(pos[:, :], rowf[:, :, :].rearrange("p t j -> p (t j)")).then_inc(s("pos_ready"), 1)

            def slot_tokens(r):
                if not isinstance(r, int):
                    V.tensor_scalar(rmr[:, :, :], rm[:, :, :], -float(P), None, ALU.add)\
                        .then_inc(s("rmr_ready"), 1)
                    dve.wait_ge(s("rmr_ready"), 2 * r - 1)
                    V.tensor_copy(rm[:, :, :], rmr[:, :, :]).then_inc(s("rmr_ready"), 1)
                    dve.wait_ge(s("rmr_ready"), 2 * r)
                for t in range(TT):
                    if not (isinstance(r, int) and t < 2):
                        dve.wait_ge(s("tok_ps"), r * TT + t - 1)
                    V.tensor_tensor(hot[t % 2], wide(i_slot[:, :].unsqueeze(1), [P, NE, P]),
                                    wide(rm[:, t, :].unsqueeze(2), [P, NE, P]), ALU.is_equal)\
                        .then_inc(s("hot_ready"), 1)
                dve.wait_ge(s("tok_ps"), r * TT + TT)
                V.tensor_copy(tok_of[:, :], bank(7)[:, 0:NE]).then_inc(s("tok_of_ready"), 1)

            def expert(n, e, first=False):
                dve.wait_ge(s("gu_used"), KD * (n + 1))
                if not first:
                    dve.wait_ge(s("act_ready"), n)
                    dve.wait_ge(s("sgm_ready"), n)
                V.tensor_tensor(glu, ps[:, 0:2, :].rearrange("p b (u d) -> p (b u) d", d=P),
                                wide(guT[:, 0:FT, ds(e, 1)], [P, FT, P]), ALU.add).then_inc(s("gu_read"), 1)
                V.tensor_tensor(lin, ps[:, 2:4, :].rearrange("p b (u d) -> p (b u) d", d=P),
                                wide(guT[:, FT:2 * FT, ds(e, 1)], [P, FT, P]), ALU.add).then_inc(s("gu_read"), 1)
                dve.wait_ge(s("gu_read"), 2 * n + 1)
                V.tensor_scalar(glu, glu, LIMIT, None, ALU.min).then_inc(s("swiglu"), 1)
                dve.wait_ge(s("gu_read"), 2 * n + 2)
                V.tensor_scalar(lin, lin, LIMIT, -LIMIT, ALU.min, ALU.max).then_inc(s("swiglu"), 1)
                dve.wait_ge(s("swiglu"), 3 * n + 1)
                dve.wait_ge(s("swiglu"), 3 * n + 2)
                V.scalar_tensor_tensor(out=lin, in0=lin, scalar=1.0, in1=glu, op0=ALU.add, op1=ALU.mult)\
                    .then_inc(s("swiglu"), 1)
                dve.wait_ge(s("swiglu"), 3 * n + 3)
                dve.wait_ge(s("sgm_ready"), n + 1)
                if not first:
                    dve.wait_ge(s("down_used"), FT // 2 * n)
                V.tensor_tensor(actT, lin, sgm, ALU.mult).then_inc(s("act_ready"), 1)

            def dve_round(r):
                n0 = r * NE
                slot_tokens(r)
                if isinstance(r, int):
                    dve.wait_ge(s("h2T_ready"), TT)
                    dve.wait_ge(s("logits_ps"), 1)
                    dve.wait_ge(s("guT_ready"), 1)
                    expert(0, 0, True)
                    with dve.Fori(1, NE) as e:
                        expert(e, e)
                else:
                    with dve.Fori(0, NE) as e:
                        expert(n0 + e, e)

            dve_round(0)
            more_rounds(dve, dve_round)
            for t in range(TT):
                for half in range(2):
                    cols = slice(half * 512, (half + 1) * 512)
                    dve.wait_ge(s("bd_ps"), 2 * t + half + 1)
                    V.tensor_tensor(xs[:, t, cols], xs[:, t, cols], bank(2 * t + half), ALU.add)\
                        .then_inc(s("bd_added"), 1)
            dve.wait_ge(s("late_params_loaded"), 96)
            for t in range(TT):
                for j in range(TOPK):
                    k = t * TOPK + j
                    dve.wait_ge(s(f"yg_loaded{j}"), 16 * (t + 1))
                    if j:
                        dve.wait_ge(s("y_added"), k)
                    else:
                        dve.wait_ge(s("bd_added"), 2 * t + 2)
                    V.scalar_tensor_tensor(out=xs[:, t, :], in0=yg[j], scalar=gate[:, t, j:j + 1], in1=xs[:, t, :],
                                           op0=ALU.mult, op1=ALU.add).then_inc(s("y_added"), 1)
                dve.wait_ge(s("ms_sum"), 2 * TT + t + 1)
                eps_and_inverse(3 + t, slice(t, t + 1))
                dve.wait_ge(s("ms_inv"), 3 + t)
                if t >= 2:
                    dve.wait_ge(s(f"out_stored{t % 2}"), 16)
                V.scalar_tensor_tensor(out=orow[t % 2], in0=xs[:, t, :], scalar=ms[:, 2, t:t + 1], in1=nwf,
                                       op0=ALU.mult, op1=ALU.mult).then_inc(s("out_ready"), 1)


_INS = ['x', 'norm1_w', 'w_in', 'conv_w', 'a_log_f', 'a_log_b', 'dt_bias_f', 'dt_bias_b', 'gdn_norm_w',
        'w_branch_a', 'w_branch_b', 'w_out', 'norm2_w', 'router_w', 'router_b', 'w_gate_up', 'b_gate_up',
        'w_down', 'b_down', 'norm_f_w']
_OUTS = [((1, 512, 1024), 'float32')]


def kernel(**inputs):
    import numpy as _np
    import concourse.bacc as _bacc
    from concourse import mybir as _mybir
    from concourse.bass_utils import run_bass_kernel_spmd as _run

    nc = _bacc.Bacc("TRN2", target_bir_lowering=False, num_devices=1)
    arrays, args = {}, []
    for name in _INS:
        a = _np.ascontiguousarray(inputs[name])
        arrays[f"in_{name}_dram"] = a
        args.append(nc.dram_tensor(f"in_{name}_dram", a.shape, _mybir.dt.from_np(a.dtype), kind="ExternalInput").ap())
    for i, (shape, dtype) in enumerate(_OUTS):
        dt = _mybir.dt.from_np(_np.dtype(dtype))
        args.append(nc.dram_tensor(f"out_{i}_dram", shape, dt, kind="ExternalOutput").ap())
    build(nc, *args)
    r = _run(nc, [arrays], core_ids=[0])
    return r.results[0]["out_0_dram"]
```

```python
from contextlib import ExitStack
import math

import concourse.bass as bass
from concourse import mybir

F32 = mybir.dt.float32
F32R = mybir.dt.float32r
F16 = mybir.dt.float16
I32 = mybir.dt.int32
U32 = mybir.dt.uint32
ALU = mybir.AluOpType
ACT = mybir.ActivationFunctionType
AX = mybir.AxisListType

P = 128
S = 512
TT = S // P
D = 1024
KD = D // P
AH, ADH = 8, 64
PAIRS = AH // 2
BH, BDH = 8, 128
CK = 5
HALO = CK // 2
NE, TOPK = 32, 4
FF = 1024
FT = FF // P
EPS = 1e-6
MASKED = -1e30
LIMIT, ALPHA = 7.0, 1.702
PATTERNS = ((128, 1), (512, 4), (2048, 16))
SLOPES = [2.0 ** (-8.0 * (h + 1) / AH) for h in range(AH)]
AW, BW = AH * ADH, BH * BDH
COL_QA, COL_KA, COL_VA = 0, AW, 2 * AW
COL_QB = 3 * AW
COL_KB, COL_VB = COL_QB + BW, COL_QB + 2 * BW
COL_Z = COL_QB + 3 * BW
COL_AB = COL_Z + BW
COL_GA = COL_AB + 4 * BH
COL_GB = COL_GA + D
IN_COLS = COL_GB + D
ROUNDS = S // P
FWD, BWD = 0, 1
LEVELS = 6


def build(nc, x, norm1_w, w_in, conv_w, a_log_f, a_log_b, dt_bias_f, dt_bias_b, gdn_norm_w,
          w_branch_a, w_branch_b, w_out, norm2_w, router_w, router_b, w_gate_up, b_gate_up,
          w_down, b_down, norm_f_w, out):
    ds = bass.ds
    x = x[0]
    out = out[0]
    w_in_v = w_in[0].rearrange("(k p) c -> p k c", p=P)
    wa_v = w_branch_a[0].rearrange("(k p) c -> p k c", p=P)
    wb_v = w_branch_b[0].rearrange("(k p) c -> p k c", p=P)
    wo_v = w_out[0].rearrange("(k p) c -> p k c", p=P)
    h2_dram = nc.dram_tensor("h2_rows", [S, D], F32).ap()
    y_dram = nc.dram_tensor("expert_rows", [NE * S, D], F32).ap()

    with ExitStack() as ctx:
        def sb(name, shape, dt=F32):
            return ctx.enter_context(nc.sbuf_tensor(name, shape, dt))

        def sem(name):
            return ctx.enter_context(nc.semaphore(name))

        ps = ctx.enter_context(nc.psum_tensor("ps", [P, 8, 512], F32))

        ARENA_FLOATS = 18432 + 20544 + 4096
        arena_at = -(-nc.sbuf_base // 32) * 32
        arena = sb("arena", [P, ARENA_FLOATS])

        def rounded(name, at, *shape, rows=P):
            return nc.alloc_sbuf_tensor_at(name, [rows, *shape], F32R, offset=arena_at + 4 * at).ap()

        def bank(b):
            return ps[:, b, :]


        def split(v, shape):
            names = "abcd"[:len(shape)]
            dims = dict(zip(names, shape))
            return v.rearrange(f"p ({' '.join(names)}) -> p {' '.join(names)}", **dims)

        class Area:

            def __init__(self, start, floats):
                self.whole, self.floats, self.at = arena[:, start:start + floats], floats, 0

            def take(self, *shape):
                n = math.prod(shape)
                v = self.whole[:, self.at:self.at + n]
                self.at += n
                assert self.at <= self.floats, (self.at, self.floats)
                return split(v, shape)

        def wide(ap, shape):
            return ap.to_broadcast(shape)

        xs = sb("xs", [P, TT, D])

        MIXER_FLOATS = 2 * KD * S + PAIRS * S + 2 * 4 * KD * P
        mixer = Area(0, MIXER_FLOATS)
        hT = mixer.take(KD, S)
        ybT = mixer.take(BH, S)
        yaT = mixer.take(PAIRS, S)
        wcols = [mixer.take(4, KD, P) for _ in range(2)]

        WORK_FLOATS = 20544
        work = Area(MIXER_FLOATS, WORK_FLOATS)
        ahead = Area(MIXER_FLOATS + WORK_FLOATS, 4096)

        ident = sb("ident", [P, P])
        ones = sb("ones", [P, P])
        upper_incl = sb("upper_incl", [P, P])
        upper_strict = sb("upper_strict", [P, P])
        lower_incl = sb("lower_incl", [P, P])
        lower_strict = sb("lower_strict", [P, P])
        vec_rows = sb("vec_rows", [P, P])
        vecT = sb("vecT", [P, P])
        CONVS = CK * 3 * BH
        gnw = sb("gnw", [P, 1])
        wab = sb("wab", [P, KD, 4 * BH])
        gate_c = sb("gate_c", [P, 4, BH])
        ab = sb("ab", [P, 4 * BH, TT])
        soft = sb("soft", [P, 2 * BH, TT])
        gk = sb("gk", [P, 10, BH, TT])
        EG, KDEC, GLAST, BETA, GATE = 0, 2, 4, 6, 8
        ms = sb("ms", [P, 3, TT])

        work.at = 0
        hrow = work.take(2, D)
        junk = work.take(D)

        work.at = 0
        raw = work.take(3, S + 2 * HALO)
        cv = work.take(3, S)
        sg = work.take(3, S)
        qkv = [work.take(3, S) for _ in range(2)]
        sq = work.take(2, S)
        zr = work.take(S)
        sz = [work.take(S) for _ in range(2)]
        k_tok = work.take(TT, P)
        v_r = work.take(TT, P)
        gmask = work.take(2, TT, P)
        decay = work.take(2, TT, P)
        d_strict = work.take(2, TT, P)
        d_incl = work.take(2, TT, P)
        qkd = work.take(2, TT, P)
        pw = work.take(2, TT, P)
        pwT = work.take(2, TT, P)
        tT = work.take(2, TT, P)
        res = work.take(2, P)
        vn = work.take(2, P)
        vs = work.take(2, P)
        state = work.take(2, P)
        o_dir = gmask
        yb = decay[:, 0, :, :]
        yb_sq = decay[:, 1, :, :]
        hs = sb("head_scalars", [P, 10, TT])
        taps = sb("taps", [P, CK, 3])
        c1 = sb("c1", [P, 2, TT])
        nc1 = sb("nc1", [P, 2, TT])
        c2 = sb("c2", [P, 2, TT])
        neg_eg = sb("neg_eg", [P, 2, TT])
        ss = sb("ss", [P, 2, TT])
        rt = sb("rt", [P, 2, TT])
        rq = sb("rq", [P, TT])
        r2 = sb("r2", [P, TT])
        oms = sb("oms", [P, 3, TT])

        DW = S + (TT - 1) * P
        work.at = 0
        dist = work.take(DW)
        lnc = work.take(DW)
        t_i = work.take(DW).bitcast(I32)
        t_j = work.take(DW).bitcast(I32)
        t_a, t_b, t_c = work.take(DW), work.take(DW), work.take(DW)
        bias = [work.take(DW) for _ in range(2)]
        qa = [work.take(S) for _ in range(2)]
        ka = [work.take(S) for _ in range(2)]
        va = [work.take(TT, P) for _ in range(2)]
        sc = [work.take(S) for _ in range(2)]
        pr = [work.take(S) for _ in range(2)]
        pn = [work.take(S) for _ in range(2)]
        prT = [work.take(TT, S)]
        slope = sb("slope", [P, AH])
        nmx = sb("nmx", [P, 2 * TT])
        mx = sb("mx", [P, 2 * TT])
        lsum = sb("lsum", [P, 2 * TT])
        rl = sb("rl", [P, 2 * TT])

        work.at = 0
        mT = work.take(KD, S)
        sig = [work.take(2, S) for _ in range(2)]
        mab = [work.take(2, S) for _ in range(2)]
        wout = work.take(KD, D)

        CHUNK = 2 * FF
        SLOTS = 4
        mixer.at = KD * S
        h2 = mixer.take(2, D)
        nw2 = mixer.take(D)
        hot_f32 = mixer.take(2, NE * P // 2)
        hot = [hot_f32[:, i, :].bitcast(F16).rearrange("p (e s) -> p e s", e=NE) for i in range(2)]
        sgm = mixer.take(D)
        act = mixer.take(D)
        nwf = mixer.take(D)
        bd_rows = mixer.take(D)
        mixer.at = KD * S
        yrow = mixer.take(D)
        mixer.at = KD * S + 2 * D
        glu = mixer.take(D)
        xg = mixer.take(D)
        lin = mixer.take(D)
        bgu_rows = arena[:, 0:2 * FF]
        orow = [h2[:, 0, :], h2[:, 1, :]]
        yg = [hot_f32[:, 0, 0:D], hot_f32[:, 0, D:2 * D], hot_f32[:, 1, 0:D], hot_f32[:, 1, D:2 * D]]
        at_bias = KD * S + 2 * D + D + 4096 + 4 * D
        bias_hl = rounded("bias_hl", at_bias, 2 * FF, rows=2 * NE)
        pick = rounded("pick", at_bias + 2 * FF, P, rows=2 * NE)
        assert at_bias + 2 * FF + P <= MIXER_FLOATS
        xgT = [rounded(f"xgT{i}", 2 * D + i * D, KD, P) for i in range(2)]
        actT = [rounded(f"actT{i}", i * D, FT, P) for i in range(2)]
        w_hl = [[rounded(f"w{b}_{i}", MIXER_FLOATS + (2 * b + i) * CHUNK, CHUNK) for i in range(2)]
                for b in range(SLOTS)]
        ahead.at = 0
        work.at = 2 * SLOTS * CHUNK
        w_raw = [ahead.take(CHUNK), ahead.take(CHUNK), work.take(CHUNK), work.take(CHUNK)]
        rw = sb("rw", [P, KD, NE])
        rb = sb("rb", [P, NE])
        lg = sb("lg", [P, TT, NE])
        mx8 = sb("mx8", [P, TT, 8])
        ix8 = sb("ix8", [P, TT, 8], U32)
        idxf = sb("idxf", [P, TT, TOPK])
        ngt = sb("ngt", [P, TT])
        gsum = sb("gsum", [P, TT])
        gate = sb("gate", [P, TT, TOPK])
        i_slot = sb("i_slot", [P, P])
        e_row = sb("e_row", [2 * NE, P])
        i_slot_i = sb("i_slot_i", [P, P], I32)
        one_v, tmp_v = (a[:, 0:TT * TOPK * NE] for a in (act, sgm))
        onehot, tmp_hot = (v.rearrange("p (t j e) -> p t j e", t=TT, j=TOPK) for v in (one_v, tmp_v))
        m4 = sb("m4", [P, TT, NE])
        gmat = sb("gmat", [P, TT, NE])
        gmatT = sb("gmatT", [P, TT, P])
        rk = sb("rk", [P, TT, NE])
        rm = sb("rm", [P, TT, NE])
        rmr = sb("rmr", [P, TT, NE])
        posf = sb("posf", [P, TT, TOPK])
        rowf = sb("rowf", [P, TT, TOPK])
        later = sb("later", [P, TT, TOPK])
        pos = sb("pos", [P, TT * TOPK], I32)
        cnt_f = sb("cnt_f", [P, 1])
        cnt = sb("cnt", [P, 1], I32)
        tokid_i = sb("tokid_i", [P, TT], I32)
        tokid = sb("tokid", [P, TT], F16)
        tok_of = sb("tok_of", [P, NE], I32)
        idx_col = sb("idx_col", [P, 1], I32)
        waited = sb("waited", [P, 2])

        sems = {}

        def s(name):
            if name not in sems:
                sems[name] = sem(name)
            return sems[name]

        block = ctx.enter_context(nc.Block())

        def tiles_of(b):
            return bank(b).rearrange("p (t d) -> p t d", t=TT)

        def heads(eng, step):
            last = BH // 2 - 1
            with eng.Fori(0, last) as i:
                step(2 * i, i, 0, True)
                step(2 * i + 1, i, 1, True)
            step(BH - 2, last, 0, True)
            step(BH - 1, last, 1, False)

        def pairs(eng, step):
            for p in range(PAIRS):
                step(p, p // 2, p % 2, p < PAIRS - 1)

        def mixer_over(eng):
            eng.wait_ge(s("x1_added"), 2 * TT)

        def deltanet_over(eng):
            eng.wait_ge(s("ybT_ready"), BH)
            eng.wait_ge(s("silu_z"), BH)

        def attention_over(eng):
            eng.wait_ge(s("yaT_ready"), 2 * PAIRS)


        def head_cols(i):
            return 64 * (i + 1)

        def pair_cols(i):
            return head_cols(BH // 2 - 1) + 48 * (i + 1)

        def merge_cols(i):
            return pair_cols(PAIRS // 2 - 1) + 64 * (i + 1)

        def more_rounds(eng, one_round):
            eng.wait_ge(s("cnt_ready"), 1)
            largest = eng.value_load(cnt[0:1, 0:1], min_val=0, max_val=S)
            with eng.If(largest > P):
                with eng.Fori(1, ROUNDS) as r:
                    with eng.If(largest > r * P):
                        one_round(r)
                        eng.nop()
                    with eng.Else():
                        eng.nop()
                eng.nop()
            with eng.Else():
                eng.nop()

        def chunk_no(n, j, first=False):
            return 3 * n + j // SLOTS if first else 3 * n - 1 + j // SLOTS

        def down_no(n, c, alone):
            return chunk_no(n, c if alone else KD + c)

        gu_v = w_gate_up[0].rearrange("e (k p) c -> e k p c", p=P)
        dn_v = w_down[0].rearrange("e (c f p) d -> e c p f d", f=2, p=P)

        @block.sync
        def _(sp):
            for t in range(TT):
                sp.dma_start(xs[:, t, :], x[t * P:(t + 1) * P, :]).then_inc(s("x_loaded"), 16)
            sp.dma_start(vec_rows[0:CONVS, :], conv_w[0].rearrange("k (c p) -> (k c) p", p=P))\
                .then_inc(s("params_loaded"), 16)
            sp.dma_start(vec_rows[CONVS:P, :], norm1_w[0].rearrange("(k p) -> k p", p=P))\
                .then_inc(s("params_loaded"), 16)
            sp.dma_start(wab[:, :, :], w_in_v[:, :, COL_AB:COL_AB + 4 * BH]).then_inc(s("params_loaded"), 16)
            for i, v in enumerate((dt_bias_f, dt_bias_b, a_log_f, a_log_b)):
                sp.dma_start(gate_c[:, i, :], v[0].partition_broadcast(P)).then_inc(s("params_loaded"), 16)
            sp.dma_start(gnw[:, :], gdn_norm_w[0].rearrange("(p a) -> p a", a=1)).then_inc(s("params_loaded"), 16)

            def load_cols(b, parts):
                for i, (view, tiles, col) in enumerate(parts):
                    sp.dma_start(wcols[b][:, i, 0:tiles, :], view[:, :, ds(col, P)])\
                        .then_inc(s(f"wcols_loaded{b}"), 16)

            def load_head(h, b):
                load_cols(b, [(w_in_v, KD, c + h * P) for c in (COL_QB, COL_KB, COL_VB, COL_Z)])

            def load_pair(p, b):
                load_cols(b, [(w_in_v, KD, c + p * P) for c in (COL_QA, COL_KA, COL_VA)])

            def load_merge(n, b):
                load_cols(b, [(w_in_v, KD, COL_GA + n * P), (w_in_v, KD, COL_GB + n * P),
                              (wa_v, PAIRS, n * P), (wb_v, KD, n * P)])

            load_head(0, 0)
            load_head(1, 1)
            with sp.Fori(0, BH // 2 - 1) as i:
                for b in range(2):
                    sp.wait_ge(s("proj_z"), 2 * i + b + 1)
                    load_head(2 * i + b + 2, b)
            for p in range(PAIRS):
                if p < 2:
                    sp.wait_ge(s("proj_z"), BH - 1 + p)
                else:
                    sp.wait_ge(s("proj_va"), p - 1)
                load_pair(p, p % 2)
            for n in range(2):
                sp.wait_ge(s("proj_va"), PAIRS - 1 + n)
                load_merge(n, n)
            attention_over(sp)
            sp.dma_start(wout, wo_v).then_inc(s("wout_loaded"), 16)
            with sp.Fori(0, KD // 2 - 1) as i:
                for b in range(2):
                    sp.wait_ge(s("merge_ps"), 2 * i + b + 1)
                    load_merge(2 * i + b + 2, b)
            mixer_over(sp)
            sp.dma_start(nw2, norm2_w[0].partition_broadcast(P)).then_inc(s("late_params_loaded"), 16)
            sp.dma_start(rw[:, :, :], router_w[0].rearrange("(k p) e -> p k e", p=P)).then_inc(s("late_params_loaded"), 16)
            sp.dma_start(rb[:, :], router_b[0].partition_broadcast(P)).then_inc(s("late_params_loaded"), 16)
            sp.dma_start(bd_rows[0:NE, :], b_down[0]).then_inc(s("late_params_loaded"), 16)
            sp.dma_start(nwf, norm_f_w.partition_broadcast(P)).then_inc(s("late_params_loaded"), 16)

            def load(b, a, src, two=False):
                if not (isinstance(a, int) and a == 0):
                    sp.wait_ge(s(f"lo_ready{b}"), a)
                dst = w_raw[b].rearrange("p (f d) -> p f d", f=2) if two else w_raw[b]
                sp.dma_start(dst, src).then_inc(s(f"raw_loaded{b}"), 16)

            def load_gate_up(n, e, first=False):
                for j in range(KD):
                    load(j % SLOTS, chunk_no(n, j, first), gu_v[ds(e, 1), j])

            def load_down(n, e, alone=False):
                for c in range(FT // 2):
                    load(c, down_no(n, c, alone), dn_v[ds(e, 1), c], two=True)

            for j in range(2):
                load(j, 0, gu_v[0:1, j])
            for t in range(TT):
                sp.wait_ge(s("h2_ready"), t + 1)
                sp.dma_start(h2_dram[t * P:(t + 1) * P, :], h2[:, t % 2, :]).then_inc(s(f"h2_stored{t % 2}"), 16)
            for j in range(2, KD):
                load(j % SLOTS, j // SLOTS, gu_v[0:1, j])
                if j == 3:
                    sp.wait_ge(s("logits_ps"), 1)
                    sp.dma_start(bgu_rows[0:NE, :], b_gate_up[0]).then_inc(s("bias_loaded"), 16)

            def sp_rest(n0):
                with sp.Fori(1, NE) as e:
                    load_gate_up(n0 + e, e)
                    load_down(n0 + e, e - 1)
                load_down(n0 + NE, NE - 1, alone=True)

            sp_rest(0)

            def sp_round(r):
                load_gate_up(r * NE, 0, True)
                sp_rest(r * NE)

            more_rounds(sp, sp_round)
            for t in range(TT):
                sp.wait_ge(s("out_ready"), t + 1)
                sp.dma_start(out[t * P:(t + 1) * P, :], orow[t % 2]).then_inc(s(f"out_stored{t % 2}"), 16)
            for b in range(2):
                sp.wait_ge(s(f"out_stored{b}"), 16 * TT // 2)

        @block.gpsimd
        def _(pool):
            pool.memset(ones[:, :], 1.0).then_inc(s("pool_setup"), 1)
            pool.wait_ge(s("pool_setup"), 1)
            for m, base, per_col, per_row in ((upper_incl, 0, 1, -1), (upper_strict, -1, 1, -1),
                                              (lower_incl, 0, -1, 1), (lower_strict, -1, -1, 1)):
                pool.affine_select(out=m[:, :], in_=ones[:, :], pattern=[[per_col, P]], base=base,
                                   channel_multiplier=per_row, compare_op=ALU.is_ge, fill=0.0)\
                    .then_inc(s("pool_setup"), 1)
            pool.wait_ge(s("pool_setup"), 5)
            pool.tensor_tensor(ident[:, :], upper_incl[:, :], upper_strict[:, :], ALU.subtract)\
                .then_inc(s("pool_setup"), 1)
            pool.iota(i_slot_i[:, :], [[1, P]], base=0, channel_multiplier=0).then_inc(s("pool_setup"), 1)
            pool.iota(tokid_i[:, :], [[P, TT]], base=0, channel_multiplier=1).then_inc(s("pool_setup"), 1)
            pool.wait_ge(s("pool_setup"), 8)
            pool.tensor_copy(i_slot[:, :], i_slot_i[:, :]).then_inc(s("pool_setup"), 1)
            pool.tensor_copy(tokid[:, :], tokid_i[:, :]).then_inc(s("pool_setup"), 1)
            for half in range(2):
                if half:
                    pool.wait_ge(s("pool_setup"), 10)
                    pool.wait_ge(s("e_row_ready"), 1)
                pool.tensor_copy(e_row[half * NE:(half + 1) * NE, :], wide(tokid_i[0:NE, 0:1], [NE, P]))\
                    .then_inc(s("e_row_ready"), 1)
            pool.wait_ge(s("e_row_ready"), 2)
            for h in range(AH):
                pool.memset(slope[:, h:h + 1], -SLOPES[h]).then_inc(s("pool_setup"), 1)

            def head(h, i, b, nxt):
                pool.wait_ge(s("hs_ready"), h + 1)
                for d, m in ((FWD, upper_incl), (BWD, lower_incl)):
                    pool.tensor_tensor(gmask[:, d], wide(m[:, :].unsqueeze(1), [P, TT, P]),
                                       wide(hs[:, GATE + d, :].unsqueeze(2), [P, TT, P]), ALU.mult)\
                        .then_inc(s("gmask_ready"), 1)
                for d, strict, incl in ((FWD, upper_strict, upper_incl), (BWD, lower_strict, lower_incl)):
                    pool.wait_ge(s("decay_ready"), 2 * h + d + 1)
                    pool.tensor_tensor(d_strict[:, d], decay[:, d], wide(strict[:, :].unsqueeze(1), [P, TT, P]),
                                       ALU.mult).then_inc(s("masked"), 1)
                    pool.tensor_tensor(d_incl[:, d], decay[:, d], wide(incl[:, :].unsqueeze(1), [P, TT, P]),
                                       ALU.mult).then_inc(s("masked"), 1)

            pool.wait_ge(s("hT_ready"), TT)
            pool.memset(raw[:, :, 0:HALO], 0.0).then_inc(s("pool_setup"), 1)
            pool.memset(raw[:, :, HALO + S:], 0.0).then_inc(s("pool_setup"), 1)
            heads(pool, head)

            deltanet_over(pool)
            pool.iota(t_i, [[1, DW]], base=-(TT - 1) * P, channel_multiplier=-1).then_inc(s("pool_setup"), 1)
            pool.iota(t_j, [[1, DW]], base=P, channel_multiplier=-1).then_inc(s("pool_setup"), 1)

            def take_wait(i=0):
                pool.tensor_tensor(waited[:, i:i + 1], ones[:, 0:1], ones[:, 0:1], ALU.mult)

            def gathers(n, e):
                if not (isinstance(n, int) and n == 0):
                    pool.wait_ge(s("xgT_ps"), n)
                    pool.wait_ge(s("xg_loaded"), 16 * n)
                    take_wait()
                pool.tensor_copy(idx_col[:, :], tok_of[:, ds(e, 1)]).then_inc(s("idx_ready"), 1)
                pool.wait_ge(s("idx_ready"), n + 1)
                take_wait(1)
                pool.indirect_dma_start(xg, None, h2_dram, bass.IndirectOffsetOnAxis(ap=idx_col[:, 0:1], axis=0))\
                    .then_inc(s("xg_loaded"), 16)

            def split_lo(j, a):
                pool.wait_ge(s("hi_ready1"), a + 1)
                pool.tensor_tensor(w_hl[1][1], w_raw[1], w_hl[1][0].bitcast(F32), ALU.subtract)\
                    .then_inc(s("lo_ready1"), 1)

            def pool_round(r):
                n0 = r * NE
                pool.wait_ge(s("tok_of_ready"), r + 1)
                take_wait()
                gathers(n0, 0)
                split_lo(1, chunk_no(n0, 1, True))
                gathers(n0 + 1, 1)
                split_lo(5, chunk_no(n0, 5, True))
                with pool.Fori(1, NE - 1) as e:
                    split_lo(1, chunk_no(n0 + e, 1))
                    gathers(n0 + e + 1, e + 1)
                    for j in (5, 9):
                        split_lo(j, chunk_no(n0 + e, j))
                for j in (1, 5, 9):
                    split_lo(j, chunk_no(n0 + NE - 1, j))
                split_lo(1, down_no(n0 + NE, 1, alone=True))
                pool.wait_ge(s("y_stored"), (r * NE + NE) * 16)

            for b in range(2):
                pool.wait_ge(s(f"h2_stored{b}"), 16 * TT // 2)
            pool_round(0)
            more_rounds(pool, pool_round)

            def results(rounds):
                for t in range(TT):
                    for j in range(TOPK):
                        k = t * TOPK + j
                        if t:
                            pool.wait_ge(s("y_added"), k - TOPK + 1)
                        pool.indirect_dma_start(yg[j], None, y_dram[0:rounds * NE * P, :],
                                                bass.IndirectOffsetOnAxis(ap=pos[:, k:k + 1], axis=0))\
                            .then_inc(s(f"yg_loaded{j}"), 16)

            def results_of(rounds, largest):
                if rounds == ROUNDS:
                    results(rounds)
                    return
                with pool.If(largest > rounds * P):
                    results_of(rounds + 1, largest)
                    pool.nop()
                with pool.Else():
                    results(rounds)

            pool.wait_ge(s("pos_ready"), 1)
            results_of(1, pool.value_load(cnt[0:1, 0:1], min_val=0, max_val=S))

        @block.tensor
        def _(pe):
            def mm(o, lhsT, rhs, start=True, stop=True, **kw):
                return nc.tensor.matmul(o, lhsT, rhs, start=start, stop=stop, **kw)

            pe.wait_ge(s("pool_setup"), 6)
            pe.wait_ge(s("params_loaded"), 128)
            nc.tensor.transpose(bank(6)[:, 0:P], vec_rows[:, :], ident[:, :]).then_inc(s("vecT_ps"), 1)

            def to_features(t, source, ready, free, name):
                pe.wait_ge(s(ready), t + 1)
                if t >= 2:
                    pe.wait_ge(s(free), t - 1)
                two = ps[:, 2 * (t % 2):2 * (t % 2) + 2, :].rearrange("p b (u d) -> p (b u) d", d=P)
                for k in range(KD):
                    last = nc.tensor.transpose(two[:, k, :], source[:, t % 2, k * P:(k + 1) * P], ident[:, :])
                last.then_inc(s(name), 1)

            for t in range(TT):
                to_features(t, hrow, "hrow_ready", "hT_ready", "hT_ps")

            pe.wait_ge(s("params_loaded"), 128)
            pe.wait_ge(s("hT_ready"), TT)
            for t in range(TT):
                for k in range(KD):
                    last = mm(bank(4)[:, t * 4 * BH:(t + 1) * 4 * BH], hT[:, k, t * P:(t + 1) * P],
                              wab[:, k, :], k == 0, k == KD - 1)
            last.then_inc(s("ab_ps"), 1)
            pe.wait_ge(s("gates_dve"), 10)
            W = BH * TT
            for j, (m, d) in enumerate(((upper_incl, FWD), (lower_incl, BWD), (lower_strict, FWD),
                                        (upper_strict, BWD), (ones, FWD), (ones, BWD))):
                last = mm(bank(5)[:, j * W:(j + 1) * W], m[:, :],
                          gk[:, GATE + d].rearrange("p h t -> p (h t)"))
            last.then_inc(s("cum_ps"), 1)

            def proj_qkv(h, i, b, part):
                if part == 0:
                    pe.wait_ge(s(f"wcols_loaded{b}"), head_cols(i))
                if not (isinstance(h, int) and h == 0 and part < 2):
                    if part == 0:
                        pe.wait_ge(s("raw_ready"), 3 * h)
                    elif part == 1:
                        pe.wait_ge(s("z_raw"), h)
                        pe.wait_ge(s("scalars_ready"), 9 * (h - 1) + 1)
                    else:
                        pe.wait_ge(s("raw_ready"), 3 * h + 1)
                for k in range(KD):
                    last = mm(bank(part % 2), wcols[b][:, part, k, :], hT[:, k, :], k == 0, k == KD - 1)
                last.then_inc(s("proj_qkv"), 1)

            def proj_z(h, b):
                pe.wait_ge(s("raw_ready"), 3 * h + 2)
                for t in range(TT):
                    for k in range(KD):
                        last = mm(tiles_of(1)[:, t, :], hT[:, k, t * P:(t + 1) * P], wcols[b][:, 3, k, :],
                                  k == 0, k == KD - 1)
                last.then_inc(s("proj_z"), 1)

            kq = ps[:, 4:6, :].rearrange("p b (u w i) -> p (b u) w i", u=2, w=2)

            def head(h, i, b, nxt):
                hn, bn = h + 1, 1 - b
                i_n = i + b
                q, k, v = qkv[b][:, 0, :], qkv[b][:, 1, :], qkv[b][:, 2, :]

                def tile(a, t):
                    return a[:, t * P:(t + 1) * P]

                pe.wait_ge(s("sq_ready"), h + 1)
                pe.wait_ge(s("z_raw"), h + 1)
                for w in range(2):
                    for t in range(TT):
                        last = mm(bank(1)[:, w * TT + t:w * TT + t + 1], tile(sq[:, w, :], t), ones[:, 0:1])
                last.then_inc(s("ss_ps"), 1)
                for d, m in ((FWD, lower_strict), (BWD, upper_strict)):
                    pe.wait_ge(s("gmask_ready"), 2 * h + d + 1)
                    mm(bank(6 + d), m[:, :], gmask[:, d].rearrange("p t i -> p (t i)")).then_inc(s("decay_ps"), 1)
                for t in range(TT):
                    nc.tensor.transpose(tiles_of(2)[:, t, :], tile(k, t), ident[:, :])
                for t in range(TT):
                    last = nc.tensor.transpose(tiles_of(3)[:, t, :], tile(v, t), ident[:, :])
                last.then_inc(s("kv_tok_ps"), 1)
                qk = qkv[b][:, 0:2, :].rearrange("p w (t i) -> p w t i", t=TT)
                for t in range(TT):
                    last = mm(kq[:, t], tile(k, t), qk[:, :, t, :])
                last.then_inc(s("kq_ps"), 1)
                if nxt:
                    proj_qkv(hn, i_n, bn, 0)

                for d in (FWD, BWD):
                    pe.wait_ge(s("pT_made"), 2 * h + d + 1)
                    if d == FWD:
                        pe.wait_ge(s("k_tok_ready"), h + 1)
                    else:
                        pe.wait_ge(s("scalars_ready"), 9 * h + 7)
                    for t in range(TT):
                        last = nc.tensor.transpose(tiles_of(2 + d)[:, t, :], pwT[:, d, t, :], ident[:, :])
                    last.then_inc(s(f"pw_ps{d}"), 1)

                def squares(d, n):
                    pe.wait_ge(s(f"pw_ready{d}"), h * (LEVELS + 1) + n)
                    if n > 1:
                        pe.wait_ge(s(f"pwT_ready{d}"), h * (LEVELS - 1) + n - 1)
                    for t in range(TT):
                        last = mm(tiles_of(2 + d)[:, t, :], pwT[:, d, t, :], pw[:, d, t, :])
                    last.then_inc(s(f"pw_ps{d}"), 1)
                    if n < LEVELS:
                        if n == 1:
                            pe.wait_ge(s("qkd_ready"), 2 * h + 2)
                        for t in range(TT):
                            last = mm(tiles_of(4 + d)[:, t, :], pw[:, d, t, :], pwT[:, d, t, :])
                        last.then_inc(s(f"pwT_ps{d}"), 1)

                def grow(d, n):
                    pe.wait_ge(s(f"pw_ready{d}"), h * (LEVELS + 1) + n + 1)
                    pe.wait_ge(s(f"tT_ready{d}"), h * (LEVELS + 1) + n)
                    for t in range(TT):
                        last = mm(tiles_of(6 + d)[:, t, :], pw[:, d, t, :], tT[:, d, t, :])
                    last.then_inc(s(f"tT_ps{d}"), 1)

                for d in (FWD, BWD):
                    squares(d, 1)
                for n in range(1, LEVELS + 1):
                    if n == 3 and nxt:
                        proj_qkv(hn, i_n, bn, 1)
                    for d in (FWD, BWD):
                        grow(d, n)
                        if n < LEVELS:
                            squares(d, n + 1)

                def scan(step):
                    for d in (FWD, BWD):
                        t = step if d == FWD else TT - 1 - step
                        bk = bank(2 + d)
                        if step:
                            pe.wait_ge(s("state_ready"), 2 * ((TT - 1) * h + step - 1) + d + 1)
                            mm(bk[:, 0:P], tile(k, t), state[:, d, :])
                            if step > 1:
                                pe.wait_ge(s("qs_ready"), 2 * ((TT - 1) * h + step - 2) + d + 1)
                            mm(bank(6 + d)[:, 0:P], tile(q, t), state[:, d, :]).then_inc(s("ks_ps"), 1)
                    for d in (FWD, BWD):
                        t = step if d == FWD else TT - 1 - step
                        if step:
                            pe.wait_ge(s("res_ready"), 2 * ((TT - 1) * h + step - 1) + d + 1)
                        else:
                            pe.wait_ge(s(f"tT_ready{d}"), (h + 1) * (LEVELS + 1))
                            pe.wait_ge(s(f"pw_ready{d}"), (h + 1) * (LEVELS + 1))
                        mm(bank(2 + d)[:, 2 * P:3 * P], tT[:, d, t, :], res[:, d, :] if step else v_r[:, t, :])\
                            .then_inc(s("y_ps"), 1)
                    for d in (FWD, BWD):
                        t = step if d == FWD else TT - 1 - step
                        pe.wait_ge(s("vn_ready"), 2 * (TT * h + step) + d + 1)
                        last = mm(bank(4 + d)[:, 0:P], qkd[:, d, t, :], vn[:, d, :])
                        if step < TT - 1:
                            pe.wait_ge(s("vs_ready"), 2 * ((TT - 1) * h + step) + d + 1)
                            last = mm(bank(4 + d)[:, P:2 * P], k_tok[:, t, :], vs[:, d, :])
                        last.then_inc(s("os_ps"), 1)

                scan(0)
                scan(1)
                if nxt:
                    proj_qkv(hn, i_n, bn, 2)
                scan(2)
                scan(3)
                if nxt:
                    proj_z(hn, bn)
                pe.wait_ge(s("tail"), 8 * h + 8)
                for t in range(TT):
                    last = nc.tensor.transpose(tiles_of(6)[:, t, :], yb[:, t, :], ident[:, :])
                last.then_inc(s("ybT_ps"), 1)

            proj_qkv(0, 0, 0, 0)
            proj_qkv(0, 0, 0, 1)
            proj_qkv(0, 0, 0, 2)
            proj_z(0, 0)
            heads(pe, head)

            def proj_pair(p, i, b):
                pe.wait_ge(s(f"wcols_loaded{b}"), pair_cols(i))
                for part in range(2):
                    if p:
                        pe.wait_ge(s("qkva_ready"), 3 * p - (2 if part == 0 else 1))
                        if part == 0:
                            pe.wait_ge(s("qkva_ready"), 3 * p)
                    else:
                        pe.wait_ge(s("z_raw"), BH)
                    for k in range(KD):
                        last = mm(bank(part), wcols[b][:, part, k, :], hT[:, k, :], k == 0, k == KD - 1)
                    last.then_inc(s("proj_qka"), 1)
                pe.wait_ge(s("qkva_ready"), 3 * p + 1)
                for t in range(TT):
                    for k in range(KD):
                        last = mm(tiles_of(0)[:, t, :], hT[:, k, t * P:(t + 1) * P], wcols[b][:, 2, k, :],
                                  k == 0, k == KD - 1)
                last.then_inc(s("proj_va"), 1)

            deltanet_over(pe)
            proj_pair(0, 0, 0)
            U = 2 * TT

            def scores(p, b, u):
                hh, t = divmod(u, TT)
                n = U * p + u
                rows = slice(ADH * hh, ADH * hh + ADH)
                if n >= 2:
                    pe.wait_ge(s("sc_ready"), n - 1)
                mm(bank(2 + u % 2), qa[b][rows, t * P:(t + 1) * P], ka[b][rows, :]).then_inc(s("sc_ps"), 1)

            def pair(p, i, b, nxt):
                pe.wait_ge(s("qkva_ready"), 3 * p + 3)
                scores(p, b, 0)
                scores(p, b, 1)
                for u in range(U):
                    hh, t = divmod(u, TT)
                    n = U * p + u
                    pe.wait_ge(s("pn_ready"), n + 1)
                    if n >= 2:
                        pe.wait_ge(s("prT_ready"), n - 1)
                    for j in range(TT):
                        last = nc.tensor.transpose(tiles_of(4 + u % 2)[:, j, :], pn[u % 2][:, j * P:(j + 1) * P],
                                                   ident[:, :])
                    last.then_inc(s("prT_ps"), 1)
                    if u + 2 < U:
                        scores(p, b, u + 2)
                    if u == 5 and nxt:
                        proj_pair(p + 1, i + b, 1 - b)
                    if t == TT - 1:
                        pe.wait_ge(s("prT_ready"), n + 1)
                        if 2 * p + hh >= 2:
                            pe.wait_ge(s("yaT_ready"), 2 * p + hh - 1)
                        for j in range(TT):
                            last = mm(ps[ADH * hh:ADH * hh + ADH, 6 + hh, :], va[b][:, j, ADH * hh:ADH * hh + ADH],
                                      prT[0][:, j, :], j == 0, j == TT - 1)
                        last.then_inc(s("pv_ps"), 1)

            pairs(pe, pair)

            attention_over(pe)

            def merge(n, i, b):
                pe.wait_ge(s(f"wcols_loaded{b}"), merge_cols(i))
                if not (isinstance(i, int) and i == 0):
                    pe.wait_ge(s("mT_ready"), n - 1)
                for j, (tiles, rhs) in enumerate(((KD, hT), (KD, hT), (PAIRS, yaT), (KD, ybT))):
                    for k in range(tiles):
                        last = mm(bank(4 * b + j), wcols[b][:, j, k, :], rhs[:, k, :], k == 0, k == tiles - 1)
                last.then_inc(s("merge_ps"), 1)

            merge(0, 0, 0)
            merge(1, 0, 1)
            with pe.Fori(1, KD // 2) as i:
                merge(2 * i, i, 0)
                merge(2 * i + 1, i, 1)
            pe.wait_ge(s("mT_ready"), KD)
            pe.wait_ge(s("wout_loaded"), 16)
            for t in range(TT):
                for half in range(2):
                    for k in range(KD):
                        last = mm(bank(2 * t + half), mT[:, k, t * P:(t + 1) * P],
                                  wout[:, k, half * 512:(half + 1) * 512], k == 0, k == KD - 1)
                    last.then_inc(s("x1_ps"), 1)
            pe.wait_ge(s("x1_added"), 2 * TT)
            for t in range(TT):
                to_features(t, h2, "h2_ready", "h2T_ready", "h2T_ps")
            pe.wait_ge(s("h2T_ready"), TT)
            pe.wait_ge(s("late_params_loaded"), 80)
            for t in range(TT):
                for k in range(KD):
                    last = mm(bank(4)[:, t * NE:(t + 1) * NE], hT[:, k, t * P:(t + 1) * P], rw[:, k, :],
                              k == 0, k == KD - 1)
            last.then_inc(s("logits_ps"), 1)
            pe.wait_ge(s("m4_ready"), 1)
            for t in range(TT):
                for u in range(t + 1):
                    last = mm(bank(6)[:, t * NE:(t + 1) * NE], (upper_strict if u == t else ones)[:, :],
                              m4[:, u, :], u == 0, u == t)
            for t in range(TT):
                last = mm(bank(7)[:, 0:NE], ones[:, :], m4[:, t, :], t == 0, t == TT - 1)
            last.then_inc(s("rank_ps"), 1)
            pe.wait_ge(s("gmat_ready"), 1)
            for t in range(TT):
                last = nc.tensor.transpose(ps[0:NE, 4, t * P:(t + 1) * P], gmat[:, t, :], ident[:, :])
            last.then_inc(s("gmatT_ps"), 1)

            def slot_tokens(r):
                for t in range(TT):
                    pe.wait_ge(s("hot_ready"), r * TT + t + 1)
                    for e in range(NE):
                        last = mm(bank(7)[:, e:e + 1], hot[t % 2][:, e, :], tokid[:, t:t + 1],
                                  t == 0 and e == 0, t == TT - 1, skip_group_check=True)
                    last.then_inc(s("tok_ps"), 1)

            def xg_to_features(n):
                pe.wait_ge(s("xg_loaded"), 16 * n + 16)
                if not (isinstance(n, int) and n < 2):
                    pe.wait_ge(s("actT_ready"), 2 * (n - 1))
                for k in range(KD):
                    last = nc.tensor.transpose(ps[:, 4 + k // 4, (k % 4) * P:(k % 4 + 1) * P],
                                               xg[:, k * P:(k + 1) * P], ident[:, :])
                last.then_inc(s("xgT_ps"), 1)

            def products(o, x_hl, w, first, last):
                for xi, wi in ((0, 0), (0, 1), (1, 0)):
                    for i, b in enumerate(o):
                        m = mm(bank(b), x_hl[xi], w[wi][:, i * 512:(i + 1) * 512],
                               first and xi == wi == 0, last and xi == 1)
                return m

            def gate_up(n, half, first=False):
                if half == 0:
                    pe.wait_ge(s("xgT_ready"), 2 * n + 2)
                    pe.wait_ge(s("pick_ready"), n + 1)
                    if not (isinstance(n, int) and n == 0):
                        pe.wait_ge(s("swiglu"), 4 * n - 2)
                    for b in range(4):
                        mm(bank(b), pick, bias_hl[:, b * 512:(b + 1) * 512], True, False)
                for j in range(4 * half, 4 * half + 4):
                    pe.wait_ge(s(f"lo_ready{j % SLOTS}"), chunk_no(n, j, first) + 1)
                    products(range(4), [x[:, j, :] for x in xgT], w_hl[j % SLOTS], False, j == KD - 1)\
                        .then_inc(s(f"split_used{j % SLOTS}"), 1)

            def act_to_features(n):
                pe.wait_ge(s("swiglu"), 4 * n + 4)
                pe.wait_ge(s("xgT_ready"), 2 * n + 2)
                for k in range(FT):
                    last = nc.tensor.transpose(ps[:, 4 + k // 4, (k % 4) * P:(k % 4 + 1) * P],
                                               act[:, k * P:(k + 1) * P], ident[:, :])
                last.then_inc(s("actT_ps"), 1)

            def down(n, alone=False):
                pe.wait_ge(s("actT_ready"), 2 * n)
                if not (isinstance(n, int) and n == 1):
                    pe.wait_ge(s("y_read"), n - 1)
                for c in range(FT // 2):
                    pe.wait_ge(s(f"lo_ready{c}"), down_no(n, c, alone) + 1)
                    for f in (2 * c, 2 * c + 1):
                        m = products((6, 7), [a[:, f, :] for a in actT],
                                     [w[:, f % 2 * D:(f % 2 + 1) * D] for w in w_hl[c]], f == 0, f == FT - 1)
                    m.then_inc(s(f"split_used{c}"), 1)

            def pe_round(r):
                n0 = r * NE
                slot_tokens(r)
                pe.wait_ge(s("tok_of_ready"), r + 1)
                if isinstance(r, int):
                    pe.wait_ge(s("gmatT_ready"), 1)
                xg_to_features(n0)
                gate_up(n0, 0, True)
                gate_up(n0, 1, True)
                xg_to_features(n0 + 1)

                def step(n, more):
                    gate_up(n, 0)
                    act_to_features(n - 1)
                    gate_up(n, 1)
                    if more:
                        xg_to_features(n + 1)
                    down(n)

                step(n0 + 1, True)
                with pe.Fori(2, NE - 1) as e:
                    step(n0 + e, True)
                step(n0 + NE - 1, False)
                act_to_features(n0 + NE - 1)
                down(n0 + NE, alone=True)

            pe_round(0)
            more_rounds(pe, pe_round)
            pe.wait_ge(s("y_all_read"), 1)
            for t in range(TT):
                for half in range(2):
                    mm(bank(2 * t + half), gmatT[0:NE, t, :], bd_rows[0:NE, half * 512:(half + 1) * 512])\
                        .then_inc(s("bd_ps"), 1)

        @block.scalar
        def _(se):
            A = nc.scalar.activation

            se.wait_ge(s("x_loaded"), 16 * TT)
            for t in range(TT):
                if t:
                    se.wait_ge(s("ms_sum"), t)
                A(junk, xs[:, t, :], ACT.Square, accum_out=ms[:, 0, t:t + 1]).then_inc(s("ms_sum"), 1)
            se.wait_ge(s("ms_eps"), 1)
            A(ms[:, 1, :], ms[:, 0, :], ACT.Sqrt).then_inc(s("ms_root"), 1)
            se.wait_ge(s("ms_inv"), 1)
            for t in range(TT):
                if t >= 2:
                    se.wait_ge(s("hT_ps"), t - 1)
                A(hrow[:, t % 2, :], xs[:, t, :], ACT.Copy, scale=ms[:, 2, t:t + 1]).then_inc(s("hrow_ready"), 1)

            se.wait_ge(s("gates_dve"), 4)
            se.wait_ge(s("params_loaded"), 128)
            A(soft[:, :, :], soft[:, :, :], ACT.Exp, scale=-1.0).then_inc(s("gates_act"), 1)
            A(gate_c[:, 2:4, :], gate_c[:, 2:4, :], ACT.Exp).then_inc(s("gates_act"), 1)
            A(ab[:, 2 * BH:4 * BH, :], ab[:, 2 * BH:4 * BH, :], ACT.Exp, scale=-1.0).then_inc(s("gates_act"), 1)
            se.wait_ge(s("gates_dve"), 5)
            A(soft[:, :, :], soft[:, :, :], ACT.Ln).then_inc(s("gates_act"), 1)
            se.wait_ge(s("cum_ps"), 1)
            A(gk[:, 0:GLAST + 2].rearrange("p k h t -> p (k h t)"), bank(5)[:, 0:6 * BH * TT], ACT.Exp)\
                .then_inc(s("gates_act"), 1)

            def evac_raw(h, part):
                se.wait_ge(s("proj_qkv"), 3 * h + part + 1)
                if not (isinstance(h, int) and h == 0):
                    se.wait_ge(s("tap"), CK * (3 * (h - 1) + part + 1))
                elif part == 0:
                    se.wait_ge(s("pool_setup"), 20)
                A(raw[:, part, HALO:HALO + S], bank(part % 2), ACT.Copy).then_inc(s("raw_ready"), 1)

            def evac_z(h):
                se.wait_ge(s("proj_z"), h + 1)
                if not (isinstance(h, int) and h == 0):
                    se.wait_ge(s("silu_z"), h)
                A(zr, bank(1), ACT.Copy).then_inc(s("z_raw"), 1)

            def silus(h, b):
                se.wait_ge(s("tap"), 3 * CK * (h + 1))
                se.wait_ge(s("silu_z"), h)
                A(sg, cv, ACT.Sigmoid).then_inc(s("sig_qkv"), 1)
                se.wait_ge(s("silu_qkv"), h + 1)
                se.wait_ge(s("z_raw"), h + 1)
                A(sg[:, 0, :], zr, ACT.Sigmoid).then_inc(s("sig_z"), 1)
                A(sq, qkv[b][:, 0:2, :], ACT.Square).then_inc(s("sq_ready"), 1)

            def head(h, i, b, nxt):
                hn, bn = h + 1, 1 - b
                se.wait_ge(s("scalars_ready"), 9 * h + 1)
                A(rt[:, :, :], ss[:, :, :], ACT.Sqrt).then_inc(s("rt_ready"), 1)
                for d in (FWD, BWD):
                    se.wait_ge(s("decay_ps"), 2 * h + d + 1)
                    A(decay[:, d].rearrange("p t i -> p (t i)"), bank(6 + d), ACT.Exp).then_inc(s("decay_ready"), 1)
                se.wait_ge(s("kv_tok_ps"), h + 1)
                A(k_tok.rearrange("p t d -> p (t d)"), bank(2), ACT.Copy).then_inc(s("k_tok_ready"), 1)
                if nxt:
                    evac_raw(hn, 0)

                def evac_pw(d, n):
                    se.wait_ge(s(f"pw_ps{d}"), h * (LEVELS + 1) + n + 1)
                    if 0 < n < LEVELS:
                        se.wait_ge(s(f"pwT_ps{d}"), h * (LEVELS - 1) + n)
                    A(pw[:, d].rearrange("p t i -> p (t i)"), bank(2 + d), ACT.Copy).then_inc(s(f"pw_ready{d}"), 1)
                    if n == 1:
                        se.wait_ge(s(f"tT_ready{d}"), h * (LEVELS + 1) + 1)
                    if 0 < n < LEVELS:
                        A(pwT[:, d].rearrange("p t i -> p (t i)"), bank(4 + d), ACT.Copy)\
                            .then_inc(s(f"pwT_ready{d}"), 1)

                for d in (FWD, BWD):
                    evac_pw(d, 0)
                for n in range(1, LEVELS + 1):
                    if n == 4 and nxt:
                        evac_raw(hn, 1)
                    for d in (FWD, BWD):
                        evac_pw(d, n)

                def scan(step):
                    for d in (FWD, BWD):
                        t = step if d == FWD else TT - 1 - step
                        if step:
                            se.wait_ge(s("ks_ps"), 2 * ((TT - 1) * h + step - 1) + d + 1)
                            A(o_dir[:, d, t, :], bank(6 + d)[:, 0:P], ACT.Copy, scale=hs[:, EG + d, t:t + 1])\
                                .then_inc(s("qs_ready"), 1)

                scan(1)
                scan(2)
                if nxt:
                    evac_raw(hn, 2)
                scan(3)
                if nxt:
                    evac_z(hn)
                se.wait_ge(s("tail"), 8 * h + 5)
                A(oms[:, 1, :], oms[:, 0, :], ACT.Sqrt).then_inc(s("oms_root"), 1)
                se.wait_ge(s("ybT_ps"), h + 1)
                A(ybT[:, ds(h, 1), :].rearrange("p a i -> p (a i)"), bank(6), ACT.Copy, scale=gnw[:, 0:1])\
                    .then_inc(s("ybT_ready"), 1)
                if nxt:
                    silus(hn, bn)

            se.wait_ge(s("params_loaded"), 128)
            for part in range(3):
                evac_raw(0, part)
            evac_z(0)
            silus(0, 0)
            heads(se, head)

            def evac_pair(p, b):
                se.wait_ge(s("proj_qka"), 2 * p + 1)
                A(qa[b], bank(0), ACT.Copy, scale=ADH ** -0.5).then_inc(s("qkva_ready"), 1)
                se.wait_ge(s("proj_qka"), 2 * p + 2)
                A(ka[b], bank(1), ACT.Copy).then_inc(s("qkva_ready"), 1)
                se.wait_ge(s("proj_va"), p + 1)
                A(va[b].rearrange("p t d -> p (t d)"), bank(0), ACT.Copy).then_inc(s("qkva_ready"), 1)

            evac_pair(0, 0)

            def pair(p, i, b, nxt):
                for u in range(2 * TT):
                    hh, t = divmod(u, TT)
                    n = 2 * TT * p + u
                    se.wait_ge(s("nmx_ready"), n + 1)
                    if n >= 2:
                        se.wait_ge(s("pn_ready"), n - 1)
                    A(pr[u % 2], sc[u % 2], ACT.Exp, bias=nmx[:, u:u + 1], accum_out=lsum[:, u:u + 1])\
                        .then_inc(s("pr_ready"), 1)
                    if u:
                        evac_prT(p, u - 1)
                    if u == 6 and nxt:
                        evac_pair(p + 1, 1 - b)
                evac_prT(p, 2 * TT - 1)

            def evac_prT(p, u):
                hh, t = divmod(u, TT)
                n = 2 * TT * p + u
                se.wait_ge(s("prT_ps"), n + 1)
                if t == 0 and n:
                    se.wait_ge(s("pv_ps"), 2 * p + hh)
                A(prT[0][:, :, t * P:(t + 1) * P], tiles_of(4 + u % 2), ACT.Copy).then_inc(s("prT_ready"), 1)

            pairs(se, pair)

            attention_over(se)

            def merge(n, i, b):
                se.wait_ge(s("merge_ps"), n + 1)
                A(sig[b].rearrange("p a i -> p (a i)"), ps[:, 4 * b:4 * b + 2, :].rearrange("p a i -> p (a i)"),
                  ACT.Sigmoid).then_inc(s("sig_ready"), 1)

            merge(0, 0, 0)
            merge(1, 0, 1)
            with se.Fori(1, KD // 2) as i:
                for b in range(2):
                    se.wait_ge(s("mab_ready"), 2 * i + b - 1)
                    merge(2 * i + b, i, b)

            for t in range(TT):
                se.wait_ge(s("x1_added"), 2 * t + 2)
                se.wait_ge(s("ms_sum"), TT + t)
                A(sgm, xs[:, t, :], ACT.Square, accum_out=ms[:, 0, t:t + 1]).then_inc(s("ms_sum"), 1)
            se.wait_ge(s("ms_eps"), 2)
            A(ms[:, 1, :], ms[:, 0, :], ACT.Sqrt).then_inc(s("ms_root"), 1)
            for t in range(TT):
                se.wait_ge(s("h2T_ps"), t + 1)
                A(hT[:, :, t * P:(t + 1) * P], ps[:, 2 * (t % 2):2 * (t % 2) + 2, :]
                  .rearrange("p b (u d) -> p (b u) d", d=P), ACT.Copy).then_inc(s("h2T_ready"), 1)
            se.wait_ge(s("ngt_ready"), 1)
            for t in range(TT):
                A(gate[:, t, :], mx8[:, t, 0:TOPK], ACT.Exp, bias=ngt[:, t:t + 1], accum_out=gsum[:, t:t + 1])\
                    .then_inc(s("gate_exp"), 1)
            se.wait_ge(s("gmatT_ps"), 1)
            A(gmatT[0:NE, :, :], ps[0:NE, 4, :].rearrange("p (t d) -> p t d", t=TT), ACT.Copy)\
                .then_inc(s("gmatT_ready"), 1)

            def split_hi(b, a):
                se.wait_ge(s(f"raw_loaded{b}"), 16 * (a + 1))
                if not (isinstance(a, int) and a == 0):
                    se.wait_ge(s(f"split_used{b}"), a)
                A(w_hl[b][0], w_raw[b], ACT.Copy).then_inc(s(f"hi_ready{b}"), 1)

            two_banks = ps[:, 4:6, :].rearrange("p b (u d) -> p (b u) d", d=P)

            def xgT_hi(n, first=False):
                se.wait_ge(s("xgT_ps"), n + 1)
                if not first:
                    se.wait_ge(s("split_used3"), chunk_no(n - 1, KD - 1) + 1)
                A(xgT[0], two_banks, ACT.Copy).then_inc(s("xgT_ready"), 1)

            def actT_hi(n, first=False):
                se.wait_ge(s("actT_ps"), n)
                if not first:
                    se.wait_ge(s("split_used3"), chunk_no(n - 1, KD + 3) + 1)
                A(actT[0], two_banks, ACT.Copy).then_inc(s("actT_ready"), 1)

            def swish(n):
                se.wait_ge(s("swiglu"), 4 * n + 1)
                A(sgm, glu, ACT.Sigmoid, scale=ALPHA).then_inc(s("sgm_ready"), 1)

            def y_out(n, e, first=False, alone=False):
                se.wait_ge(s("split_used3"), down_no(n, 3, alone) + 1)
                if not first:
                    se.wait_ge(s("y_stored"), 16 * (n - 1))
                A(yrow, ps[:, 6:8, :].rearrange("p b d -> p (b d)"), ACT.Copy).then_inc(s("y_read"), 1)
                se.wait_ge(s("y_read"), n)
                se.dma_start(y_v[r_of[0], ds(e, 1)], yrow).then_inc(s("y_stored"), 16)

            se.wait_ge(s("bias_loaded"), 16)
            A(bias_hl[0:NE, :], bgu_rows[0:NE, :], ACT.Copy).then_inc(s("bias_hi"), 1)

            y_v = y_dram.rearrange("(r e p) d -> r e p d", r=ROUNDS, p=P)
            r_of = [0]

            def act_round(r):
                n0 = r * NE
                r_of[0] = ds(r, 1)
                first = isinstance(r, int)
                if first:
                    for b in range(2):
                        se.wait_ge(s(f"h2_stored{b}"), 16 * TT // 2)
                if first:
                    se.wait_ge(s("tok_of_ready"), 1)
                for j in range(SLOTS):
                    split_hi(j, chunk_no(n0, j, True))
                xgT_hi(n0, first)
                for j in range(SLOTS, KD):
                    split_hi(j % SLOTS, chunk_no(n0, j, True))
                se.wait_ge(s("xgT_ps"), n0 + 2)
                se.wait_ge(s("split_used3"), chunk_no(n0, KD - 1, True) + 1)
                A(xgT[0], two_banks, ACT.Copy).then_inc(s("xgT_ready"), 1)
                swish(n0)

                def step(n, e, y, first_down=False, more=True):
                    for j in range(4):
                        split_hi(j, chunk_no(n, j))
                    if y:
                        y_out(n - 1, e - 2, y == "first")
                    for j in range(4, 8):
                        split_hi(j % SLOTS, chunk_no(n, j))
                    actT_hi(n, first_down)
                    for j in range(8, 12):
                        split_hi(j % SLOTS, chunk_no(n, j))
                    if more:
                        xgT_hi(n + 1)
                    swish(n)

                step(n0 + 1, 1, False, first)
                step(n0 + 2, 2, "first" if first else True)
                with se.Fori(3, NE - 1) as e:
                    step(n0 + e, e, True)
                step(n0 + NE - 1, NE - 1, True, more=False)
                for c in range(FT // 2):
                    split_hi(c, down_no(n0 + NE, c, alone=True))
                y_out(n0 + NE - 1, NE - 2)
                actT_hi(n0 + NE)
                y_out(n0 + NE, NE - 1, alone=True)

            act_round(0)
            more_rounds(se, act_round)
            se.nop().then_inc(s("y_all_read"), 1)
            for t in range(TT):
                se.wait_ge(s("y_added"), TOPK * (t + 1))
                se.wait_ge(s("ms_sum"), 2 * TT + t)
                A(glu, xs[:, t, :], ACT.Square, accum_out=ms[:, 0, t:t + 1])\
                    .then_inc(s("ms_sum"), 1)
                se.wait_ge(s("ms_eps"), 3 + t)
                A(ms[:, 1, t:t + 1], ms[:, 0, t:t + 1], ACT.Sqrt).then_inc(s("ms_root"), 1)

        @block.vector
        def _(dve):
            V = nc.vector

            def eps_and_inverse(k, view=slice(0, TT)):
                V.tensor_scalar(ms[:, 0, view], ms[:, 0, view], 1.0 / D, EPS, ALU.mult, ALU.add)\
                    .then_inc(s("ms_eps"), 1)
                dve.wait_ge(s("ms_root"), k)
                V.reciprocal(ms[:, 2, view], ms[:, 1, view]).then_inc(s("ms_inv"), 1)

            dve.wait_ge(s("vecT_ps"), 1)
            V.tensor_copy(vecT[:, :], bank(6)[:, 0:P]).then_inc(s("vecT_ready"), 1)
            dve.wait_ge(s("ms_sum"), TT)
            eps_and_inverse(1)
            dve.wait_ge(s("vecT_ready"), 1)
            for t in range(TT):
                dve.wait_ge(s("hT_ps"), t + 1)
                V.tensor_tensor(hT[:, :, t * P:(t + 1) * P],
                                ps[:, 2 * (t % 2):2 * (t % 2) + 2, :].rearrange("p b (u d) -> p (b u) d", d=P),
                                wide(vecT[:, CONVS:P].unsqueeze(2), [P, KD, P]), ALU.mult)\
                    .then_inc(s("hT_ready"), 1)

            dve.wait_ge(s("ab_ps"), 1)
            V.tensor_copy(ab[:, :, :], bank(4)[:, 0:TT * 4 * BH].rearrange("p (t c) -> p c t", t=TT))\
                .then_inc(s("gates_dve"), 1)
            dve.wait_ge(s("gates_dve"), 1)
            dve.wait_ge(s("params_loaded"), 128)
            a_part, b_part = ab[:, 0:2 * BH, :], ab[:, 2 * BH:4 * BH, :]
            V.tensor_tensor(a_part, a_part,
                            wide(gate_c[:, 0:2, :].rearrange("p a h -> p (a h)").unsqueeze(2), [P, 2 * BH, TT]),
                            ALU.add).then_inc(s("gates_dve"), 1)
            dve.wait_ge(s("gates_dve"), 2)
            V.tensor_scalar(soft[:, :, :], a_part, -1.0, None, ALU.mult).then_inc(s("gates_dve"), 1)
            dve.wait_ge(s("gates_dve"), 3)
            V.tensor_tensor(soft[:, :, :], soft[:, :, :], a_part, ALU.max).then_inc(s("gates_dve"), 1)
            dve.wait_ge(s("gates_act"), 3)
            V.tensor_scalar(soft[:, :, :], soft[:, :, :], 1.0, None, ALU.add).then_inc(s("gates_dve"), 1)
            V.tensor_scalar(b_part, b_part, 1.0, None, ALU.add).then_inc(s("gates_dve"), 1)
            dve.wait_ge(s("gates_dve"), 6)
            V.reciprocal(gk[:, BETA:BETA + 2].rearrange("p k h t -> p (k h) t"), b_part).then_inc(s("gates_dve"), 1)
            V.tensor_scalar(a_part, a_part, 0.0, None, ALU.max).then_inc(s("gates_dve"), 1)
            dve.wait_ge(s("gates_dve"), 8)
            dve.wait_ge(s("gates_act"), 4)
            V.tensor_tensor(soft[:, :, :], soft[:, :, :], a_part, ALU.add).then_inc(s("gates_dve"), 1)
            dve.wait_ge(s("gates_dve"), 9)
            V.scalar_tensor_tensor(out=gk[:, GATE:GATE + 2].rearrange("p k h t -> p (k h) t"), in0=soft[:, :, :],
                                   scalar=-1.0,
                                   in1=wide(gate_c[:, 2:4, :].rearrange("p a h -> p (a h)").unsqueeze(2),
                                            [P, 2 * BH, TT]),
                                   op0=ALU.mult, op1=ALU.mult).then_inc(s("gates_dve"), 1)

            def conv(h, part):
                n0 = CK * (3 * h + part)
                dve.wait_ge(s("raw_ready"), 3 * h + part + 1)
                if part == 0:
                    if not (isinstance(h, int) and h == 0):
                        dve.wait_ge(s("sig_qkv"), h)
                    V.tensor_copy(taps[:, :, :].rearrange("p k w -> p (k w)").unsqueeze(2),
                                  vecT[:, 0:CONVS].rearrange("p (k h) -> p k h", h=BH)[:, :, ds(h, 1)])\
                        .then_inc(s("taps_ready"), 1)
                    dve.wait_ge(s("taps_ready"), h + 1)
                V.tensor_scalar(cv[:, part, :], raw[:, part, 0:S], taps[:, 0, part:part + 1], None, ALU.mult)\
                    .then_inc(s("tap"), 1)
                for k in range(1, CK):
                    dve.wait_ge(s("tap"), n0 + k)
                    V.scalar_tensor_tensor(out=cv[:, part, :], in0=raw[:, part, k:k + S],
                                           scalar=taps[:, k, part:part + 1], in1=cv[:, part, :],
                                           op0=ALU.mult, op1=ALU.add).then_inc(s("tap"), 1)

            def silus(h, b):
                dve.wait_ge(s("sig_qkv"), h + 1)
                V.tensor_tensor(qkv[b], cv, sg, ALU.mult).then_inc(s("silu_qkv"), 1)
                dve.wait_ge(s("sig_z"), h + 1)
                V.tensor_tensor(sz[b], zr, sg[:, 0, :], ALU.mult).then_inc(s("silu_z"), 1)

            kq = ps[:, 4:6, :].rearrange("p b (u w i) -> p (b u) w i", u=2, w=2)

            def head_scalars(h):
                V.tensor_copy(hs[:, :, :].unsqueeze(2), gk[:, :, ds(h, 1), :]).then_inc(s("hs_ready"), 1)

            def head(h, i, b, nxt):
                hn, bn = h + 1, 1 - b
                dve.wait_ge(s("ss_ps"), h + 1)
                V.tensor_scalar(ss[:, :, :].rearrange("p w t -> p (w t)"), bank(1)[:, 0:2 * TT], EPS, None, ALU.add)\
                    .then_inc(s("scalars_ready"), 1)
                dve.wait_ge(s("scalars_ready"), 9 * h + 1)
                V.reciprocal(r2[:, :], ss[:, 1, :]).then_inc(s("scalars_ready"), 1)
                dve.wait_ge(s("scalars_ready"), 9 * h + 2)
                dve.wait_ge(s("hs_ready"), h + 1)
                V.tensor_tensor(c1[:, :, :], hs[:, BETA:BETA + 2, :], wide(r2[:, :].unsqueeze(1), [P, 2, TT]),
                                ALU.mult).then_inc(s("scalars_ready"), 1)
                V.tensor_scalar(neg_eg[:, :, :], hs[:, EG:EG + 2, :], -1.0, None, ALU.mult)\
                    .then_inc(s("scalars_ready"), 1)
                dve.wait_ge(s("scalars_ready"), 9 * h + 3)
                V.tensor_scalar(nc1[:, :, :], c1[:, :, :], -1.0, None, ALU.mult).then_inc(s("scalars_ready"), 1)
                V.tensor_tensor(c2[:, :, :], c1[:, :, :], hs[:, KDEC:KDEC + 2, :], ALU.mult).then_inc(s("scalars_ready"), 1)
                dve.wait_ge(s("rt_ready"), h + 1)
                dve.wait_ge(s("kv_tok_ps"), h + 1)
                V.tensor_tensor(v_r, tiles_of(3), wide(rt[:, 1, :].unsqueeze(2), [P, TT, P]), ALU.mult)\
                    .then_inc(s("scalars_ready"), 1)
                V.reciprocal(rq[:, :], rt[:, 0, :]).then_inc(s("scalars_ready"), 1)
                dve.wait_ge(s("scalars_ready"), 9 * h + 8)
                V.tensor_scalar(rq[:, :], rq[:, :], BDH ** -0.5, None, ALU.mult).then_inc(s("scalars_ready"), 1)
                dve.wait_ge(s("kq_ps"), h + 1)
                dve.wait_ge(s("scalars_ready"), 9 * h + 5)
                for d in (FWD, BWD):
                    dve.wait_ge(s("masked"), 4 * h + 2 * d + 1)
                    for t in range(TT):
                        last = V.scalar_tensor_tensor(out=pwT[:, d, t, :], in0=kq[:, t, 1, :],
                                                      scalar=nc1[:, d, t:t + 1], in1=d_strict[:, d, t, :],
                                                      op0=ALU.mult, op1=ALU.mult)
                    last.then_inc(s("pT_made"), 1)
                for d in (FWD, BWD):
                    dve.wait_ge(s("masked"), 4 * h + 2 * d + 2)
                    V.tensor_tensor(qkd[:, d], kq[:, :, 0, :], d_incl[:, d], ALU.mult).then_inc(s("qkd_ready"), 1)
                dve.wait_ge(s("pT_made"), 2 * h + 2)
                for d in (FWD, BWD):
                    V.tensor_tensor(tT[:, d], pwT[:, d], wide(ident[:, :].unsqueeze(1), [P, TT, P]), ALU.add)\
                        .then_inc(s(f"tT_ready{d}"), 1)
                if nxt:
                    conv(hn, 0)

                for n in range(1, LEVELS + 1):
                    for d in (FWD, BWD):
                        dve.wait_ge(s(f"tT_ps{d}"), h * LEVELS + n)
                        dve.wait_ge(s(f"tT_ready{d}"), h * (LEVELS + 1) + n)
                        V.tensor_tensor(tT[:, d], tT[:, d], tiles_of(6 + d), ALU.add).then_inc(s(f"tT_ready{d}"), 1)
                    if n == 4 and nxt:
                        conv(hn, 1)

                def scan(step):
                    for d in (FWD, BWD):
                        t = step if d == FWD else TT - 1 - step
                        if step:
                            dve.wait_ge(s("ks_ps"), 2 * ((TT - 1) * h + step - 1) + d + 1)
                            dve.wait_ge(s("scalars_ready"), 9 * h + 4)
                            V.scalar_tensor_tensor(out=res[:, d, :], in0=bank(2 + d)[:, 0:P],
                                                   scalar=neg_eg[:, d, t:t + 1], in1=v_r[:, t, :],
                                                   op0=ALU.mult, op1=ALU.add).then_inc(s("res_ready"), 1)
                    for d in (FWD, BWD):
                        t = step if d == FWD else TT - 1 - step
                        dve.wait_ge(s("y_ps"), 2 * (TT * h + step) + d + 1)
                        V.tensor_scalar(vn[:, d, :], bank(2 + d)[:, 2 * P:3 * P], c1[:, d, t:t + 1], None,
                                        ALU.mult).then_inc(s("vn_ready"), 1)
                        if step < TT - 1:
                            dve.wait_ge(s("scalars_ready"), 9 * h + 6)
                            V.tensor_scalar(vs[:, d, :], bank(2 + d)[:, 2 * P:3 * P], c2[:, d, t:t + 1], None,
                                            ALU.mult).then_inc(s("vs_ready"), 1)
                    for d in (FWD, BWD):
                        t = step if d == FWD else TT - 1 - step
                        dve.wait_ge(s("os_ps"), 2 * (TT * h + step) + d + 1)
                        if step == 0:
                            V.tensor_copy(state[:, d, :], bank(4 + d)[:, P:2 * P]).then_inc(s("state_ready"), 1)
                            V.tensor_copy(o_dir[:, d, t, :], bank(4 + d)[:, 0:P]).then_inc(s("o_done"), 1)
                        else:
                            if step < TT - 1:
                                V.scalar_tensor_tensor(out=state[:, d, :], in0=state[:, d, :],
                                                       scalar=hs[:, GLAST + d, t:t + 1],
                                                       in1=bank(4 + d)[:, P:2 * P], op0=ALU.mult, op1=ALU.add)\
                                    .then_inc(s("state_ready"), 1)
                            dve.wait_ge(s("qs_ready"), 2 * ((TT - 1) * h + step - 1) + d + 1)
                            V.tensor_tensor(o_dir[:, d, t, :], o_dir[:, d, t, :], bank(4 + d)[:, 0:P], ALU.add)\
                                .then_inc(s("o_done"), 1)

                scan(0)
                scan(1)
                scan(2)
                scan(3)
                dve.wait_ge(s("o_done"), 2 * TT * (h + 1))
                V.tensor_tensor(yb, o_dir[:, FWD], o_dir[:, BWD], ALU.add).then_inc(s("tail"), 1)
                dve.wait_ge(s("tail"), 8 * h + 1)
                dve.wait_ge(s("scalars_ready"), 9 * h + 9)
                V.tensor_tensor(yb, yb, wide(rq[:, :].unsqueeze(2), [P, TT, P]), ALU.mult).then_inc(s("tail"), 1)
                dve.wait_ge(s("tail"), 8 * h + 2)
                V.tensor_tensor(yb_sq, yb, yb, ALU.mult).then_inc(s("tail"), 1)
                dve.wait_ge(s("tail"), 8 * h + 3)
                V.tensor_reduce(oms[:, 2, :], yb_sq, AX.X, ALU.add).then_inc(s("tail"), 1)
                dve.wait_ge(s("tail"), 8 * h + 4)
                V.tensor_scalar(oms[:, 0, :], oms[:, 2, :], 1.0 / BDH, EPS, ALU.mult, ALU.add)\
                    .then_inc(s("tail"), 1)
                if nxt:
                    head_scalars(hn)
                    conv(hn, 2)
                dve.wait_ge(s("oms_root"), h + 1)
                V.reciprocal(oms[:, 2, :], oms[:, 1, :]).then_inc(s("tail"), 1)
                dve.wait_ge(s("tail"), 8 * h + 6)
                V.tensor_tensor(yb, yb, wide(oms[:, 2, :].unsqueeze(2), [P, TT, P]), ALU.mult)\
                    .then_inc(s("tail"), 1)
                dve.wait_ge(s("tail"), 8 * h + 7)
                dve.wait_ge(s("silu_z"), h + 1)
                V.tensor_tensor(yb, yb, sz[b].rearrange("p (t d) -> p t d", t=TT), ALU.mult)\
                    .then_inc(s("tail"), 1)
                if nxt:
                    silus(hn, bn)

            dve.wait_ge(s("gates_act"), 5)
            dve.wait_ge(s("gates_dve"), 7)
            dve.wait_ge(s("gates_dve"), 10)
            head_scalars(0)
            for part in range(3):
                conv(0, part)
            silus(0, 0)
            heads(dve, head)

            deltanet_over(dve)
            dve.wait_ge(s("pool_setup"), 22)
            V.tensor_copy(dist, t_i).then_inc(s("mk"), 1)
            made = [1]

            def mk(ins):
                ins.then_inc(s("mk"), 1)
                made[0] += 1
                dve.wait_ge(s("mk"), made[0])

            dve.wait_ge(s("mk"), 1)
            mk(V.tensor_scalar(t_a, dist, -1.0, None, ALU.mult))
            mk(V.tensor_tensor(dist, dist, t_a, ALU.max))
            for gi, (window, dilation) in enumerate(PATTERNS):
                reach = (window // (2 * dilation)) * dilation
                dst = lnc if gi == 0 else t_b
                mk(V.tensor_scalar(dst, dist, float(reach), None, ALU.is_le))
                if dilation > 1:
                    mk(V.tensor_scalar(t_i, t_j, dilation - 1, None, ALU.bitwise_and))
                    mk(V.tensor_copy(t_a, t_i))
                    mk(V.tensor_scalar(t_a, t_a, 0.0, None, ALU.is_equal))
                    mk(V.tensor_tensor(t_b, t_b, t_a, ALU.mult))
                    mk(V.tensor_tensor(lnc, lnc, t_b, ALU.add))
            mk(V.tensor_scalar(t_a, lnc, 2.0, math.log(2.0), ALU.is_equal, ALU.mult))
            mk(V.tensor_scalar(t_b, lnc, 3.0, math.log(3.0), ALU.is_equal, ALU.mult))
            mk(V.tensor_scalar(t_c, lnc, 0.0, MASKED, ALU.is_equal, ALU.mult))
            mk(V.tensor_tensor(t_a, t_a, t_b, ALU.add))
            mk(V.tensor_tensor(lnc, t_a, t_c, ALU.add))
            dve.wait_ge(s("pool_setup"), 18)

            def pair(p, i, b, nxt):
                for u in range(2 * TT):
                    hh, t = divmod(u, TT)
                    n = 2 * TT * p + u
                    if t == 0:
                        if n:
                            dve.wait_ge(s("sc_made"), n)
                        V.scalar_tensor_tensor(out=bias[hh], in0=dist, scalar=slope[:, 2 * p + hh:2 * p + hh + 1],
                                               in1=lnc, op0=ALU.mult, op1=ALU.add).then_inc(s("bias_ready"), 1)
                        dve.wait_ge(s("bias_ready"), 2 * p + hh + 1)
                    dve.wait_ge(s("sc_ps"), n + 1)
                    if n >= 2:
                        dve.wait_ge(s("pr_ready"), n - 1)
                    c0 = (TT - 1 - t) * P
                    V.tensor_tensor(sc[u % 2], bank(2 + u % 2), bias[hh][:, c0:c0 + S], ALU.add)\
                        .then_inc(s("sc_ready"), 1)
                    dve.wait_ge(s("sc_ready"), n + 1)
                    V.tensor_reduce(mx[:, u:u + 1], sc[u % 2], AX.X, ALU.max).then_inc(s("sc_made"), 1)
                    dve.wait_ge(s("sc_made"), n + 1)
                    V.tensor_scalar(nmx[:, u:u + 1], mx[:, u:u + 1], -1.0, None, ALU.mult).then_inc(s("nmx_ready"), 1)
                    if u:
                        normalise(p, u - 1)
                    if u in (TT, ):
                        pv_out(p, 0)
                normalise(p, 2 * TT - 1)
                pv_out(p, 1)

            def normalise(p, u):
                n = 2 * TT * p + u
                dve.wait_ge(s("pr_ready"), n + 1)
                V.reciprocal(rl[:, u:u + 1], lsum[:, u:u + 1]).then_inc(s("rl_ready"), 1)
                dve.wait_ge(s("rl_ready"), n + 1)
                if n >= 2:
                    dve.wait_ge(s("prT_ps"), n - 1)
                V.tensor_scalar(pn[u % 2], pr[u % 2], rl[:, u:u + 1], None, ALU.mult).then_inc(s("pn_ready"), 1)

            def pv_out(p, hh):
                rows = slice(ADH * hh, ADH * hh + ADH)
                dve.wait_ge(s("pv_ps"), 2 * p + hh + 1)
                V.tensor_copy(yaT[rows, p, :], ps[rows, 6 + hh, :]).then_inc(s("yaT_ready"), 1)

            pairs(dve, pair)

            attention_over(dve)

            def merge(n, i, b):
                dve.wait_ge(s("sig_ready"), n + 1)
                V.tensor_tensor(mab[b], sig[b], ps[:, 4 * b + 2:4 * b + 4, :], ALU.mult).then_inc(s("mab_ready"), 1)
                dve.wait_ge(s("mab_ready"), n + 1)
                V.tensor_tensor(mT[:, ds(n, 1), :].rearrange("p a i -> p (a i)"), mab[b][:, 0, :], mab[b][:, 1, :],
                                ALU.add).then_inc(s("mT_ready"), 1)

            with dve.Fori(0, KD // 2) as i:
                merge(2 * i, i, 0)
                merge(2 * i + 1, i, 1)
            for t in range(TT):
                for half in range(2):
                    dve.wait_ge(s("x1_ps"), 2 * t + half + 1)
                    cols = slice(half * 512, (half + 1) * 512)
                    V.tensor_tensor(xs[:, t, cols], xs[:, t, cols], bank(2 * t + half), ALU.add)\
                        .then_inc(s("x1_added"), 1)

            dve.wait_ge(s("ms_sum"), 2 * TT)
            eps_and_inverse(2)
            dve.wait_ge(s("ms_inv"), 2)
            dve.wait_ge(s("late_params_loaded"), 80)
            for t in range(TT):
                if t >= 2:
                    dve.wait_ge(s("h2T_ps"), t - 1)
                    dve.wait_ge(s(f"h2_stored{t % 2}"), 16)
                V.scalar_tensor_tensor(out=h2[:, t % 2, :], in0=xs[:, t, :], scalar=ms[:, 2, t:t + 1], in1=nw2,
                                       op0=ALU.mult, op1=ALU.mult).then_inc(s("h2_ready"), 1)
            made_r = [0]

            def rt_step(ins):
                ins.then_inc(s("routing"), 1)
                made_r[0] += 1
                dve.wait_ge(s("routing"), made_r[0])

            dve.wait_ge(s("logits_ps"), 1)
            rt_step(V.tensor_tensor(lg[:, :, :], bank(4)[:, 0:TT * NE].rearrange("p (t e) -> p t e", t=TT),
                                    wide(rb[:, :].unsqueeze(1), [P, TT, NE]), ALU.add))
            for t in range(TT):
                rt_step(V.max(mx8[:, t, :], lg[:, t, :]))
                rt_step(V.max_index(ix8[:, t, :], mx8[:, t, :], lg[:, t, :]))
            V.tensor_scalar(ngt[:, :].unsqueeze(2), mx8[:, :, 0:1], -1.0, None, ALU.mult).then_inc(s("ngt_ready"), 1)
            rt_step(V.tensor_copy(idxf[:, :, :], ix8[:, :, 0:TOPK]))
            dve.wait_ge(s("pool_setup"), 10)
            n_rep = TT * TOPK
            oh = onehot[:, :, :, :].rearrange("p t j e -> p (t j) e")
            th = tmp_hot[:, :, :, :].rearrange("p t j e -> p (t j) e")

            def each(a):
                return wide(a[:, :, :].rearrange("p t j -> p (t j)").unsqueeze(2), [P, n_rep, NE])

            rt_step(V.tensor_tensor(oh, wide(i_slot[:, 0:NE].unsqueeze(1), [P, n_rep, NE]), each(idxf), ALU.is_equal))
            V.tensor_reduce(m4[:, :, :], onehot[:, :, :, :].rearrange("p t j e -> p t e j"), AX.X, ALU.add)\
                .then_inc(s("m4_ready"), 1)
            dve.wait_ge(s("gate_exp"), TT)
            rt_step(V.reciprocal(gsum[:, :], gsum[:, :]))
            rt_step(V.tensor_tensor(gate[:, :, :], gate[:, :, :], wide(gsum[:, :].unsqueeze(2), [P, TT, TOPK]),
                                    ALU.mult))
            rt_step(V.tensor_tensor(th, oh, each(gate), ALU.mult))
            rt_step(V.tensor_reduce(gmat[:, :, :], tmp_hot[:, :, :, :].rearrange("p t j e -> p t e j"), AX.X, ALU.add))
            V.nop().then_inc(s("gmat_ready"), 1)
            dve.wait_ge(s("rank_ps"), 1)
            dve.wait_ge(s("m4_ready"), 1)
            rt_step(V.tensor_copy(rk[:, :, :].rearrange("p t e -> p (t e)"), bank(6)[:, 0:TT * NE]))
            rt_step(V.tensor_reduce(cnt_f[:, :], bank(7)[:, 0:NE], AX.X, ALU.max))
            V.tensor_copy(cnt[:, :], cnt_f[:, :]).then_inc(s("cnt_ready"), 1)
            rt_step(V.scalar_tensor_tensor(out=rm[:, :, :].rearrange("p t e -> p (t e)"),
                                           in0=rk[:, :, :].rearrange("p t e -> p (t e)"), scalar=1.0,
                                           in1=m4[:, :, :].rearrange("p t e -> p (t e)"),
                                           op0=ALU.add, op1=ALU.mult))
            rt_step(V.tensor_scalar(rm[:, :, :], rm[:, :, :], -1.0, None, ALU.add))
            for t in range(TT):
                rt_step(V.tensor_tensor(tmp_hot[:, t], onehot[:, t], wide(rk[:, t, :].unsqueeze(1), [P, TOPK, NE]),
                                        ALU.mult))
            rt_step(V.tensor_reduce(posf[:, :, :].rearrange("p t j -> p (t j)"), th, AX.X, ALU.add))
            rt_step(V.scalar_tensor_tensor(out=rowf[:, :, :], in0=idxf[:, :, :], scalar=float(P), in1=posf[:, :, :],
                                           op0=ALU.mult, op1=ALU.add))
            for r in range(1, ROUNDS):
                rt_step(V.tensor_scalar(later[:, :, :], posf[:, :, :], float(r * P), float((NE - 1) * P),
                                        ALU.is_ge, ALU.mult))
                rt_step(V.tensor_tensor(rowf[:, :, :], rowf[:, :, :], later[:, :, :], ALU.add))
            V.tensor_copy(pos[:, :], rowf[:, :, :].rearrange("p t j -> p (t j)")).then_inc(s("pos_ready"), 1)

            def slot_tokens(r):
                if not isinstance(r, int):
                    V.tensor_scalar(rmr[:, :, :], rm[:, :, :], -float(P), None, ALU.add)\
                        .then_inc(s("rmr_ready"), 1)
                    dve.wait_ge(s("rmr_ready"), 2 * r - 1)
                    V.tensor_copy(rm[:, :, :], rmr[:, :, :]).then_inc(s("rmr_ready"), 1)
                    dve.wait_ge(s("rmr_ready"), 2 * r)
                for t in range(TT):
                    if not (isinstance(r, int) and t < 2):
                        dve.wait_ge(s("tok_ps"), r * TT + t - 1)
                    V.tensor_tensor(hot[t % 2], wide(i_slot[:, :].unsqueeze(1), [P, NE, P]),
                                    wide(rm[:, t, :].unsqueeze(2), [P, NE, P]), ALU.is_equal)\
                        .then_inc(s("hot_ready"), 1)
                dve.wait_ge(s("tok_ps"), r * TT + TT)
                V.tensor_copy(tok_of[:, :], bank(7)[:, 0:NE]).then_inc(s("tok_of_ready"), 1)

            def split_lo(b, a):
                if b == 1:
                    return
                dve.wait_ge(s(f"hi_ready{b}"), a + 1)
                V.tensor_tensor(w_hl[b][1], w_raw[b], w_hl[b][0].bitcast(F32), ALU.subtract)\
                    .then_inc(s(f"lo_ready{b}"), 1)

            two_banks = ps[:, 4:6, :].rearrange("p b (u d) -> p (b u) d", d=P)

            def xgT_lo(n):
                dve.wait_ge(s("xgT_ready"), 2 * n + 1)
                V.tensor_tensor(xgT[1], two_banks, xgT[0].bitcast(F32), ALU.subtract).then_inc(s("xgT_ready"), 1)

            def actT_lo(n):
                dve.wait_ge(s("actT_ready"), 2 * n - 1)
                V.tensor_tensor(actT[1], two_banks, actT[0].bitcast(F32), ALU.subtract)\
                    .then_inc(s("actT_ready"), 1)

            def picks(n, e, first=False):
                V.tensor_scalar(pick, e_row[:, :], i_slot[0:2 * NE, ds(e, 1)], None, ALU.is_equal)\
                    .then_inc(s("pick_ready"), 1)

            def clips(n, first=False):
                dve.wait_ge(s("split_used3"), chunk_no(n, KD - 1, first) + 1)
                if not (isinstance(n, int) and n == 0):
                    dve.wait_ge(s("sgm_ready"), n)
                V.tensor_scalar(glu, ps[:, 0:2, :].rearrange("p b d -> p (b d)"), LIMIT, None, ALU.min)\
                    .then_inc(s("swiglu"), 1)
                V.tensor_scalar(lin, ps[:, 2:4, :].rearrange("p b d -> p (b d)"), LIMIT, -LIMIT, ALU.min, ALU.max)\
                    .then_inc(s("swiglu"), 1)

            def product(n):
                dve.wait_ge(s("swiglu"), 4 * n + 2)
                V.scalar_tensor_tensor(out=lin, in0=lin, scalar=1.0, in1=glu, op0=ALU.add, op1=ALU.mult)\
                    .then_inc(s("swiglu"), 1)

            def activation(n):
                dve.wait_ge(s("swiglu"), 4 * n + 3)
                dve.wait_ge(s("sgm_ready"), n + 1)
                if not (isinstance(n, int) and n == 0):
                    dve.wait_ge(s("actT_ps"), n)
                V.tensor_tensor(act, lin, sgm, ALU.mult).then_inc(s("swiglu"), 1)

            def dve_round(r):
                n0 = r * NE
                slot_tokens(r)
                first = isinstance(r, int)
                if first:
                    dve.wait_ge(s("bias_hi"), 1)
                    V.tensor_tensor(bias_hl[NE:2 * NE, :], bgu_rows[0:NE, :], bias_hl[0:NE, :].bitcast(F32),
                                    ALU.subtract).then_inc(s("bias_lo"), 1)
                    dve.wait_ge(s("e_row_ready"), 2)
                    dve.wait_ge(s("bias_lo"), 1)
                picks(n0, 0)
                for j in range(SLOTS):
                    split_lo(j, chunk_no(n0, j, True))
                xgT_lo(n0)
                for j in range(SLOTS, KD):
                    split_lo(j % SLOTS, chunk_no(n0, j, True))
                clips(n0, True)
                picks(n0 + 1, 1)
                xgT_lo(n0 + 1)

                def step(n, e, more=True):
                    split_lo(0, chunk_no(n, 0))
                    product(n - 1)
                    split_lo(2, chunk_no(n, 2))
                    activation(n - 1)
                    for j in range(3, 8):
                        split_lo(j % SLOTS, chunk_no(n, j))
                    actT_lo(n)
                    for j in range(8, 11):
                        split_lo(j % SLOTS, chunk_no(n, j))
                    clips(n)
                    split_lo(3, chunk_no(n, 11))
                    if more:
                        picks(n + 1, e + 1)
                        xgT_lo(n + 1)

                step(n0 + 1, 1)
                with dve.Fori(2, NE - 1) as e:
                    step(n0 + e, e)
                step(n0 + NE - 1, NE - 1, more=False)
                product(n0 + NE - 1)
                activation(n0 + NE - 1)
                for c in range(FT // 2):
                    split_lo(c, down_no(n0 + NE, c, alone=True))
                actT_lo(n0 + NE)

            dve_round(0)
            more_rounds(dve, dve_round)
            for t in range(TT):
                for half in range(2):
                    cols = slice(half * 512, (half + 1) * 512)
                    dve.wait_ge(s("bd_ps"), 2 * t + half + 1)
                    V.tensor_tensor(xs[:, t, cols], xs[:, t, cols], bank(2 * t + half), ALU.add)\
                        .then_inc(s("bd_added"), 1)
            dve.wait_ge(s("late_params_loaded"), 80)
            for t in range(TT):
                for j in range(TOPK):
                    k = t * TOPK + j
                    dve.wait_ge(s(f"yg_loaded{j}"), 16 * (t + 1))
                    if j:
                        dve.wait_ge(s("y_added"), k)
                    else:
                        dve.wait_ge(s("bd_added"), 2 * t + 2)
                    V.scalar_tensor_tensor(out=xs[:, t, :], in0=yg[j], scalar=gate[:, t, j:j + 1], in1=xs[:, t, :],
                                           op0=ALU.mult, op1=ALU.add).then_inc(s("y_added"), 1)
                dve.wait_ge(s("ms_sum"), 2 * TT + t + 1)
                eps_and_inverse(3 + t, slice(t, t + 1))
                dve.wait_ge(s("ms_inv"), 3 + t)
                if t >= 2:
                    dve.wait_ge(s(f"out_stored{t % 2}"), 16)
                V.scalar_tensor_tensor(out=orow[t % 2], in0=xs[:, t, :], scalar=ms[:, 2, t:t + 1], in1=nwf,
                                       op0=ALU.mult, op1=ALU.mult).then_inc(s("out_ready"), 1)


_INS = ['x', 'norm1_w', 'w_in', 'conv_w', 'a_log_f', 'a_log_b', 'dt_bias_f', 'dt_bias_b', 'gdn_norm_w',
        'w_branch_a', 'w_branch_b', 'w_out', 'norm2_w', 'router_w', 'router_b', 'w_gate_up', 'b_gate_up',
        'w_down', 'b_down', 'norm_f_w']
_OUTS = [((1, 512, 1024), 'float32')]


def kernel(**inputs):
    import numpy as _np
    import concourse.bacc as _bacc
    from concourse import mybir as _mybir
    from concourse.bass_utils import run_bass_kernel_spmd as _run

    nc = _bacc.Bacc("TRN2", target_bir_lowering=False, num_devices=1)
    arrays, args = {}, []
    for name in _INS:
        a = _np.ascontiguousarray(inputs[name])
        arrays[f"in_{name}_dram"] = a
        args.append(nc.dram_tensor(f"in_{name}_dram", a.shape, _mybir.dt.from_np(a.dtype), kind="ExternalInput").ap())
    for i, (shape, dtype) in enumerate(_OUTS):
        dt = _mybir.dt.from_np(_np.dtype(dtype))
        args.append(nc.dram_tensor(f"out_{i}_dram", shape, dt, kind="ExternalOutput").ap())
    build(nc, *args)
    r = _run(nc, [arrays], core_ids=[0])
    return r.results[0]["out_0_dram"]
```

```python
from contextlib import ExitStack
import math

import concourse.bass as bass
from concourse import mybir

F32 = mybir.dt.float32
F32R = mybir.dt.float32r
F16 = mybir.dt.float16
I32 = mybir.dt.int32
U32 = mybir.dt.uint32
ALU = mybir.AluOpType
ACT = mybir.ActivationFunctionType
AX = mybir.AxisListType

P = 128
S = 512
TT = S // P
D = 1024
KD = D // P
AH, ADH = 8, 64
PAIRS = AH // 2
BH, BDH = 8, 128
CK = 5
HALO = CK // 2
NE, TOPK = 32, 4
FF = 1024
FT = FF // P
EPS = 1e-6
MASKED = -1e30
LIMIT, ALPHA = 7.0, 1.702
PATTERNS = ((128, 1), (512, 4), (2048, 16))
SLOPES = [2.0 ** (-8.0 * (h + 1) / AH) for h in range(AH)]
AW, BW = AH * ADH, BH * BDH
COL_QA, COL_KA, COL_VA = 0, AW, 2 * AW
COL_QB = 3 * AW
COL_KB, COL_VB = COL_QB + BW, COL_QB + 2 * BW
COL_Z = COL_QB + 3 * BW
COL_AB = COL_Z + BW
COL_GA = COL_AB + 4 * BH
COL_GB = COL_GA + D
IN_COLS = COL_GB + D
ROUNDS = S // P
FWD, BWD = 0, 1
LEVELS = 6


def build(nc, x, norm1_w, w_in, conv_w, a_log_f, a_log_b, dt_bias_f, dt_bias_b, gdn_norm_w,
          w_branch_a, w_branch_b, w_out, norm2_w, router_w, router_b, w_gate_up, b_gate_up,
          w_down, b_down, norm_f_w, out):
    ds = bass.ds
    x = x[0]
    out = out[0]
    w_in_v = w_in[0].rearrange("(k p) c -> p k c", p=P)
    wa_v = w_branch_a[0].rearrange("(k p) c -> p k c", p=P)
    wb_v = w_branch_b[0].rearrange("(k p) c -> p k c", p=P)
    wo_v = w_out[0].rearrange("(k p) c -> p k c", p=P)
    h2_dram = nc.dram_tensor("h2_rows", [S, D], F32).ap()
    y_dram = nc.dram_tensor("expert_rows", [NE * S, D], F32).ap()

    with ExitStack() as ctx:
        def sb(name, shape, dt=F32):
            return ctx.enter_context(nc.sbuf_tensor(name, shape, dt))

        def sem(name):
            return ctx.enter_context(nc.semaphore(name))

        ps = ctx.enter_context(nc.psum_tensor("ps", [P, 8, 512], F32))

        ARENA_FLOATS = 18432 + 20544 + 4096
        arena_at = -(-nc.sbuf_base // 32) * 32
        arena = sb("arena", [P, ARENA_FLOATS])

        def rounded(name, at, *shape, rows=P):
            return nc.alloc_sbuf_tensor_at(name, [rows, *shape], F32R, offset=arena_at + 4 * at).ap()

        def bank(b):
            return ps[:, b, :]

        def split(v, shape):
            names = "abcd"[:len(shape)]
            dims = dict(zip(names, shape))
            return v.rearrange(f"p ({' '.join(names)}) -> p {' '.join(names)}", **dims)

        class Area:

            def __init__(self, start, floats):
                self.whole, self.floats, self.at = arena[:, start:start + floats], floats, 0

            def take(self, *shape):
                n = math.prod(shape)
                v = self.whole[:, self.at:self.at + n]
                self.at += n
                assert self.at <= self.floats, (self.at, self.floats)
                return split(v, shape)

        def wide(ap, shape):
            return ap.to_broadcast(shape)

        xs = sb("xs", [P, TT, D])

        MIXER_FLOATS = 2 * KD * S + PAIRS * S + 2 * 4 * KD * P
        mixer = Area(0, MIXER_FLOATS)
        hT = mixer.take(KD, S)
        ybT = mixer.take(BH, S)
        yaT = mixer.take(PAIRS, S)
        wcols = [mixer.take(4, KD, P) for _ in range(2)]

        WORK_FLOATS = 20544
        work = Area(MIXER_FLOATS, WORK_FLOATS)
        ahead = Area(MIXER_FLOATS + WORK_FLOATS, 4096)

        ident = sb("ident", [P, P])
        ones = sb("ones", [P, P])
        upper_incl = sb("upper_incl", [P, P])
        upper_strict = sb("upper_strict", [P, P])
        lower_incl = sb("lower_incl", [P, P])
        lower_strict = sb("lower_strict", [P, P])
        vec_rows = sb("vec_rows", [P, P])
        vecT = sb("vecT", [P, P])
        CONVS = CK * 3 * BH
        gnw = sb("gnw", [P, 1])
        wab = sb("wab", [P, KD, 4 * BH])
        gate_c = sb("gate_c", [P, 4, BH])
        ab = sb("ab", [P, 4 * BH, TT])
        soft = sb("soft", [P, 2 * BH, TT])
        gk = sb("gk", [P, 10, BH, TT])
        EG, KDEC, GLAST, BETA, GATE = 0, 2, 4, 6, 8
        ms = sb("ms", [P, 3, TT])

        work.at = 0
        hrow = work.take(2, D)
        junk = work.take(D)

        work.at = 0
        raw = work.take(3, S + 2 * HALO)
        cv = work.take(3, S)
        sg = work.take(3, S)
        qkv = [work.take(3, S) for _ in range(2)]
        sq = work.take(2, S)
        zr = work.take(S)
        sz = [work.take(S) for _ in range(2)]
        k_tok = work.take(TT, P)
        v_r = work.take(TT, P)
        gmask = work.take(2, TT, P)
        decay = work.take(2, TT, P)
        d_strict = work.take(2, TT, P)
        d_incl = work.take(2, TT, P)
        qkd = work.take(2, TT, P)
        pw = work.take(2, TT, P)
        pwT = work.take(2, TT, P)
        tT = work.take(2, TT, P)
        res = work.take(2, P)
        vn = work.take(2, P)
        vs = work.take(2, P)
        state = work.take(2, P)
        o_dir = gmask
        yb = decay[:, 0, :, :]
        yb_sq = decay[:, 1, :, :]
        sgz = ahead.take(S)
        hs = sb("head_scalars", [P, 10, TT])
        taps = sb("taps", [P, CK, 3])
        c1 = sb("c1", [P, 2, TT])
        nc1 = sb("nc1", [P, 2, TT])
        c2 = sb("c2", [P, 2, TT])
        neg_eg = sb("neg_eg", [P, 2, TT])
        ss = sb("ss", [P, 2, TT])
        rt = sb("rt", [P, 2, TT])
        rq = sb("rq", [P, TT])
        r2 = sb("r2", [P, TT])
        oms = sb("oms", [P, 3, TT])

        DW = S + (TT - 1) * P
        work.at = 0
        dist = work.take(DW)
        lnc = work.take(DW)
        t_i = work.take(DW).bitcast(I32)
        t_j = work.take(DW).bitcast(I32)
        t_a, t_b, t_c = work.take(DW), work.take(DW), work.take(DW)
        bias = [work.take(DW) for _ in range(2)]
        qa = [work.take(S) for _ in range(2)]
        ka = [work.take(S) for _ in range(2)]
        va = [work.take(TT, P) for _ in range(2)]
        sc = [work.take(S) for _ in range(2)]
        pr = [work.take(S) for _ in range(2)]
        pn = [work.take(S) for _ in range(2)]
        prT = [work.take(TT, S)]
        slope = sb("slope", [P, AH])
        nmx = sb("nmx", [P, 2 * TT])
        mx = sb("mx", [P, 2 * TT])
        lsum = sb("lsum", [P, 2 * TT])
        rl = sb("rl", [P, 2 * TT])

        ATTENTION_FLOATS = 16256
        assert work.at <= ATTENTION_FLOATS
        at_lo = {"hT": 0, "ybT": KD * S, "yaT": (KD + BH) * S}
        at_cols = (KD + BH + PAIRS) * S
        at_merge = MIXER_FLOATS
        mT_hl = [rounded(f"mT{i}", at_merge + i * KD * S, KD, S) for i in range(2)]
        yaT_hl = [rounded("yaT_hi", at_merge + 2 * KD * S, PAIRS, S), rounded("yaT_lo", at_lo["yaT"], PAIRS, S)]
        PIECES = ((0, KD, 0), (1, KD, KD), (3, KD, 2 * KD), (2, PAIRS, 3 * KD))
        at_hi = at_merge + 2 * KD * S + PAIRS * S
        cols_hi = rounded("cols_hi", at_hi, 3 * KD + PAIRS, P)
        cols_lo = [rounded(f"cols_lo{b}", at_cols + b * 4 * KD * P, 4, KD, P) for b in range(2)]
        work.at = at_hi + (3 * KD + PAIRS) * P - MIXER_FLOATS
        sig = [work.take(2, S) for _ in range(2)]
        assert work.at <= ATTENTION_FLOATS
        at_free = MIXER_FLOATS + ATTENTION_FLOATS
        hT_hl = [rounded("hT_hi", at_free, KD, S), rounded("hT_lo", at_lo["hT"], KD, S)]
        ybT_hl = [rounded("ybT_hi", at_free + KD * S, BH, S), rounded("ybT_lo", at_lo["ybT"], BH, S)]
        WK = KD // 2
        wout = [arena[:, at_cols + b * 4 * KD * P:at_cols + b * 4 * KD * P + WK * D]
                .rearrange("p (k d) -> p k d", k=WK) for b in range(2)]
        wout_lo = [rounded(f"wout_lo{b}", at_cols + b * 4 * KD * P, WK, D) for b in range(2)]
        wout_hi = [rounded("wout_hi0", at_lo["hT"], WK, D), rounded("wout_hi1", at_hi, WK, D)]

        CHUNK = 2 * FF
        SLOTS = 4
        mixer.at = KD * S
        h2 = mixer.take(2, D)
        nw2 = mixer.take(D)
        GROUP = NE // 4
        HOTS = 4
        mixer.at += D
        hot = [mixer.take(GROUP * P // 2).bitcast(F16).rearrange("p (e s) -> p e s", e=GROUP) for _ in range(HOTS)]
        mixer.at = KD * S + 2 * D + D + 4096
        sgm = mixer.take(D)
        act = mixer.take(D)
        nwf = mixer.take(D)
        bd_rows = mixer.take(D)
        mixer.at = KD * S
        yrow = mixer.take(D)
        xg = mixer.take(D)
        glu = mixer.take(D)
        lin = mixer.take(D)
        bgu_rows = arena[:, 0:2 * FF]
        orow = [h2[:, 0, :], h2[:, 1, :]]
        yg = [arena[:, MIXER_FLOATS + k * D:MIXER_FLOATS + (k + 1) * D] for k in range(TT * TOPK)]
        at_bias = KD * S + 2 * D + D + 4096 + 4 * D
        bias_hl = rounded("bias_hl", at_bias, 2 * FF, rows=2 * NE)
        pick = rounded("pick", at_bias + 2 * FF, P, rows=2 * NE)
        assert at_bias + 2 * FF + P <= MIXER_FLOATS
        xgT = [rounded(f"xgT{i}", 2 * D + i * D, KD, P) for i in range(2)]
        actT = [rounded(f"actT{i}", i * D, FT, P) for i in range(2)]
        w_hl = [[rounded(f"w{b}_{i}", MIXER_FLOATS + (2 * b + i) * CHUNK, CHUNK) for i in range(2)]
                for b in range(SLOTS)]
        ahead.at = 0
        work.at = 2 * SLOTS * CHUNK
        w_raw = [ahead.take(CHUNK), ahead.take(CHUNK), work.take(CHUNK), work.take(CHUNK)]
        rw = sb("rw", [P, KD, NE])
        rb = sb("rb", [P, NE])
        lg = sb("lg", [P, TT, NE])
        mx8 = sb("mx8", [P, TT, 8])
        ix8 = sb("ix8", [P, TT, 8], U32)
        idxf = sb("idxf", [P, TT, TOPK])
        ngt = sb("ngt", [P, TT])
        gsum = sb("gsum", [P, TT])
        gate = sb("gate", [P, TT, TOPK])
        i_slot = sb("i_slot", [P, P])
        e_row = sb("e_row", [2 * NE, P])
        i_slot_i = sb("i_slot_i", [P, P], I32)
        one_v, tmp_v = (a[:, 0:TT * TOPK * NE] for a in (act, sgm))
        onehot, tmp_hot = (v.rearrange("p (t j e) -> p t j e", t=TT, j=TOPK) for v in (one_v, tmp_v))
        m4 = sb("m4", [P, TT, NE])
        gmat = sb("gmat", [P, TT, NE])
        gmatT = sb("gmatT", [P, TT, P])
        rk = sb("rk", [P, TT, NE])
        rm = sb("rm", [P, TT, NE])
        rmr = sb("rmr", [P, TT, NE])
        posf = sb("posf", [P, TT, TOPK])
        rowf = sb("rowf", [P, TT, TOPK])
        later = sb("later", [P, TT, TOPK])
        pos = sb("pos", [P, TT * TOPK], I32)
        cnt_f = sb("cnt_f", [P, 1])
        cnt = sb("cnt", [P, 1], I32)
        tokid_i = sb("tokid_i", [P, TT], I32)
        tokid = sb("tokid", [P, TT], F16)
        tok_of = sb("tok_of", [P, NE], I32)
        idx_col = sb("idx_col", [P, 1], I32)
        waited = sb("waited", [P, 4])

        sems = {}

        def s(name):
            if name not in sems:
                sems[name] = sem(name)
            return sems[name]

        block = ctx.enter_context(nc.Block())

        def tiles_of(b):
            return bank(b).rearrange("p (t d) -> p t d", t=TT)

        def heads(eng, step):
            last = BH // 2 - 1
            with eng.Fori(0, last) as i:
                step(2 * i, i, 0, True)
                step(2 * i + 1, i, 1, True)
            step(BH - 2, last, 0, True)
            step(BH - 1, last, 1, False)

        def pairs(eng, step):
            for p in range(PAIRS):
                step(p, p // 2, p % 2, p < PAIRS - 1)

        YB_H_SPLIT, YA_SPLIT, WOUT_SPLIT, BIAS_SPLIT = 8, 9, 9 + KD, 9 + KD + 1

        def operand_split(p):
            return (hT_hl, hT) if p == PAIRS - 1 else (ybT_hl, ybT)

        def mixer_over(eng):
            eng.wait_ge(s("x1_added"), 2 * TT)

        def deltanet_over(eng):
            eng.wait_ge(s("ybT_ready"), BH)
            eng.wait_ge(s("silu_z"), BH)

        def attention_over(eng):
            eng.wait_ge(s("yaT_ready"), 2 * PAIRS)


        def head_cols(i):
            return 64 * (i + 1)

        def pair_cols(i):
            return head_cols(BH // 2 - 1) + 48 * (i + 1)

        def merge_cols(i):
            return pair_cols(PAIRS // 2 - 1) + 64 * (i + 1)

        def more_rounds(eng, one_round):
            eng.wait_ge(s("cnt_ready"), 1)
            largest = eng.value_load(cnt[0:1, 0:1], min_val=0, max_val=S)
            with eng.If(largest > P):
                with eng.Fori(1, ROUNDS) as r:
                    with eng.If(largest > r * P):
                        one_round(r)
                        eng.nop()
                    with eng.Else():
                        eng.nop()
                eng.nop()
            with eng.Else():
                eng.nop()

        def chunk_no(n, j, first=False):
            return 3 * n + j // SLOTS if first else 3 * n - 1 + j // SLOTS

        def down_no(n, c, alone):
            return chunk_no(n, c if alone else KD + c)

        gu_v = w_gate_up[0].rearrange("e (k p) c -> e k p c", p=P)
        dn_v = w_down[0].rearrange("e (c f p) d -> e c p f d", f=2, p=P)

        @block.sync
        def _(sp):
            for t in range(TT):
                sp.dma_start(xs[:, t, :], x[t * P:(t + 1) * P, :]).then_inc(s("x_loaded"), 16)
            sp.dma_start(vec_rows[0:CONVS, :], conv_w[0].rearrange("k (c p) -> (k c) p", p=P))\
                .then_inc(s("params_loaded"), 16)
            sp.dma_start(vec_rows[CONVS:P, :], norm1_w[0].rearrange("(k p) -> k p", p=P))\
                .then_inc(s("params_loaded"), 16)
            sp.dma_start(wab[:, :, :], w_in_v[:, :, COL_AB:COL_AB + 4 * BH]).then_inc(s("params_loaded"), 16)
            for i, v in enumerate((dt_bias_f, dt_bias_b, a_log_f, a_log_b)):
                sp.dma_start(gate_c[:, i, :], v[0].partition_broadcast(P)).then_inc(s("params_loaded"), 16)
            sp.dma_start(gnw[:, :], gdn_norm_w[0].rearrange("(p a) -> p a", a=1)).then_inc(s("params_loaded"), 16)

            def load_cols(b, parts):
                for i, (view, tiles, col) in enumerate(parts):
                    sp.dma_start(wcols[b][:, i, 0:tiles, :], view[:, :, ds(col, P)])\
                        .then_inc(s(f"wcols_loaded{b}"), 16)

            def load_head(h, b):
                load_cols(b, [(w_in_v, KD, c + h * P) for c in (COL_QB, COL_KB, COL_VB, COL_Z)])

            def load_pair(p, b):
                load_cols(b, [(w_in_v, KD, c + p * P) for c in (COL_QA, COL_KA, COL_VA)])

            def load_merge(n, b):
                load_cols(b, [(w_in_v, KD, COL_GA + n * P), (w_in_v, KD, COL_GB + n * P),
                              (wa_v, PAIRS, n * P), (wb_v, KD, n * P)])

            load_head(0, 0)
            load_head(1, 1)
            with sp.Fori(0, BH // 2 - 1) as i:
                for b in range(2):
                    sp.wait_ge(s("proj_z"), 2 * i + b + 1)
                    load_head(2 * i + b + 2, b)
            for p in range(PAIRS):
                if p < 2:
                    sp.wait_ge(s("proj_z"), BH - 1 + p)
                else:
                    sp.wait_ge(s("proj_va"), p - 1)
                load_pair(p, p % 2)
            for n in range(2):
                sp.wait_ge(s("proj_va"), PAIRS - 1 + n)
                load_merge(n, n)
            attention_over(sp)
            with sp.Fori(0, KD // 2 - 1) as i:
                for b in range(2):
                    sp.wait_ge(s("merge_ps"), 4 * (2 * i + b + 1))
                    load_merge(2 * i + b + 2, b)
            for b in range(2):
                sp.wait_ge(s("merge_ps"), 4 * (KD - 1 + b))
                sp.dma_start(wout[b], wo_v[:, b * WK:(b + 1) * WK, :]).then_inc(s(f"wcols_loaded{b}"), 16)
            sp.dma_start(nw2, norm2_w[0].partition_broadcast(P)).then_inc(s("router_params_loaded"), 16)
            sp.dma_start(rw[:, :, :], router_w[0].rearrange("(k p) e -> p k e", p=P)).then_inc(s("router_params_loaded"), 16)
            sp.dma_start(rb[:, :], router_b[0].partition_broadcast(P)).then_inc(s("router_params_loaded"), 16)
            for j in range(SLOTS):
                sp.dma_start(w_raw[j], gu_v[0, j]).then_inc(s(f"raw_loaded{j}"), 16)
            mixer_over(sp)
            sp.dma_start(bd_rows[0:NE, :], b_down[0]).then_inc(s("late_params_loaded"), 16)
            sp.dma_start(nwf, norm_f_w.partition_broadcast(P)).then_inc(s("late_params_loaded"), 16)

            def load(b, a, src, two=False):
                if not (isinstance(a, int) and a == 0):
                    sp.wait_ge(s(f"lo_ready{b}"), a)
                dst = w_raw[b].rearrange("p (f d) -> p f d", f=2) if two else w_raw[b]
                sp.dma_start(dst, src).then_inc(s(f"raw_loaded{b}"), 16)

            def load_gate_up(n, e, first=False):
                for j in range(KD):
                    load(j % SLOTS, chunk_no(n, j, first), gu_v[ds(e, 1), j])

            def load_down(n, e, alone=False):
                for c in range(FT // 2):
                    load(c, down_no(n, c, alone), dn_v[ds(e, 1), c], two=True)

            for t in range(TT):
                sp.wait_ge(s("h2_ready"), t + 1)
                sp.dma_start(h2_dram[t * P:(t + 1) * P, :], h2[:, t % 2, :]).then_inc(s(f"h2_stored{t % 2}"), 16)
            for j in range(SLOTS, KD):
                load(j % SLOTS, j // SLOTS, gu_v[0:1, j])
            sp.wait_ge(s("logits_ps"), 1)
            sp.dma_start(bgu_rows[0:NE, :], b_gate_up[0]).then_inc(s("bias_loaded"), 16)

            def sp_rest(n0):
                with sp.Fori(1, NE) as e:
                    load_gate_up(n0 + e, e)
                    load_down(n0 + e, e - 1)
                load_down(n0 + NE, NE - 1, alone=True)

            sp_rest(0)

            def sp_round(r):
                load_gate_up(r * NE, 0, True)
                sp_rest(r * NE)

            more_rounds(sp, sp_round)
            for t in range(TT):
                sp.wait_ge(s("out_ready"), t + 1)
                sp.dma_start(out[t * P:(t + 1) * P, :], orow[t % 2]).then_inc(s(f"out_stored{t % 2}"), 16)
            for b in range(2):
                sp.wait_ge(s(f"out_stored{b}"), 16 * TT // 2)

        @block.gpsimd
        def _(pool):
            pool.memset(ones[:, :], 1.0).then_inc(s("pool_setup"), 1)
            pool.wait_ge(s("pool_setup"), 1)
            for m, base, per_col, per_row in ((upper_incl, 0, 1, -1), (upper_strict, -1, 1, -1),
                                              (lower_incl, 0, -1, 1), (lower_strict, -1, -1, 1)):
                pool.affine_select(out=m[:, :], in_=ones[:, :], pattern=[[per_col, P]], base=base,
                                   channel_multiplier=per_row, compare_op=ALU.is_ge, fill=0.0)\
                    .then_inc(s("pool_setup"), 1)
            pool.wait_ge(s("pool_setup"), 5)
            pool.tensor_tensor(ident[:, :], upper_incl[:, :], upper_strict[:, :], ALU.subtract)\
                .then_inc(s("pool_setup"), 1)
            pool.iota(i_slot_i[:, :], [[1, P]], base=0, channel_multiplier=0).then_inc(s("pool_setup"), 1)
            pool.iota(tokid_i[:, :], [[P, TT]], base=0, channel_multiplier=1).then_inc(s("pool_setup"), 1)
            pool.wait_ge(s("pool_setup"), 8)
            pool.tensor_copy(i_slot[:, :], i_slot_i[:, :]).then_inc(s("pool_setup"), 1)
            pool.tensor_copy(tokid[:, :], tokid_i[:, :]).then_inc(s("pool_setup"), 1)
            for half in range(2):
                if half:
                    pool.wait_ge(s("pool_setup"), 10)
                    pool.wait_ge(s("e_row_ready"), 1)
                pool.tensor_copy(e_row[half * NE:(half + 1) * NE, :], wide(tokid_i[0:NE, 0:1], [NE, P]))\
                    .then_inc(s("e_row_ready"), 1)
            pool.wait_ge(s("e_row_ready"), 2)
            for h in range(AH):
                pool.memset(slope[:, h:h + 1], -SLOPES[h]).then_inc(s("pool_setup"), 1)

            def head(h, i, b, nxt):
                pool.wait_ge(s("hs_ready"), h + 1)
                for d, m in ((FWD, upper_incl), (BWD, lower_incl)):
                    pool.tensor_tensor(gmask[:, d], wide(m[:, :].unsqueeze(1), [P, TT, P]),
                                       wide(hs[:, GATE + d, :].unsqueeze(2), [P, TT, P]), ALU.mult)\
                        .then_inc(s("gmask_ready"), 1)
                for d, strict, incl in ((FWD, upper_strict, upper_incl), (BWD, lower_strict, lower_incl)):
                    pool.wait_ge(s("decay_ready"), 2 * h + d + 1)
                    pool.tensor_tensor(d_strict[:, d], decay[:, d], wide(strict[:, :].unsqueeze(1), [P, TT, P]),
                                       ALU.mult).then_inc(s("masked"), 1)
                    pool.tensor_tensor(d_incl[:, d], decay[:, d], wide(incl[:, :].unsqueeze(1), [P, TT, P]),
                                       ALU.mult).then_inc(s("masked"), 1)

            pool.wait_ge(s("hT_ready"), TT)
            pool.memset(raw[:, :, 0:HALO], 0.0).then_inc(s("pool_setup"), 1)
            pool.memset(raw[:, :, HALO + S:], 0.0).then_inc(s("pool_setup"), 1)
            heads(pool, head)

            deltanet_over(pool)
            pool.iota(t_i, [[1, DW]], base=-(TT - 1) * P, channel_multiplier=-1).then_inc(s("pool_setup"), 1)
            pool.iota(t_j, [[1, DW]], base=P, channel_multiplier=-1).then_inc(s("pool_setup"), 1)

            def take_wait(i=0):
                pool.tensor_tensor(waited[:, i:i + 1], ones[:, 0:1], ones[:, 0:1], ALU.mult)

            def gathers(n, e):
                if not (isinstance(n, int) and n == 0):
                    pool.wait_ge(s("xgT_ps"), n)
                    pool.wait_ge(s("xg_loaded"), 16 * n)
                    take_wait()
                pool.tensor_copy(idx_col[:, :], tok_of[:, ds(e, 1)]).then_inc(s("idx_ready"), 1)
                pool.wait_ge(s("idx_ready"), n + 1)
                take_wait(1)
                pool.indirect_dma_start(xg, None, h2_dram, bass.IndirectOffsetOnAxis(ap=idx_col[:, 0:1], axis=0))\
                    .then_inc(s("xg_loaded"), 16)

            def split_lo(j, a):
                pool.wait_ge(s("hi_ready1"), a + 1)
                pool.tensor_tensor(w_hl[1][1], w_raw[1], w_hl[1][0].bitcast(F32), ALU.subtract)\
                    .then_inc(s("lo_ready1"), 1)

            def pool_round(r):
                n0 = r * NE
                if isinstance(r, int):
                    split_lo(1, 0)
                    for b in range(2):
                        pool.wait_ge(s(f"h2_stored{b}"), 16 * TT // 2)
                pool.wait_ge(s("tok_of_ready"), 4 * r + 1)
                take_wait(3)
                gathers(n0, 0)
                if not isinstance(r, int):
                    split_lo(1, chunk_no(n0, 1, True))
                gathers(n0 + 1, 1)
                split_lo(5, chunk_no(n0, 5, True))

                def step(e):
                    split_lo(1, chunk_no(n0 + e, 1))
                    gathers(n0 + e + 1, e + 1)
                    for j in (5, 9):
                        split_lo(j, chunk_no(n0 + e, j))

                with pool.Fori(1, GROUP - 1) as e:
                    step(e)
                pool.wait_ge(s("tok_of_ready"), 4 * r + 4)
                take_wait(2)
                with pool.Fori(GROUP - 1, NE - 1) as e:
                    step(e)
                for j in (1, 5, 9):
                    split_lo(j, chunk_no(n0 + NE - 1, j))
                split_lo(1, down_no(n0 + NE, 1, alone=True))
                pool.wait_ge(s("y_stored"), (r * NE + NE) * 16)

            pool_round(0)
            more_rounds(pool, pool_round)

            def results(rounds):
                for t in range(TT):
                    for j in range(TOPK):
                        k = t * TOPK + j
                        pool.indirect_dma_start(yg[k], None, y_dram[0:rounds * NE * P, :],
                                                bass.IndirectOffsetOnAxis(ap=pos[:, k:k + 1], axis=0))\
                            .then_inc(s(f"yg_loaded{t}"), 16)

            def results_of(rounds, largest):
                if rounds == ROUNDS:
                    results(rounds)
                    return
                with pool.If(largest > rounds * P):
                    results_of(rounds + 1, largest)
                    pool.nop()
                with pool.Else():
                    results(rounds)

            pool.wait_ge(s("pos_ready"), 1)
            results_of(1, pool.value_load(cnt[0:1, 0:1], min_val=0, max_val=S))

        @block.tensor
        def _(pe):
            def mm(o, lhsT, rhs, start=True, stop=True, **kw):
                return nc.tensor.matmul(o, lhsT, rhs, start=start, stop=stop, **kw)

            pe.wait_ge(s("pool_setup"), 6)
            pe.wait_ge(s("params_loaded"), 128)
            nc.tensor.transpose(bank(6)[:, 0:P], vec_rows[:, :], ident[:, :]).then_inc(s("vecT_ps"), 1)

            def to_features(t, source, ready, free, name):
                pe.wait_ge(s(ready), t + 1)
                if t >= 2:
                    pe.wait_ge(s(free), t - 1)
                two = ps[:, 2 * (t % 2):2 * (t % 2) + 2, :].rearrange("p b (u d) -> p (b u) d", d=P)
                for k in range(KD):
                    last = nc.tensor.transpose(two[:, k, :], source[:, t % 2, k * P:(k + 1) * P], ident[:, :])
                last.then_inc(s(name), 1)

            for t in range(TT):
                to_features(t, hrow, "hrow_ready", "hT_ready", "hT_ps")

            pe.wait_ge(s("params_loaded"), 128)
            pe.wait_ge(s("hT_ready"), TT)
            for t in range(TT):
                for k in range(KD):
                    last = mm(bank(4)[:, t * 4 * BH:(t + 1) * 4 * BH], hT[:, k, t * P:(t + 1) * P],
                              wab[:, k, :], k == 0, k == KD - 1)
            last.then_inc(s("ab_ps"), 1)

            def proj_qkv(h, i, b, part):
                if part == 0:
                    pe.wait_ge(s(f"wcols_loaded{b}"), head_cols(i))
                if not (isinstance(h, int) and h == 0 and part < 2):
                    if part == 0:
                        pe.wait_ge(s("raw_ready"), 3 * h)
                    elif part == 1:
                        pe.wait_ge(s("z_raw"), h)
                        pe.wait_ge(s("scalars_ready"), 9 * (h - 1) + 1)
                    else:
                        pe.wait_ge(s("raw_ready"), 3 * h + 1)
                for k in range(KD):
                    last = mm(bank(part % 2), wcols[b][:, part, k, :], hT[:, k, :], k == 0, k == KD - 1)
                last.then_inc(s("proj_qkv"), 1)

            def proj_z(h, b):
                pe.wait_ge(s("raw_ready"), 3 * h + 2)
                for t in range(TT):
                    for k in range(KD):
                        last = mm(tiles_of(1)[:, t, :], hT[:, k, t * P:(t + 1) * P], wcols[b][:, 3, k, :],
                                  k == 0, k == KD - 1)
                last.then_inc(s("proj_z"), 1)

            kq = ps[:, 4:6, :].rearrange("p b (u w i) -> p (b u) w i", u=2, w=2)

            def head(h, i, b, nxt):
                hn, bn = h + 1, 1 - b
                i_n = i + b
                q, k, v = qkv[b][:, 0, :], qkv[b][:, 1, :], qkv[b][:, 2, :]

                def tile(a, t):
                    return a[:, t * P:(t + 1) * P]

                pe.wait_ge(s("sq_ready"), h + 1)
                pe.wait_ge(s("z_raw"), h + 1)
                for w in range(2):
                    for t in range(TT):
                        last = mm(bank(1)[:, w * TT + t:w * TT + t + 1], tile(sq[:, w, :], t), ones[:, 0:1])
                last.then_inc(s("ss_ps"), 1)
                for d, m in ((FWD, lower_strict), (BWD, upper_strict)):
                    pe.wait_ge(s("gmask_ready"), 2 * h + d + 1)
                    mm(bank(6 + d), m[:, :], gmask[:, d].rearrange("p t i -> p (t i)")).then_inc(s("decay_ps"), 1)
                for t in range(TT):
                    nc.tensor.transpose(tiles_of(2)[:, t, :], tile(k, t), ident[:, :])
                for t in range(TT):
                    last = nc.tensor.transpose(tiles_of(3)[:, t, :], tile(v, t), ident[:, :])
                last.then_inc(s("kv_tok_ps"), 1)
                qk = qkv[b][:, 0:2, :].rearrange("p w (t i) -> p w t i", t=TT)
                for t in range(TT):
                    last = mm(kq[:, t], tile(k, t), qk[:, :, t, :])
                last.then_inc(s("kq_ps"), 1)
                if nxt:
                    proj_qkv(hn, i_n, bn, 0)

                for d in (FWD, BWD):
                    pe.wait_ge(s("pT_made"), 2 * h + d + 1)
                    if d == FWD:
                        pe.wait_ge(s("k_tok_ready"), h + 1)
                    else:
                        pe.wait_ge(s("scalars_ready"), 9 * h + 7)
                    for t in range(TT):
                        last = nc.tensor.transpose(tiles_of(2 + d)[:, t, :], pwT[:, d, t, :], ident[:, :])
                    last.then_inc(s(f"pw_ps{d}"), 1)

                def squares(d, n):
                    pe.wait_ge(s(f"pw_ready{d}"), h * (LEVELS + 1) + n)
                    if n > 1:
                        pe.wait_ge(s(f"pwT_ready{d}"), h * (LEVELS - 1) + n - 1)
                    for t in range(TT):
                        last = mm(tiles_of(2 + d)[:, t, :], pwT[:, d, t, :], pw[:, d, t, :])
                    last.then_inc(s(f"pw_ps{d}"), 1)
                    if n < LEVELS:
                        if n == 1:
                            pe.wait_ge(s("qkd_ready"), 2 * h + 2)
                        for t in range(TT):
                            last = mm(tiles_of(4 + d)[:, t, :], pw[:, d, t, :], pwT[:, d, t, :])
                        last.then_inc(s(f"pwT_ps{d}"), 1)

                def grow(d, n):
                    pe.wait_ge(s(f"pw_ready{d}"), h * (LEVELS + 1) + n + 1)
                    pe.wait_ge(s(f"tT_ready{d}"), h * (LEVELS + 1) + n)
                    for t in range(TT):
                        last = mm(tiles_of(6 + d)[:, t, :], pw[:, d, t, :], tT[:, d, t, :])
                    last.then_inc(s(f"tT_ps{d}"), 1)

                for d in (FWD, BWD):
                    squares(d, 1)
                for n in range(1, LEVELS + 1):
                    if n in (3, 5) and nxt:
                        proj_qkv(hn, i_n, bn, n // 2)
                    for d in (FWD, BWD):
                        grow(d, n)
                        if n < LEVELS:
                            squares(d, n + 1)

                def scan(step):
                    for d in (FWD, BWD):
                        t = step if d == FWD else TT - 1 - step
                        bk = bank(2 + d)
                        if step:
                            pe.wait_ge(s("state_ready"), 2 * ((TT - 1) * h + step - 1) + d + 1)
                            mm(bk[:, 0:P], tile(k, t), state[:, d, :])
                            if step > 1:
                                pe.wait_ge(s("qs_ready"), 2 * ((TT - 1) * h + step - 2) + d + 1)
                            mm(bank(6 + d)[:, 0:P], tile(q, t), state[:, d, :]).then_inc(s("ks_ps"), 1)
                    for d in (FWD, BWD):
                        t = step if d == FWD else TT - 1 - step
                        if step:
                            pe.wait_ge(s("res_ready"), 2 * ((TT - 1) * h + step - 1) + d + 1)
                        else:
                            pe.wait_ge(s(f"tT_ready{d}"), (h + 1) * (LEVELS + 1))
                            pe.wait_ge(s(f"pw_ready{d}"), (h + 1) * (LEVELS + 1))
                        mm(bank(2 + d)[:, 2 * P:3 * P], tT[:, d, t, :], res[:, d, :] if step else v_r[:, t, :])\
                            .then_inc(s("y_ps"), 1)
                    for d in (FWD, BWD):
                        t = step if d == FWD else TT - 1 - step
                        pe.wait_ge(s("vn_ready"), 2 * (TT * h + step) + d + 1)
                        last = mm(bank(4 + d)[:, 0:P], qkd[:, d, t, :], vn[:, d, :])
                        if step < TT - 1:
                            pe.wait_ge(s("vs_ready"), 2 * ((TT - 1) * h + step) + d + 1)
                            last = mm(bank(4 + d)[:, P:2 * P], k_tok[:, t, :], vs[:, d, :])
                        last.then_inc(s("os_ps"), 1)

                scan(0)
                scan(1)
                if nxt:
                    proj_z(hn, bn)
                scan(2)
                scan(3)
                pe.wait_ge(s("tail"), 8 * h + 8)
                for t in range(TT):
                    last = nc.tensor.transpose(tiles_of(6)[:, t, :], yb[:, t, :], ident[:, :])
                last.then_inc(s("ybT_ps"), 1)
                if nxt:
                    pe.wait_ge(s("ybT_ready"), h + 1)

            proj_qkv(0, 0, 0, 0)
            proj_qkv(0, 0, 0, 1)
            pe.wait_ge(s("gates_dve"), 10)
            W = BH * TT
            for j, (m, d) in enumerate(((upper_incl, FWD), (lower_incl, BWD), (lower_strict, FWD),
                                        (upper_strict, BWD), (ones, FWD), (ones, BWD))):
                last = mm(bank(5)[:, j * W:(j + 1) * W], m[:, :],
                          gk[:, GATE + d].rearrange("p h t -> p (h t)"))
            last.then_inc(s("cum_ps"), 1)
            proj_qkv(0, 0, 0, 2)
            proj_z(0, 0)
            heads(pe, head)

            def proj_pair(p, i, b):
                pe.wait_ge(s(f"wcols_loaded{b}"), pair_cols(i))
                for part in range(2):
                    if p:
                        pe.wait_ge(s("qkva_ready"), 3 * p - (2 if part == 0 else 1))
                        if part == 0:
                            pe.wait_ge(s("qkva_ready"), 3 * p)
                    else:
                        pe.wait_ge(s("z_raw"), BH)
                    for k in range(KD):
                        last = mm(bank(part), wcols[b][:, part, k, :], hT[:, k, :], k == 0, k == KD - 1)
                    last.then_inc(s("proj_qka"), 1)
                pe.wait_ge(s("qkva_ready"), 3 * p + 1)
                for t in range(TT):
                    for k in range(KD):
                        last = mm(tiles_of(0)[:, t, :], hT[:, k, t * P:(t + 1) * P], wcols[b][:, 2, k, :],
                                  k == 0, k == KD - 1)
                last.then_inc(s("proj_va"), 1)

            deltanet_over(pe)
            proj_pair(0, 0, 0)
            U = 2 * TT

            def scores(p, b, u):
                hh, t = divmod(u, TT)
                n = U * p + u
                rows = slice(ADH * hh, ADH * hh + ADH)
                if n >= 2:
                    pe.wait_ge(s("sc_ready"), n - 1)
                mm(bank(2 + u % 2), qa[b][rows, t * P:(t + 1) * P], ka[b][rows, :]).then_inc(s("sc_ps"), 1)

            def pair(p, i, b, nxt):
                pe.wait_ge(s("qkva_ready"), 3 * p + 3)
                scores(p, b, 0)
                scores(p, b, 1)
                for u in range(U):
                    hh, t = divmod(u, TT)
                    n = U * p + u
                    if u + 2 < U:
                        scores(p, b, u + 2)
                    pe.wait_ge(s("pn_ready"), n + 1)
                    if n >= 2:
                        pe.wait_ge(s("prT_ready"), n - 1)
                    for j in range(TT):
                        last = nc.tensor.transpose(tiles_of(4 + u % 2)[:, j, :], pn[u % 2][:, j * P:(j + 1) * P],
                                                   ident[:, :])
                    last.then_inc(s("prT_ps"), 1)
                    if u == 5 and nxt:
                        proj_pair(p + 1, i + b, 1 - b)
                    if t == TT - 1:
                        pe.wait_ge(s("prT_ready"), n + 1)
                        if 2 * p + hh >= 2:
                            pe.wait_ge(s("yaT_ready"), 2 * p + hh - 1)
                        for j in range(TT):
                            last = mm(ps[ADH * hh:ADH * hh + ADH, 6 + hh, :], va[b][:, j, ADH * hh:ADH * hh + ADH],
                                      prT[0][:, j, :], j == 0, j == TT - 1)
                        last.then_inc(s("pv_ps"), 1)

            pairs(pe, pair)

            attention_over(pe)

            def merge(n, i, b):
                pe.wait_ge(s(f"wcols_loaded{b}"), merge_cols(i))
                if not (isinstance(i, int) and i == 0):
                    pe.wait_ge(s("mT_ready"), n - 1)
                first = isinstance(n, int) and n == 0
                if first:
                    pe.wait_ge(s("operand_lo"), YB_H_SPLIT)
                for j, ((part, tiles, at), x) in enumerate(zip(PIECES, (hT_hl, hT_hl, ybT_hl, yaT_hl))):
                    if first and x is yaT_hl:
                        pe.wait_ge(s("operand_lo"), YA_SPLIT)
                    pe.wait_ge(s("cols_lo"), 4 * n + j + 1)
                    for k in range(tiles):
                        w = (cols_hi[:, at + k, :], cols_lo[b][:, part, k, :])
                        for wi, xi in ((0, 0), (0, 1), (1, 0)):
                            last = mm(bank(4 * b + part), w[wi], x[xi][:, k, :], k == 0 and wi == xi == 0,
                                      k == tiles - 1 and wi == 1)
                    last.then_inc(s("merge_ps"), 1)

            merge(0, 0, 0)
            merge(1, 0, 1)
            with pe.Fori(1, KD // 2) as i:
                merge(2 * i, i, 0)
                merge(2 * i + 1, i, 1)
            pe.wait_ge(s("mT_ready"), KD)

            def out_product(t, half, k):
                cols = slice(half * 512, (half + 1) * 512)
                w = (wout_hi[k // WK][:, k % WK, cols], wout_lo[k // WK][:, k % WK, cols])
                for wi, xi in ((0, 0), (0, 1), (1, 0)):
                    last = mm(bank(2 * t + half), mT_hl[xi][:, k, t * P:(t + 1) * P], w[wi],
                              k == 0 and wi == xi == 0, k == KD - 1 and wi == 1)
                return last

            for k in range(WK):
                pe.wait_ge(s("operand_lo"), YA_SPLIT + k + 1)
                for t in range(TT):
                    for half in range(2):
                        out_product(t, half, k)
            pe.wait_ge(s("operand_lo"), WOUT_SPLIT)
            for t in range(TT):
                for half in range(2):
                    for k in range(WK, KD):
                        last = out_product(t, half, k)
                    last.then_inc(s("x1_ps"), 1)
            pe.wait_ge(s("x1_added"), 2 * TT)
            for t in range(TT):
                to_features(t, h2, "h2_ready", "h2T_ready", "h2T_ps")
            pe.wait_ge(s("h2T_ready"), TT)
            pe.wait_ge(s("router_params_loaded"), 48)
            for t in range(TT):
                for k in range(KD):
                    last = mm(bank(4)[:, t * NE:(t + 1) * NE], hT[:, k, t * P:(t + 1) * P], rw[:, k, :],
                              k == 0, k == KD - 1)
            last.then_inc(s("logits_ps"), 1)
            pe.wait_ge(s("m4_ready"), 1)
            for t in range(TT):
                for u in range(t + 1):
                    last = mm(bank(6)[:, t * NE:(t + 1) * NE], (upper_strict if u == t else ones)[:, :],
                              m4[:, u, :], u == 0, u == t)
            for t in range(TT):
                last = mm(bank(7)[:, 0:NE], ones[:, :], m4[:, t, :], t == 0, t == TT - 1)
            last.then_inc(s("rank_ps"), 1)
            pe.wait_ge(s("gmat_ready"), 1)
            for t in range(TT):
                last = nc.tensor.transpose(ps[0:NE, 4, t * P:(t + 1) * P], gmat[:, t, :], ident[:, :])
            last.then_inc(s("gmatT_ps"), 1)

            def slot_tokens(r, g):
                if g >= 2:
                    pe.wait_ge(s("tok_of_ready"), 4 * r + g - 1)
                for t in range(TT):
                    n = g * TT + t
                    pe.wait_ge(s("hot_ready"), r * 4 * TT + n + 1)
                    for e in range(GROUP):
                        last = mm(bank(7 - g % 2)[:, e:e + 1], hot[n % HOTS][:, e, :], tokid[:, t:t + 1],
                                  t == 0 and e == 0, t == TT - 1, skip_group_check=True)
                    last.then_inc(s("tok_ps"), 1)

            def xg_to_features(n):
                pe.wait_ge(s("xg_loaded"), 16 * n + 16)
                if not (isinstance(n, int) and n < 2):
                    pe.wait_ge(s("actT_ready"), 2 * (n - 1))
                for k in range(KD):
                    last = nc.tensor.transpose(ps[:, 4 + k // 4, (k % 4) * P:(k % 4 + 1) * P],
                                               xg[:, k * P:(k + 1) * P], ident[:, :])
                last.then_inc(s("xgT_ps"), 1)

            def products(o, x_hl, w, first, last):
                for xi, wi in ((0, 0), (0, 1), (1, 0)):
                    for i, b in enumerate(o):
                        m = mm(bank(b), x_hl[xi], w[wi][:, i * 512:(i + 1) * 512],
                               first and xi == wi == 0, last and xi == 1)
                return m

            def gate_up(n, half, first=False, beside=None):
                if half == 0:
                    pe.wait_ge(s("xgT_ready"), 2 * n + 2)
                    pe.wait_ge(s("pick_ready"), n + 1)
                    if not (isinstance(n, int) and n == 0):
                        pe.wait_ge(s("swiglu"), 4 * n - 2)
                    for b in range(4):
                        mm(bank(b), pick, bias_hl[:, b * 512:(b + 1) * 512], True, False)
                for j in range(4 * half, 4 * half + 4):
                    pe.wait_ge(s(f"lo_ready{j % SLOTS}"), chunk_no(n, j, first) + 1)
                    products(range(4), [x[:, j, :] for x in xgT], w_hl[j % SLOTS], False, j == KD - 1)\
                        .then_inc(s(f"split_used{j % SLOTS}"), 1)
                    if beside:
                        beside(j)

            def bias_part(k):
                if k >= 2:
                    pe.wait_ge(s("bd_added"), k - 1)
                mm(bank(6 + k % 2), gmatT[0:NE, k // 2, :], bd_rows[0:NE, k % 2 * 512:(k % 2 + 1) * 512])\
                    .then_inc(s("bd_ps"), 1)

            def act_to_features(n):
                pe.wait_ge(s("swiglu"), 4 * n + 4)
                pe.wait_ge(s("xgT_ready"), 2 * n + 2)
                for k in range(FT):
                    last = nc.tensor.transpose(ps[:, 4 + k // 4, (k % 4) * P:(k % 4 + 1) * P],
                                               act[:, k * P:(k + 1) * P], ident[:, :])
                last.then_inc(s("actT_ps"), 1)

            def down(n, alone=False):
                pe.wait_ge(s("actT_ready"), 2 * n)
                if not (isinstance(n, int) and n == 1):
                    pe.wait_ge(s("y_read"), n - 1)
                for c in range(FT // 2):
                    pe.wait_ge(s(f"lo_ready{c}"), down_no(n, c, alone) + 1)
                    for f in (2 * c, 2 * c + 1):
                        m = products((6, 7), [a[:, f, :] for a in actT],
                                     [w[:, f % 2 * D:(f % 2 + 1) * D] for w in w_hl[c]], f == 0, f == FT - 1)
                    m.then_inc(s(f"split_used{c}"), 1)

            def pe_round(r):
                n0 = r * NE
                first = isinstance(r, int)
                if not first:
                    pe.wait_ge(s("y_read"), n0)
                slot_tokens(r, 0)
                pe.wait_ge(s("tok_of_ready"), 4 * r + 1)
                if first:
                    pe.wait_ge(s("gmatT_ready"), 1)
                    pe.wait_ge(s("late_params_loaded"), 32)
                xg_to_features(n0)
                for half in range(2):
                    gate_up(n0, half, True, bias_part if first else None)
                xg_to_features(n0 + 1)
                if first:
                    pe.wait_ge(s("bd_added"), 2 * TT)
                slot_tokens(r, 1)

                def step(n, more, second=False):
                    gate_up(n, 0)
                    if second:
                        slot_tokens(r, 2)
                    act_to_features(n - 1)
                    gate_up(n, 1)
                    if second:
                        slot_tokens(r, 3)
                    if more:
                        xg_to_features(n + 1)
                    if second:
                        pe.wait_ge(s("tok_of_ready"), 4 * r + 4)
                    down(n)

                step(n0 + 1, True, second=True)
                with pe.Fori(2, NE - 1) as e:
                    step(n0 + e, True)
                step(n0 + NE - 1, False)
                act_to_features(n0 + NE - 1)
                down(n0 + NE, alone=True)

            pe_round(0)
            more_rounds(pe, pe_round)

        @block.scalar
        def _(se):
            A = nc.scalar.activation

            se.wait_ge(s("x_loaded"), 16 * TT)
            for t in range(TT):
                if t:
                    se.wait_ge(s("ms_sum"), t)
                A(junk, xs[:, t, :], ACT.Square, accum_out=ms[:, 0, t:t + 1]).then_inc(s("ms_sum"), 1)
            se.wait_ge(s("ms_eps"), 1)
            A(ms[:, 1, :], ms[:, 0, :], ACT.Sqrt).then_inc(s("ms_root"), 1)
            se.wait_ge(s("ms_inv"), 1)
            for t in range(TT):
                if t >= 2:
                    se.wait_ge(s("hT_ps"), t - 1)
                A(hrow[:, t % 2, :], xs[:, t, :], ACT.Copy, scale=ms[:, 2, t:t + 1]).then_inc(s("hrow_ready"), 1)

            se.wait_ge(s("gates_dve"), 4)
            se.wait_ge(s("params_loaded"), 128)
            A(soft[:, :, :], soft[:, :, :], ACT.Exp, scale=-1.0).then_inc(s("gates_act"), 1)
            A(gate_c[:, 2:4, :], gate_c[:, 2:4, :], ACT.Exp).then_inc(s("gates_act"), 1)
            A(ab[:, 2 * BH:4 * BH, :], ab[:, 2 * BH:4 * BH, :], ACT.Exp, scale=-1.0).then_inc(s("gates_act"), 1)
            se.wait_ge(s("gates_dve"), 5)
            A(soft[:, :, :], soft[:, :, :], ACT.Ln).then_inc(s("gates_act"), 1)
            se.wait_ge(s("cum_ps"), 1)
            A(gk[:, 0:GLAST + 2].rearrange("p k h t -> p (k h t)"), bank(5)[:, 0:6 * BH * TT], ACT.Exp)\
                .then_inc(s("gates_act"), 1)

            def evac_raw(h, part):
                se.wait_ge(s("proj_qkv"), 3 * h + part + 1)
                if not (isinstance(h, int) and h == 0):
                    se.wait_ge(s("tap"), CK * (3 * (h - 1) + part + 1))
                elif part == 0:
                    se.wait_ge(s("pool_setup"), 20)
                A(raw[:, part, HALO:HALO + S], bank(part % 2), ACT.Copy).then_inc(s("raw_ready"), 1)

            def evac_z(h):
                se.wait_ge(s("proj_z"), h + 1)
                if not (isinstance(h, int) and h == 0):
                    se.wait_ge(s("silu_z"), h)
                A(zr, bank(1), ACT.Copy).then_inc(s("z_raw"), 1)

            def sigmoids(h):
                se.wait_ge(s("tap"), 3 * CK * (h + 1))
                if not (isinstance(h, int) and h == 0):
                    se.wait_ge(s("silu_z"), h)
                A(sg, cv, ACT.Sigmoid).then_inc(s("sig_qkv"), 1)
                se.wait_ge(s("z_raw"), h + 1)
                A(sgz, zr, ACT.Sigmoid).then_inc(s("sig_z"), 1)

            def squares(h, b):
                se.wait_ge(s("silu_qkv"), h + 1)
                A(sq, qkv[b][:, 0:2, :], ACT.Square).then_inc(s("sq_ready"), 1)

            def head(h, i, b, nxt):
                hn, bn = h + 1, 1 - b
                se.wait_ge(s("scalars_ready"), 9 * h + 1)
                A(rt[:, :, :], ss[:, :, :], ACT.Sqrt).then_inc(s("rt_ready"), 1)
                for d in (FWD, BWD):
                    se.wait_ge(s("decay_ps"), 2 * h + d + 1)
                    A(decay[:, d].rearrange("p t i -> p (t i)"), bank(6 + d), ACT.Exp).then_inc(s("decay_ready"), 1)
                se.wait_ge(s("kv_tok_ps"), h + 1)
                A(k_tok.rearrange("p t d -> p (t d)"), bank(2), ACT.Copy).then_inc(s("k_tok_ready"), 1)
                if nxt:
                    evac_raw(hn, 0)

                def evac_pw(d, n):
                    se.wait_ge(s(f"pw_ps{d}"), h * (LEVELS + 1) + n + 1)
                    if 0 < n < LEVELS:
                        se.wait_ge(s(f"pwT_ps{d}"), h * (LEVELS - 1) + n)
                    A(pw[:, d].rearrange("p t i -> p (t i)"), bank(2 + d), ACT.Copy).then_inc(s(f"pw_ready{d}"), 1)
                    if n == 1:
                        se.wait_ge(s(f"tT_ready{d}"), h * (LEVELS + 1) + 1)
                    if 0 < n < LEVELS:
                        A(pwT[:, d].rearrange("p t i -> p (t i)"), bank(4 + d), ACT.Copy)\
                            .then_inc(s(f"pwT_ready{d}"), 1)

                for d in (FWD, BWD):
                    evac_pw(d, 0)
                for n in range(1, LEVELS + 1):
                    if n in (4, 6) and nxt:
                        evac_raw(hn, n // 2 - 1)
                    for d in (FWD, BWD):
                        evac_pw(d, n)

                def scan(step):
                    for d in (FWD, BWD):
                        t = step if d == FWD else TT - 1 - step
                        if step:
                            se.wait_ge(s("ks_ps"), 2 * ((TT - 1) * h + step - 1) + d + 1)
                            A(o_dir[:, d, t, :], bank(6 + d)[:, 0:P], ACT.Copy, scale=hs[:, EG + d, t:t + 1])\
                                .then_inc(s("qs_ready"), 1)

                scan(1)
                if nxt:
                    evac_z(hn)
                scan(2)
                if nxt:
                    sigmoids(hn)
                scan(3)
                se.wait_ge(s("tail"), 8 * h + 5)
                A(oms[:, 1, :], oms[:, 0, :], ACT.Sqrt).then_inc(s("oms_root"), 1)
                if nxt:
                    squares(hn, bn)
                se.wait_ge(s("ybT_ps"), h + 1)
                A(ybT[:, ds(h, 1), :].rearrange("p a i -> p (a i)"), bank(6), ACT.Copy, scale=gnw[:, 0:1])\
                    .then_inc(s("ybT_ready"), 1)

            se.wait_ge(s("params_loaded"), 128)
            for part in range(3):
                evac_raw(0, part)
            evac_z(0)
            sigmoids(0)
            squares(0, 0)
            heads(se, head)

            def evac_pair(p, b):
                se.wait_ge(s("proj_qka"), 2 * p + 1)
                A(qa[b], bank(0), ACT.Copy, scale=ADH ** -0.5).then_inc(s("qkva_ready"), 1)
                se.wait_ge(s("proj_qka"), 2 * p + 2)
                A(ka[b], bank(1), ACT.Copy).then_inc(s("qkva_ready"), 1)
                se.wait_ge(s("proj_va"), p + 1)
                A(va[b].rearrange("p t d -> p (t d)"), bank(0), ACT.Copy).then_inc(s("qkva_ready"), 1)

            evac_pair(0, 0)

            def pair(p, i, b, nxt):
                for u in range(2 * TT):
                    hh, t = divmod(u, TT)
                    n = 2 * TT * p + u
                    se.wait_ge(s("nmx_ready"), n + 1)
                    if n >= 2:
                        se.wait_ge(s("pn_ready"), n - 1)
                    A(pr[u % 2], sc[u % 2], ACT.Exp, bias=nmx[:, u:u + 1], accum_out=lsum[:, u:u + 1])\
                        .then_inc(s("pr_ready"), 1)
                    if p >= PAIRS - 2 and u < 4:
                        if p == PAIRS - 1:
                            se.wait_ge(s("proj_va"), PAIRS)
                        (hi, _), whole = operand_split(p)
                        A(hi[:, 2 * u:2 * u + 2, :], whole[:, 2 * u:2 * u + 2, :], ACT.Copy)\
                            .then_inc(s("operand_hi"), 1)
                    if u:
                        evac_prT(p, u - 1)
                    if u == 6 and nxt:
                        evac_pair(p + 1, 1 - b)
                evac_prT(p, 2 * TT - 1)

            def evac_prT(p, u):
                hh, t = divmod(u, TT)
                n = 2 * TT * p + u
                se.wait_ge(s("prT_ps"), n + 1)
                if t == 0 and n:
                    se.wait_ge(s("pv_ps"), 2 * p + hh)
                A(prT[0][:, :, t * P:(t + 1) * P], tiles_of(4 + u % 2), ACT.Copy).then_inc(s("prT_ready"), 1)

            pairs(se, pair)

            attention_over(se)

            def cols_to_hi(n, i, b):
                se.wait_ge(s(f"wcols_loaded{b}"), merge_cols(i))
                for j, (part, tiles, at) in enumerate(PIECES):
                    if not (isinstance(n, int) and n == 0):
                        se.wait_ge(s("merge_ps"), 4 * (n - 1) + j + 1)
                    A(cols_hi[:, at:at + tiles, :], wcols[b][:, part, 0:tiles, :], ACT.Copy)\
                        .then_inc(s("cols_hi"), 1)

            def gates(n, b):
                if not (isinstance(n, int) and n < 2):
                    se.wait_ge(s("mT_ready"), n - 1)
                se.wait_ge(s("merge_ps"), 4 * n + 4)
                A(sig[b].rearrange("p a i -> p (a i)"), ps[:, 4 * b:4 * b + 2, :].rearrange("p a i -> p (a i)"),
                  ACT.Sigmoid).then_inc(s("sig_ready"), 1)

            def wout_to_hi(half):
                se.wait_ge(s(f"wcols_loaded{half}"), merge_cols(KD // 2 - 1) + 16)
                for k in range(WK):
                    A(wout_hi[half][:, k, :], wout[half][:, k, :], ACT.Copy).then_inc(s("operand_hi"), 1)

            cols_to_hi(0, 0, 0)
            A(yaT_hl[0], yaT, ACT.Copy).then_inc(s("operand_hi"), 1)
            cols_to_hi(1, 0, 1)
            gates(0, 0)
            cols_to_hi(2, 1, 0)
            gates(1, 1)
            with se.Fori(1, KD // 2 - 1) as i:
                cols_to_hi(2 * i + 1, i, 1)
                gates(2 * i, 0)
                cols_to_hi(2 * i + 2, i + 1, 0)
                gates(2 * i + 1, 1)
            cols_to_hi(KD - 1, KD // 2 - 1, 1)
            gates(KD - 2, 0)
            se.wait_ge(s("merge_ps"), 4 * KD - 2)
            wout_to_hi(0)
            gates(KD - 1, 1)
            se.wait_ge(s("mT_ready"), KD - 1)
            wout_to_hi(1)

            for t in range(TT):
                se.wait_ge(s("x1_added"), 2 * t + 2)
                se.wait_ge(s("ms_sum"), TT + t)
                A(sgm, xs[:, t, :], ACT.Square, accum_out=ms[:, 0, t:t + 1]).then_inc(s("ms_sum"), 1)
            se.wait_ge(s("ms_eps"), 2)
            A(ms[:, 1, :], ms[:, 0, :], ACT.Sqrt).then_inc(s("ms_root"), 1)
            for t in range(TT):
                se.wait_ge(s("h2T_ps"), t + 1)
                A(hT[:, :, t * P:(t + 1) * P], ps[:, 2 * (t % 2):2 * (t % 2) + 2, :]
                  .rearrange("p b (u d) -> p (b u) d", d=P), ACT.Copy).then_inc(s("h2T_ready"), 1)

            def split_hi(b, a):
                se.wait_ge(s(f"raw_loaded{b}"), 16 * (a + 1))
                if not (isinstance(a, int) and a == 0):
                    se.wait_ge(s(f"split_used{b}"), a)
                A(w_hl[b][0], w_raw[b], ACT.Copy).then_inc(s(f"hi_ready{b}"), 1)

            for j in range(SLOTS):
                split_hi(j, 0)
            se.wait_ge(s("ngt_ready"), 1)
            for t in range(TT):
                A(gate[:, t, :], mx8[:, t, 0:TOPK], ACT.Exp, bias=ngt[:, t:t + 1], accum_out=gsum[:, t:t + 1])\
                    .then_inc(s("gate_exp"), 1)
            se.wait_ge(s("gmatT_ps"), 1)
            A(gmatT[0:NE, :, :], ps[0:NE, 4, :].rearrange("p (t d) -> p t d", t=TT), ACT.Copy)\
                .then_inc(s("gmatT_ready"), 1)

            two_banks = ps[:, 4:6, :].rearrange("p b (u d) -> p (b u) d", d=P)

            def xgT_hi(n, first=False):
                se.wait_ge(s("xgT_ps"), n + 1)
                if not first:
                    se.wait_ge(s("split_used3"), chunk_no(n - 1, KD - 1) + 1)
                A(xgT[0], two_banks, ACT.Copy).then_inc(s("xgT_ready"), 1)

            def actT_hi(n, first=False):
                se.wait_ge(s("actT_ps"), n)
                if not first:
                    se.wait_ge(s("split_used3"), chunk_no(n - 1, KD + 3) + 1)
                A(actT[0], two_banks, ACT.Copy).then_inc(s("actT_ready"), 1)

            def swish(n):
                se.wait_ge(s("swiglu"), 4 * n + 1)
                A(sgm, glu, ACT.Sigmoid, scale=ALPHA).then_inc(s("sgm_ready"), 1)

            def y_out(n, e, first=False, alone=False):
                se.wait_ge(s("split_used3"), down_no(n, 3, alone) + 1)
                if not first:
                    se.wait_ge(s("y_stored"), 16 * (n - 1))
                A(yrow, ps[:, 6:8, :].rearrange("p b d -> p (b d)"), ACT.Copy).then_inc(s("y_read"), 1)
                se.wait_ge(s("y_read"), n)
                se.dma_start(y_v[r_of[0], ds(e, 1)], yrow).then_inc(s("y_stored"), 16)

            se.wait_ge(s("bias_loaded"), 16)
            A(bias_hl[0:NE, :], bgu_rows[0:NE, :], ACT.Copy).then_inc(s("operand_hi"), 1)

            y_v = y_dram.rearrange("(r e p) d -> r e p d", r=ROUNDS, p=P)
            r_of = [0]

            def act_round(r):
                n0 = r * NE
                r_of[0] = ds(r, 1)
                first = isinstance(r, int)
                if first:
                    for b in range(2):
                        se.wait_ge(s(f"h2_stored{b}"), 16 * TT // 2)
                else:
                    for j in range(SLOTS):
                        split_hi(j, chunk_no(n0, j, True))
                xgT_hi(n0, first)
                for j in range(SLOTS, KD):
                    split_hi(j % SLOTS, chunk_no(n0, j, True))
                se.wait_ge(s("xgT_ps"), n0 + 2)
                se.wait_ge(s("split_used3"), chunk_no(n0, KD - 1, True) + 1)
                A(xgT[0], two_banks, ACT.Copy).then_inc(s("xgT_ready"), 1)
                swish(n0)

                def step(n, e, y, first_down=False, more=True):
                    for j in range(4):
                        split_hi(j, chunk_no(n, j))
                    if y:
                        y_out(n - 1, e - 2, y == "first")
                    for j in range(4, 8):
                        split_hi(j % SLOTS, chunk_no(n, j))
                    actT_hi(n, first_down)
                    for j in range(8, 12):
                        split_hi(j % SLOTS, chunk_no(n, j))
                    if more:
                        xgT_hi(n + 1)
                    swish(n)

                step(n0 + 1, 1, False, first)
                step(n0 + 2, 2, "first" if first else True)
                with se.Fori(3, NE - 1) as e:
                    step(n0 + e, e, True)
                step(n0 + NE - 1, NE - 1, True, more=False)
                for c in range(FT // 2):
                    split_hi(c, down_no(n0 + NE, c, alone=True))
                y_out(n0 + NE - 1, NE - 2)
                actT_hi(n0 + NE)
                y_out(n0 + NE, NE - 1, alone=True)

            act_round(0)
            more_rounds(se, act_round)
            for t in range(TT):
                se.wait_ge(s("y_added"), TOPK * (t + 1))
                se.wait_ge(s("ms_sum"), 2 * TT + t)
                A(glu, xs[:, t, :], ACT.Square, accum_out=ms[:, 0, t:t + 1])\
                    .then_inc(s("ms_sum"), 1)
                se.wait_ge(s("ms_eps"), 3 + t)
                A(ms[:, 1, t:t + 1], ms[:, 0, t:t + 1], ACT.Sqrt).then_inc(s("ms_root"), 1)

        @block.vector
        def _(dve):
            V = nc.vector

            def eps_and_inverse(k, view=slice(0, TT)):
                V.tensor_scalar(ms[:, 0, view], ms[:, 0, view], 1.0 / D, EPS, ALU.mult, ALU.add)\
                    .then_inc(s("ms_eps"), 1)
                dve.wait_ge(s("ms_root"), k)
                V.reciprocal(ms[:, 2, view], ms[:, 1, view]).then_inc(s("ms_inv"), 1)

            dve.wait_ge(s("vecT_ps"), 1)
            V.tensor_copy(vecT[:, :], bank(6)[:, 0:P]).then_inc(s("vecT_ready"), 1)
            dve.wait_ge(s("ms_sum"), TT)
            eps_and_inverse(1)
            dve.wait_ge(s("vecT_ready"), 1)
            for t in range(TT):
                dve.wait_ge(s("hT_ps"), t + 1)
                V.tensor_tensor(hT[:, :, t * P:(t + 1) * P],
                                ps[:, 2 * (t % 2):2 * (t % 2) + 2, :].rearrange("p b (u d) -> p (b u) d", d=P),
                                wide(vecT[:, CONVS:P].unsqueeze(2), [P, KD, P]), ALU.mult)\
                    .then_inc(s("hT_ready"), 1)

            dve.wait_ge(s("ab_ps"), 1)
            V.tensor_copy(ab[:, :, :], bank(4)[:, 0:TT * 4 * BH].rearrange("p (t c) -> p c t", t=TT))\
                .then_inc(s("gates_dve"), 1)
            dve.wait_ge(s("gates_dve"), 1)
            dve.wait_ge(s("params_loaded"), 128)
            a_part, b_part = ab[:, 0:2 * BH, :], ab[:, 2 * BH:4 * BH, :]
            V.tensor_tensor(a_part, a_part,
                            wide(gate_c[:, 0:2, :].rearrange("p a h -> p (a h)").unsqueeze(2), [P, 2 * BH, TT]),
                            ALU.add).then_inc(s("gates_dve"), 1)
            dve.wait_ge(s("gates_dve"), 2)
            V.tensor_scalar(soft[:, :, :], a_part, -1.0, None, ALU.mult).then_inc(s("gates_dve"), 1)
            dve.wait_ge(s("gates_dve"), 3)
            V.tensor_tensor(soft[:, :, :], soft[:, :, :], a_part, ALU.max).then_inc(s("gates_dve"), 1)
            dve.wait_ge(s("gates_act"), 3)
            V.tensor_scalar(soft[:, :, :], soft[:, :, :], 1.0, None, ALU.add).then_inc(s("gates_dve"), 1)
            V.tensor_scalar(b_part, b_part, 1.0, None, ALU.add).then_inc(s("gates_dve"), 1)
            dve.wait_ge(s("gates_dve"), 6)
            V.reciprocal(gk[:, BETA:BETA + 2].rearrange("p k h t -> p (k h) t"), b_part).then_inc(s("gates_dve"), 1)
            V.tensor_scalar(a_part, a_part, 0.0, None, ALU.max).then_inc(s("gates_dve"), 1)
            dve.wait_ge(s("gates_dve"), 8)
            dve.wait_ge(s("gates_act"), 4)
            V.tensor_tensor(soft[:, :, :], soft[:, :, :], a_part, ALU.add).then_inc(s("gates_dve"), 1)
            dve.wait_ge(s("gates_dve"), 9)
            V.scalar_tensor_tensor(out=gk[:, GATE:GATE + 2].rearrange("p k h t -> p (k h) t"), in0=soft[:, :, :],
                                   scalar=-1.0,
                                   in1=wide(gate_c[:, 2:4, :].rearrange("p a h -> p (a h)").unsqueeze(2),
                                            [P, 2 * BH, TT]),
                                   op0=ALU.mult, op1=ALU.mult).then_inc(s("gates_dve"), 1)

            def conv(h, part):
                n0 = CK * (3 * h + part)
                dve.wait_ge(s("raw_ready"), 3 * h + part + 1)
                if part == 0:
                    if not (isinstance(h, int) and h == 0):
                        dve.wait_ge(s("sig_qkv"), h)
                    V.tensor_copy(taps[:, :, :].rearrange("p k w -> p (k w)").unsqueeze(2),
                                  vecT[:, 0:CONVS].rearrange("p (k h) -> p k h", h=BH)[:, :, ds(h, 1)])\
                        .then_inc(s("taps_ready"), 1)
                    dve.wait_ge(s("taps_ready"), h + 1)
                V.tensor_scalar(cv[:, part, :], raw[:, part, 0:S], taps[:, 0, part:part + 1], None, ALU.mult)\
                    .then_inc(s("tap"), 1)
                for k in range(1, CK):
                    dve.wait_ge(s("tap"), n0 + k)
                    V.scalar_tensor_tensor(out=cv[:, part, :], in0=raw[:, part, k:k + S],
                                           scalar=taps[:, k, part:part + 1], in1=cv[:, part, :],
                                           op0=ALU.mult, op1=ALU.add).then_inc(s("tap"), 1)

            def silus(h, b):
                dve.wait_ge(s("sig_qkv"), h + 1)
                V.tensor_tensor(qkv[b], cv, sg, ALU.mult).then_inc(s("silu_qkv"), 1)
                dve.wait_ge(s("sig_z"), h + 1)
                V.tensor_tensor(sz[b], zr, sgz, ALU.mult).then_inc(s("silu_z"), 1)

            kq = ps[:, 4:6, :].rearrange("p b (u w i) -> p (b u) w i", u=2, w=2)

            def head_scalars(h):
                V.tensor_copy(hs[:, :, :].unsqueeze(2), gk[:, :, ds(h, 1), :]).then_inc(s("hs_ready"), 1)

            def head(h, i, b, nxt):
                hn, bn = h + 1, 1 - b
                dve.wait_ge(s("ss_ps"), h + 1)
                V.tensor_scalar(ss[:, :, :].rearrange("p w t -> p (w t)"), bank(1)[:, 0:2 * TT], EPS, None, ALU.add)\
                    .then_inc(s("scalars_ready"), 1)
                dve.wait_ge(s("scalars_ready"), 9 * h + 1)
                V.reciprocal(r2[:, :], ss[:, 1, :]).then_inc(s("scalars_ready"), 1)
                dve.wait_ge(s("scalars_ready"), 9 * h + 2)
                dve.wait_ge(s("hs_ready"), h + 1)
                V.tensor_tensor(c1[:, :, :], hs[:, BETA:BETA + 2, :], wide(r2[:, :].unsqueeze(1), [P, 2, TT]),
                                ALU.mult).then_inc(s("scalars_ready"), 1)
                V.tensor_scalar(neg_eg[:, :, :], hs[:, EG:EG + 2, :], -1.0, None, ALU.mult)\
                    .then_inc(s("scalars_ready"), 1)
                dve.wait_ge(s("scalars_ready"), 9 * h + 3)
                V.tensor_scalar(nc1[:, :, :], c1[:, :, :], -1.0, None, ALU.mult).then_inc(s("scalars_ready"), 1)
                V.tensor_tensor(c2[:, :, :], c1[:, :, :], hs[:, KDEC:KDEC + 2, :], ALU.mult).then_inc(s("scalars_ready"), 1)
                dve.wait_ge(s("rt_ready"), h + 1)
                dve.wait_ge(s("kv_tok_ps"), h + 1)
                V.tensor_tensor(v_r, tiles_of(3), wide(rt[:, 1, :].unsqueeze(2), [P, TT, P]), ALU.mult)\
                    .then_inc(s("scalars_ready"), 1)
                V.reciprocal(rq[:, :], rt[:, 0, :]).then_inc(s("scalars_ready"), 1)
                dve.wait_ge(s("scalars_ready"), 9 * h + 8)
                V.tensor_scalar(rq[:, :], rq[:, :], BDH ** -0.5, None, ALU.mult).then_inc(s("scalars_ready"), 1)
                dve.wait_ge(s("kq_ps"), h + 1)
                dve.wait_ge(s("scalars_ready"), 9 * h + 5)
                for d in (FWD, BWD):
                    dve.wait_ge(s("masked"), 4 * h + 2 * d + 1)
                    for t in range(TT):
                        last = V.scalar_tensor_tensor(out=pwT[:, d, t, :], in0=kq[:, t, 1, :],
                                                      scalar=nc1[:, d, t:t + 1], in1=d_strict[:, d, t, :],
                                                      op0=ALU.mult, op1=ALU.mult)
                    last.then_inc(s("pT_made"), 1)
                for d in (FWD, BWD):
                    dve.wait_ge(s("masked"), 4 * h + 2 * d + 2)
                    V.tensor_tensor(qkd[:, d], kq[:, :, 0, :], d_incl[:, d], ALU.mult).then_inc(s("qkd_ready"), 1)
                dve.wait_ge(s("pT_made"), 2 * h + 2)
                for d in (FWD, BWD):
                    V.tensor_tensor(tT[:, d], pwT[:, d], wide(ident[:, :].unsqueeze(1), [P, TT, P]), ALU.add)\
                        .then_inc(s(f"tT_ready{d}"), 1)
                if nxt:
                    conv(hn, 0)

                for n in range(1, LEVELS + 1):
                    for d in (FWD, BWD):
                        dve.wait_ge(s(f"tT_ps{d}"), h * LEVELS + n)
                        dve.wait_ge(s(f"tT_ready{d}"), h * (LEVELS + 1) + n)
                        V.tensor_tensor(tT[:, d], tT[:, d], tiles_of(6 + d), ALU.add).then_inc(s(f"tT_ready{d}"), 1)
                    if n == 4 and nxt:
                        conv(hn, 1)

                def scan(step):
                    for d in (FWD, BWD):
                        t = step if d == FWD else TT - 1 - step
                        if step:
                            dve.wait_ge(s("ks_ps"), 2 * ((TT - 1) * h + step - 1) + d + 1)
                            dve.wait_ge(s("scalars_ready"), 9 * h + 4)
                            V.scalar_tensor_tensor(out=res[:, d, :], in0=bank(2 + d)[:, 0:P],
                                                   scalar=neg_eg[:, d, t:t + 1], in1=v_r[:, t, :],
                                                   op0=ALU.mult, op1=ALU.add).then_inc(s("res_ready"), 1)
                    for d in (FWD, BWD):
                        t = step if d == FWD else TT - 1 - step
                        dve.wait_ge(s("y_ps"), 2 * (TT * h + step) + d + 1)
                        V.tensor_scalar(vn[:, d, :], bank(2 + d)[:, 2 * P:3 * P], c1[:, d, t:t + 1], None,
                                        ALU.mult).then_inc(s("vn_ready"), 1)
                        if step < TT - 1:
                            dve.wait_ge(s("scalars_ready"), 9 * h + 6)
                            V.tensor_scalar(vs[:, d, :], bank(2 + d)[:, 2 * P:3 * P], c2[:, d, t:t + 1], None,
                                            ALU.mult).then_inc(s("vs_ready"), 1)
                    for d in (FWD, BWD):
                        t = step if d == FWD else TT - 1 - step
                        dve.wait_ge(s("os_ps"), 2 * (TT * h + step) + d + 1)
                        if step == 0:
                            V.tensor_copy(state[:, d, :], bank(4 + d)[:, P:2 * P]).then_inc(s("state_ready"), 1)
                            V.tensor_copy(o_dir[:, d, t, :], bank(4 + d)[:, 0:P]).then_inc(s("o_done"), 1)
                        else:
                            if step < TT - 1:
                                V.scalar_tensor_tensor(out=state[:, d, :], in0=state[:, d, :],
                                                       scalar=hs[:, GLAST + d, t:t + 1],
                                                       in1=bank(4 + d)[:, P:2 * P], op0=ALU.mult, op1=ALU.add)\
                                    .then_inc(s("state_ready"), 1)
                            dve.wait_ge(s("qs_ready"), 2 * ((TT - 1) * h + step - 1) + d + 1)
                            V.tensor_tensor(o_dir[:, d, t, :], o_dir[:, d, t, :], bank(4 + d)[:, 0:P], ALU.add)\
                                .then_inc(s("o_done"), 1)

                scan(0)
                scan(1)
                if nxt:
                    conv(hn, 2)
                scan(2)
                scan(3)
                dve.wait_ge(s("o_done"), 2 * TT * (h + 1))
                V.tensor_tensor(yb, o_dir[:, FWD], o_dir[:, BWD], ALU.add).then_inc(s("tail"), 1)
                dve.wait_ge(s("tail"), 8 * h + 1)
                dve.wait_ge(s("scalars_ready"), 9 * h + 9)
                V.tensor_tensor(yb, yb, wide(rq[:, :].unsqueeze(2), [P, TT, P]), ALU.mult).then_inc(s("tail"), 1)
                dve.wait_ge(s("tail"), 8 * h + 2)
                V.tensor_tensor(yb_sq, yb, yb, ALU.mult).then_inc(s("tail"), 1)
                dve.wait_ge(s("tail"), 8 * h + 3)
                V.tensor_reduce(oms[:, 2, :], yb_sq, AX.X, ALU.add).then_inc(s("tail"), 1)
                dve.wait_ge(s("tail"), 8 * h + 4)
                V.tensor_scalar(oms[:, 0, :], oms[:, 2, :], 1.0 / BDH, EPS, ALU.mult, ALU.add)\
                    .then_inc(s("tail"), 1)
                if nxt:
                    head_scalars(hn)
                    silus(hn, bn)
                dve.wait_ge(s("oms_root"), h + 1)
                V.reciprocal(oms[:, 2, :], oms[:, 1, :]).then_inc(s("tail"), 1)
                dve.wait_ge(s("tail"), 8 * h + 6)
                V.tensor_tensor(yb, yb, wide(oms[:, 2, :].unsqueeze(2), [P, TT, P]), ALU.mult)\
                    .then_inc(s("tail"), 1)
                dve.wait_ge(s("tail"), 8 * h + 7)
                dve.wait_ge(s("silu_z"), h + 1)
                V.tensor_tensor(yb, yb, sz[b].rearrange("p (t d) -> p t d", t=TT), ALU.mult)\
                    .then_inc(s("tail"), 1)

            dve.wait_ge(s("gates_act"), 5)
            dve.wait_ge(s("gates_dve"), 7)
            dve.wait_ge(s("gates_dve"), 10)
            head_scalars(0)
            for part in range(3):
                conv(0, part)
            silus(0, 0)
            heads(dve, head)

            deltanet_over(dve)
            dve.wait_ge(s("pool_setup"), 22)
            V.tensor_copy(dist, t_i).then_inc(s("mk"), 1)
            made = [1]

            def mk(ins):
                ins.then_inc(s("mk"), 1)
                made[0] += 1
                dve.wait_ge(s("mk"), made[0])

            dve.wait_ge(s("mk"), 1)
            mk(V.tensor_scalar(t_a, dist, -1.0, None, ALU.mult))
            mk(V.tensor_tensor(dist, dist, t_a, ALU.max))
            for gi, (window, dilation) in enumerate(PATTERNS):
                reach = (window // (2 * dilation)) * dilation
                dst = lnc if gi == 0 else t_b
                mk(V.tensor_scalar(dst, dist, float(reach), None, ALU.is_le))
                if dilation > 1:
                    mk(V.tensor_scalar(t_i, t_j, dilation - 1, None, ALU.bitwise_and))
                    mk(V.tensor_copy(t_a, t_i))
                    mk(V.tensor_scalar(t_a, t_a, 0.0, None, ALU.is_equal))
                    mk(V.tensor_tensor(t_b, t_b, t_a, ALU.mult))
                    mk(V.tensor_tensor(lnc, lnc, t_b, ALU.add))
            mk(V.tensor_scalar(t_a, lnc, 2.0, math.log(2.0), ALU.is_equal, ALU.mult))
            mk(V.tensor_scalar(t_b, lnc, 3.0, math.log(3.0), ALU.is_equal, ALU.mult))
            mk(V.tensor_scalar(t_c, lnc, 0.0, MASKED, ALU.is_equal, ALU.mult))
            mk(V.tensor_tensor(t_a, t_a, t_b, ALU.add))
            mk(V.tensor_tensor(lnc, t_a, t_c, ALU.add))
            dve.wait_ge(s("pool_setup"), 18)

            def pair(p, i, b, nxt):
                for u in range(2 * TT):
                    hh, t = divmod(u, TT)
                    n = 2 * TT * p + u
                    if t == 0:
                        if n:
                            dve.wait_ge(s("sc_made"), n)
                        V.scalar_tensor_tensor(out=bias[hh], in0=dist, scalar=slope[:, 2 * p + hh:2 * p + hh + 1],
                                               in1=lnc, op0=ALU.mult, op1=ALU.add).then_inc(s("bias_ready"), 1)
                        dve.wait_ge(s("bias_ready"), 2 * p + hh + 1)
                    dve.wait_ge(s("sc_ps"), n + 1)
                    if n >= 2:
                        dve.wait_ge(s("pr_ready"), n - 1)
                    c0 = (TT - 1 - t) * P
                    V.tensor_tensor(sc[u % 2], bank(2 + u % 2), bias[hh][:, c0:c0 + S], ALU.add)\
                        .then_inc(s("sc_ready"), 1)
                    dve.wait_ge(s("sc_ready"), n + 1)
                    V.tensor_reduce(mx[:, u:u + 1], sc[u % 2], AX.X, ALU.max).then_inc(s("sc_made"), 1)
                    dve.wait_ge(s("sc_made"), n + 1)
                    V.tensor_scalar(nmx[:, u:u + 1], mx[:, u:u + 1], -1.0, None, ALU.mult).then_inc(s("nmx_ready"), 1)
                    if u:
                        normalise(p, u - 1)
                    if p >= PAIRS - 2 and 1 <= u < 5:
                        (hi, lo), whole = operand_split(p)
                        q = slice(2 * u - 2, 2 * u)
                        dve.wait_ge(s("operand_hi"), 4 * (p - PAIRS + 2) + u)
                        V.tensor_tensor(lo[:, q, :], whole[:, q, :], hi[:, q, :].bitcast(F32), ALU.subtract)\
                            .then_inc(s("operand_lo"), 1)
                    if u in (TT, ):
                        pv_out(p, 0)
                normalise(p, 2 * TT - 1)
                pv_out(p, 1)

            def normalise(p, u):
                n = 2 * TT * p + u
                dve.wait_ge(s("pr_ready"), n + 1)
                V.reciprocal(rl[:, u:u + 1], lsum[:, u:u + 1]).then_inc(s("rl_ready"), 1)
                dve.wait_ge(s("rl_ready"), n + 1)
                if n >= 2:
                    dve.wait_ge(s("prT_ps"), n - 1)
                V.tensor_scalar(pn[u % 2], pr[u % 2], rl[:, u:u + 1], None, ALU.mult).then_inc(s("pn_ready"), 1)

            def pv_out(p, hh):
                rows = slice(ADH * hh, ADH * hh + ADH)
                dve.wait_ge(s("pv_ps"), 2 * p + hh + 1)
                V.tensor_copy(yaT[rows, p, :], ps[rows, 6 + hh, :]).then_inc(s("yaT_ready"), 1)

            pairs(dve, pair)

            attention_over(dve)

            def cols_to_lo(n, b):
                for j, (part, tiles, at) in enumerate(PIECES):
                    dve.wait_ge(s("cols_hi"), 4 * n + j + 1)
                    V.tensor_tensor(cols_lo[b][:, part, 0:tiles, :], wcols[b][:, part, 0:tiles, :],
                                    cols_hi[:, at:at + tiles, :].bitcast(F32), ALU.subtract)\
                        .then_inc(s("cols_lo"), 1)

            def combine(n, b):
                dve.wait_ge(s("sig_ready"), n + 1)
                V.tensor_tensor(sig[b], sig[b], ps[:, 4 * b + 2:4 * b + 4, :], ALU.mult).then_inc(s("mab_ready"), 1)
                dve.wait_ge(s("mab_ready"), 3 * n + 1)
                total = sig[b][:, 0, :]
                V.tensor_tensor(total, total, sig[b][:, 1, :], ALU.add).then_inc(s("mab_ready"), 1)
                dve.wait_ge(s("mab_ready"), 3 * n + 2)
                hi, lo = (m[:, ds(n, 1), :].rearrange("p a i -> p (a i)") for m in mT_hl)
                V.tensor_copy(hi, total).then_inc(s("mab_ready"), 1)
                dve.wait_ge(s("mab_ready"), 3 * n + 3)
                V.tensor_tensor(lo, total, hi.bitcast(F32), ALU.subtract).then_inc(s("mT_ready"), 1)

            def wout_to_lo(half):
                for k in range(WK):
                    dve.wait_ge(s("operand_hi"), YA_SPLIT + WK * half + k + 1)
                    V.tensor_tensor(wout_lo[half][:, k, :], wout[half][:, k, :],
                                    wout_hi[half][:, k, :].bitcast(F32), ALU.subtract).then_inc(s("operand_lo"), 1)

            cols_to_lo(0, 0)
            dve.wait_ge(s("operand_hi"), YA_SPLIT)
            V.tensor_tensor(yaT_hl[1], yaT, yaT_hl[0].bitcast(F32), ALU.subtract).then_inc(s("operand_lo"), 1)
            cols_to_lo(1, 1)
            combine(0, 0)
            cols_to_lo(2, 0)
            combine(1, 1)
            with dve.Fori(1, KD // 2 - 1) as i:
                cols_to_lo(2 * i + 1, 1)
                combine(2 * i, 0)
                cols_to_lo(2 * i + 2, 0)
                combine(2 * i + 1, 1)
            cols_to_lo(KD - 1, 1)
            combine(KD - 2, 0)
            wout_to_lo(0)
            combine(KD - 1, 1)
            wout_to_lo(1)
            for t in range(TT):
                for half in range(2):
                    dve.wait_ge(s("x1_ps"), 2 * t + half + 1)
                    cols = slice(half * 512, (half + 1) * 512)
                    V.tensor_tensor(xs[:, t, cols], xs[:, t, cols], bank(2 * t + half), ALU.add)\
                        .then_inc(s("x1_added"), 1)

            dve.wait_ge(s("ms_sum"), 2 * TT)
            eps_and_inverse(2)
            dve.wait_ge(s("ms_inv"), 2)
            dve.wait_ge(s("router_params_loaded"), 48)
            for t in range(TT):
                if t >= 2:
                    dve.wait_ge(s("h2T_ps"), t - 1)
                    dve.wait_ge(s(f"h2_stored{t % 2}"), 16)
                V.scalar_tensor_tensor(out=h2[:, t % 2, :], in0=xs[:, t, :], scalar=ms[:, 2, t:t + 1], in1=nw2,
                                       op0=ALU.mult, op1=ALU.mult).then_inc(s("h2_ready"), 1)

            def split_lo(b, a):
                if b == 1:
                    return
                dve.wait_ge(s(f"hi_ready{b}"), a + 1)
                V.tensor_tensor(w_hl[b][1], w_raw[b], w_hl[b][0].bitcast(F32), ALU.subtract)\
                    .then_inc(s(f"lo_ready{b}"), 1)

            for j in range(SLOTS):
                split_lo(j, 0)
            made_r = [0]

            def rt_step(ins):
                ins.then_inc(s("routing"), 1)
                made_r[0] += 1
                dve.wait_ge(s("routing"), made_r[0])

            dve.wait_ge(s("logits_ps"), 1)
            rt_step(V.tensor_tensor(lg[:, :, :], bank(4)[:, 0:TT * NE].rearrange("p (t e) -> p t e", t=TT),
                                    wide(rb[:, :].unsqueeze(1), [P, TT, NE]), ALU.add))
            for t in range(TT):
                rt_step(V.max(mx8[:, t, :], lg[:, t, :]))
                rt_step(V.max_index(ix8[:, t, :], mx8[:, t, :], lg[:, t, :]))
            V.tensor_scalar(ngt[:, :].unsqueeze(2), mx8[:, :, 0:1], -1.0, None, ALU.mult).then_inc(s("ngt_ready"), 1)
            rt_step(V.tensor_copy(idxf[:, :, :], ix8[:, :, 0:TOPK]))
            dve.wait_ge(s("pool_setup"), 10)
            n_rep = TT * TOPK
            oh = onehot[:, :, :, :].rearrange("p t j e -> p (t j) e")
            th = tmp_hot[:, :, :, :].rearrange("p t j e -> p (t j) e")

            def each(a):
                return wide(a[:, :, :].rearrange("p t j -> p (t j)").unsqueeze(2), [P, n_rep, NE])

            rt_step(V.tensor_tensor(oh, wide(i_slot[:, 0:NE].unsqueeze(1), [P, n_rep, NE]), each(idxf), ALU.is_equal))
            V.tensor_reduce(m4[:, :, :], onehot[:, :, :, :].rearrange("p t j e -> p t e j"), AX.X, ALU.add)\
                .then_inc(s("m4_ready"), 1)
            dve.wait_ge(s("gate_exp"), TT)
            rt_step(V.reciprocal(gsum[:, :], gsum[:, :]))
            rt_step(V.tensor_tensor(gate[:, :, :], gate[:, :, :], wide(gsum[:, :].unsqueeze(2), [P, TT, TOPK]),
                                    ALU.mult))
            rt_step(V.tensor_tensor(th, oh, each(gate), ALU.mult))
            rt_step(V.tensor_reduce(gmat[:, :, :], tmp_hot[:, :, :, :].rearrange("p t j e -> p t e j"), AX.X, ALU.add))
            V.nop().then_inc(s("gmat_ready"), 1)
            dve.wait_ge(s("rank_ps"), 1)
            dve.wait_ge(s("m4_ready"), 1)
            rt_step(V.tensor_copy(rk[:, :, :].rearrange("p t e -> p (t e)"), bank(6)[:, 0:TT * NE]))
            rt_step(V.tensor_reduce(cnt_f[:, :], bank(7)[:, 0:NE], AX.X, ALU.max))
            V.tensor_copy(cnt[:, :], cnt_f[:, :]).then_inc(s("cnt_ready"), 1)
            rt_step(V.scalar_tensor_tensor(out=rm[:, :, :].rearrange("p t e -> p (t e)"),
                                           in0=rk[:, :, :].rearrange("p t e -> p (t e)"), scalar=1.0,
                                           in1=m4[:, :, :].rearrange("p t e -> p (t e)"),
                                           op0=ALU.add, op1=ALU.mult))
            rt_step(V.tensor_scalar(rm[:, :, :], rm[:, :, :], -1.0, None, ALU.add))
            def positions():
                for t in range(TT):
                    rt_step(V.tensor_tensor(tmp_hot[:, t], onehot[:, t], wide(rk[:, t, :].unsqueeze(1), [P, TOPK, NE]),
                                            ALU.mult))
                rt_step(V.tensor_reduce(posf[:, :, :].rearrange("p t j -> p (t j)"), th, AX.X, ALU.add))
                rt_step(V.scalar_tensor_tensor(out=rowf[:, :, :], in0=idxf[:, :, :], scalar=float(P), in1=posf[:, :, :],
                                               op0=ALU.mult, op1=ALU.add))
                for r in range(1, ROUNDS):
                    rt_step(V.tensor_scalar(later[:, :, :], posf[:, :, :], float(r * P), float((NE - 1) * P),
                                            ALU.is_ge, ALU.mult))
                    rt_step(V.tensor_tensor(rowf[:, :, :], rowf[:, :, :], later[:, :, :], ALU.add))
                V.tensor_copy(pos[:, :], rowf[:, :, :].rearrange("p t j -> p (t j)")).then_inc(s("pos_ready"), 1)

            def ranks(r):
                if not isinstance(r, int):
                    V.tensor_scalar(rmr[:, :, :], rm[:, :, :], -float(P), None, ALU.add)\
                        .then_inc(s("rmr_ready"), 1)
                    dve.wait_ge(s("rmr_ready"), 2 * r - 1)
                    V.tensor_copy(rm[:, :, :], rmr[:, :, :]).then_inc(s("rmr_ready"), 1)
                    dve.wait_ge(s("rmr_ready"), 2 * r)

            def hots(r, g):
                for t in range(TT):
                    n = g * TT + t
                    if not (isinstance(r, int) and n < HOTS):
                        dve.wait_ge(s("tok_ps"), r * 4 * TT + n - HOTS + 1)
                    V.tensor_tensor(hot[n % HOTS], wide(i_slot[:, :].unsqueeze(1), [P, GROUP, P]),
                                    wide(rm[:, t, g * GROUP:(g + 1) * GROUP].unsqueeze(2), [P, GROUP, P]),
                                    ALU.is_equal).then_inc(s("hot_ready"), 1)

            def table(r, g):
                dve.wait_ge(s("tok_ps"), r * 4 * TT + (g + 1) * TT)
                V.tensor_copy(tok_of[:, g * GROUP:(g + 1) * GROUP], bank(7 - g % 2)[:, 0:GROUP])\
                    .then_inc(s("tok_of_ready"), 1)

            two_banks = ps[:, 4:6, :].rearrange("p b (u d) -> p (b u) d", d=P)

            def xgT_lo(n):
                dve.wait_ge(s("xgT_ready"), 2 * n + 1)
                V.tensor_tensor(xgT[1], two_banks, xgT[0].bitcast(F32), ALU.subtract).then_inc(s("xgT_ready"), 1)

            def actT_lo(n):
                dve.wait_ge(s("actT_ready"), 2 * n - 1)
                V.tensor_tensor(actT[1], two_banks, actT[0].bitcast(F32), ALU.subtract)\
                    .then_inc(s("actT_ready"), 1)

            def picks(n, e):
                V.tensor_scalar(pick, e_row[:, :], i_slot[0:2 * NE, ds(e, 1)], None, ALU.is_equal)\
                    .then_inc(s("pick_ready"), 1)

            def clips(n, first=False):
                dve.wait_ge(s("split_used3"), chunk_no(n, KD - 1, first) + 1)
                if not (isinstance(n, int) and n == 0):
                    dve.wait_ge(s("sgm_ready"), n)
                V.tensor_scalar(glu, ps[:, 0:2, :].rearrange("p b d -> p (b d)"), LIMIT, None, ALU.min)\
                    .then_inc(s("swiglu"), 1)
                V.tensor_scalar(lin, ps[:, 2:4, :].rearrange("p b d -> p (b d)"), LIMIT, -LIMIT, ALU.min, ALU.max)\
                    .then_inc(s("swiglu"), 1)

            def product(n):
                dve.wait_ge(s("swiglu"), 4 * n + 2)
                V.scalar_tensor_tensor(out=lin, in0=lin, scalar=1.0, in1=glu, op0=ALU.add, op1=ALU.mult)\
                    .then_inc(s("swiglu"), 1)

            def activation(n):
                dve.wait_ge(s("swiglu"), 4 * n + 3)
                dve.wait_ge(s("sgm_ready"), n + 1)
                if not (isinstance(n, int) and n == 0):
                    dve.wait_ge(s("actT_ps"), n)
                V.tensor_tensor(act, lin, sgm, ALU.mult).then_inc(s("swiglu"), 1)

            def bias_part_in(k):
                cols = slice(k % 2 * 512, (k % 2 + 1) * 512)
                dve.wait_ge(s("bd_ps"), k + 1)
                V.tensor_tensor(xs[:, k // 2, cols], xs[:, k // 2, cols], bank(6 + k % 2), ALU.add)\
                    .then_inc(s("bd_added"), 1)

            def dve_round(r):
                n0 = r * NE
                ranks(r)
                hots(r, 0)
                table(r, 0)
                first = isinstance(r, int)
                if first:
                    positions()
                    dve.wait_ge(s("operand_hi"), BIAS_SPLIT)
                    V.tensor_tensor(bias_hl[NE:2 * NE, :], bgu_rows[0:NE, :], bias_hl[0:NE, :].bitcast(F32),
                                    ALU.subtract).then_inc(s("operand_lo"), 1)
                    dve.wait_ge(s("e_row_ready"), 2)
                    dve.wait_ge(s("operand_lo"), BIAS_SPLIT)
                picks(n0, 0)
                if not first:
                    for j in range(SLOTS):
                        split_lo(j, chunk_no(n0, j, True))
                xgT_lo(n0)
                for j in range(SLOTS, KD):
                    split_lo(j % SLOTS, chunk_no(n0, j, True))
                    if first:
                        bias_part_in(2 * (j - SLOTS))
                        bias_part_in(2 * (j - SLOTS) + 1)
                clips(n0, True)
                picks(n0 + 1, 1)
                xgT_lo(n0 + 1)
                hots(r, 1)
                table(r, 1)

                def step(n, e, more=True, second=False):
                    split_lo(0, chunk_no(n, 0))
                    product(n - 1)
                    split_lo(2, chunk_no(n, 2))
                    activation(n - 1)
                    split_lo(3, chunk_no(n, 3))
                    if second:
                        hots(r, 2)
                    split_lo(0, chunk_no(n, 4))
                    if second:
                        table(r, 2)
                    for j in range(5, 8):
                        split_lo(j % SLOTS, chunk_no(n, j))
                    actT_lo(n)
                    if second:
                        hots(r, 3)
                    for j in range(8, 11):
                        split_lo(j % SLOTS, chunk_no(n, j))
                    clips(n)
                    if second:
                        table(r, 3)
                    split_lo(3, chunk_no(n, 11))
                    if more:
                        picks(n + 1, e + 1)
                        xgT_lo(n + 1)

                step(n0 + 1, 1, second=True)
                with dve.Fori(2, NE - 1) as e:
                    step(n0 + e, e)
                step(n0 + NE - 1, NE - 1, more=False)
                product(n0 + NE - 1)
                activation(n0 + NE - 1)
                for c in range(FT // 2):
                    split_lo(c, down_no(n0 + NE, c, alone=True))
                actT_lo(n0 + NE)

            dve_round(0)
            more_rounds(dve, dve_round)
            dve.wait_ge(s("late_params_loaded"), 32)
            for t in range(TT):
                for j in range(TOPK):
                    k = t * TOPK + j
                    dve.wait_ge(s(f"yg_loaded{t}"), 16 * TOPK)
                    if j:
                        dve.wait_ge(s("y_added"), k)
                    else:
                        dve.wait_ge(s("bd_added"), 2 * t + 2)
                    V.scalar_tensor_tensor(out=xs[:, t, :], in0=yg[k], scalar=gate[:, t, j:j + 1], in1=xs[:, t, :],
                                           op0=ALU.mult, op1=ALU.add).then_inc(s("y_added"), 1)
                dve.wait_ge(s("ms_sum"), 2 * TT + t + 1)
                eps_and_inverse(3 + t, slice(t, t + 1))
                dve.wait_ge(s("ms_inv"), 3 + t)
                if t >= 2:
                    dve.wait_ge(s(f"out_stored{t % 2}"), 16)
                V.scalar_tensor_tensor(out=orow[t % 2], in0=xs[:, t, :], scalar=ms[:, 2, t:t + 1], in1=nwf,
                                       op0=ALU.mult, op1=ALU.mult).then_inc(s("out_ready"), 1)


_INS = ['x', 'norm1_w', 'w_in', 'conv_w', 'a_log_f', 'a_log_b', 'dt_bias_f', 'dt_bias_b', 'gdn_norm_w',
        'w_branch_a', 'w_branch_b', 'w_out', 'norm2_w', 'router_w', 'router_b', 'w_gate_up', 'b_gate_up',
        'w_down', 'b_down', 'norm_f_w']
_OUTS = [((1, 512, 1024), 'float32')]


def kernel(**inputs):
    import numpy as _np
    import concourse.bacc as _bacc
    from concourse import mybir as _mybir
    from concourse.bass_utils import run_bass_kernel_spmd as _run

    nc = _bacc.Bacc("TRN2", target_bir_lowering=False, num_devices=1)
    arrays, args = {}, []
    for name in _INS:
        a = _np.ascontiguousarray(inputs[name])
        arrays[f"in_{name}_dram"] = a
        args.append(nc.dram_tensor(f"in_{name}_dram", a.shape, _mybir.dt.from_np(a.dtype), kind="ExternalInput").ap())
    for i, (shape, dtype) in enumerate(_OUTS):
        dt = _mybir.dt.from_np(_np.dtype(dtype))
        args.append(nc.dram_tensor(f"out_{i}_dram", shape, dt, kind="ExternalOutput").ap())
    build(nc, *args)
    r = _run(nc, [arrays], core_ids=[0])
    return r.results[0]["out_0_dram"]
```
